# Optimizing a Trainium2 kernel written in Bass

```python
import math
import jax, jax.numpy as jnp
from jax import lax
import numpy as np
import jax
import jax.numpy as jnp

D_MODEL = 1024
BATCH = 1
SEQ = 256
DEPTH = 2

CHUNK = 64
N_EVEN = (DEPTH + 1) // 2
N_ODD = DEPTH // 2
EPS = 1e-6
LN_EPS = 1e-5
ROPE_THETA = 10000.0

CONV_DIM = D_MODEL
CONV_WIDTH = 31
RWKV_HEAD = 64
RWKV_HEADS = D_MODEL // RWKV_HEAD
RWKV_DIM = RWKV_HEADS * RWKV_HEAD
LORA_DIM = 64
GN_EPS = 64e-5
ATT_HEADS = 16
ATT_HEAD_DIM = 128
ATT_DIM = ATT_HEADS * ATT_HEAD_DIM
IDX_HEADS = 8
IDX_HEAD_DIM = 64
TOPK_MAX = 256
Q_BLOCK = 128

EVEN_SIZES = (CONV_DIM, CONV_DIM, CONV_DIM,
              RWKV_DIM, RWKV_DIM, RWKV_DIM,
              LORA_DIM, LORA_DIM, RWKV_DIM)
EVEN_COLS = sum(EVEN_SIZES)
EVEN_OUT = CONV_DIM + RWKV_DIM
ODD_SIZES = (ATT_DIM, ATT_HEAD_DIM, ATT_HEAD_DIM,
             IDX_HEADS * IDX_HEAD_DIM, IDX_HEAD_DIM, IDX_HEADS,
             ATT_DIM)
ODD_COLS = sum(ODD_SIZES)


def split_cols(z, sizes):
    idx = np.cumsum(sizes)[:-1].tolist()
    return jnp.split(z, idx, axis=-1)

def rms_norm(x, g):
    xf = x.astype(jnp.float32)
    y = xf * lax.rsqrt(jnp.mean(xf * xf, axis=-1, keepdims=True) + EPS)
    return (y * g.astype(jnp.float32)).astype(x.dtype)

def layer_norm(x, w, b, eps):
    xf = x.astype(jnp.float32)
    mu = jnp.mean(xf, axis=-1, keepdims=True)
    var = jnp.mean(jnp.square(xf - mu), axis=-1, keepdims=True)
    y = (xf - mu) * lax.rsqrt(var + eps)
    return (y * w.astype(jnp.float32) + b.astype(jnp.float32)).astype(x.dtype)

def rope(x, pos):
    d = x.shape[-1]
    inv = ROPE_THETA ** (-jnp.arange(0, d, 2, dtype=jnp.float32) / d)
    ang = pos.astype(jnp.float32)[..., None] * inv
    cos = jnp.cos(ang)[:, :, None, :]
    sin = jnp.sin(ang)[:, :, None, :]
    xf = x.astype(jnp.float32)
    x1, x2 = jnp.split(xf, 2, axis=-1)
    out = jnp.concatenate([x1 * cos - x2 * sin, x2 * cos + x1 * sin], axis=-1)
    return out.astype(x.dtype)

def token_shift(z):
    return jnp.pad(z[:, :-1], ((0, 0), (1, 0), (0, 0)))

def conformer_conv(val, glu, conv_w, conv_vec):
    u = val * jax.nn.sigmoid(glu)
    y = lax.conv_general_dilated(u, conv_w.astype(u.dtype), window_strides=(1,),
                                 padding=[(CONV_WIDTH - 1, 0)],
                                 dimension_numbers=('NWC', 'WIO', 'NWC'),
                                 feature_group_count=CONV_DIM)
    y = y + conv_vec[0]
    y = layer_norm(y, conv_vec[1], conv_vec[2], LN_EPS)
    return jax.nn.silu(y)

def rwkv7_step(state, inp):
    r_t, w_t, k_t, v_t, kk_t, a_t = inp
    sa = jnp.einsum('bhvk,bhk->bhv', state, -kk_t)
    state = (state * w_t[:, :, None, :]
             + sa[..., None] * (kk_t * a_t)[:, :, None, :]
             + v_t[..., None] * k_t[:, :, None, :])
    y = jnp.einsum('bhvk,bhk->bhv', state, r_t)
    return state, y

def rwkv7_mix(r, k, v, wd, ad, mu_rkv, mu_lora, vec, w_up, a_up, r_k):
    B, S, _ = r.shape
    f32 = jnp.float32
    lerp = lambda z, mu: z + (token_shift(z) - z) * mu
    r = lerp(r, mu_rkv[0]).astype(f32)
    k = lerp(k, mu_rkv[1]).astype(f32)
    v = lerp(v, mu_rkv[2]).astype(f32)
    wd = lerp(wd, mu_lora[0]).astype(f32)
    ad = lerp(ad, mu_lora[1]).astype(f32)
    vec = vec.astype(f32)
    w0, a0, k_k, k_a, lnx_w, lnx_b = vec[0], vec[1], vec[2], vec[3], vec[4], vec[5]
    w_log = -jax.nn.softplus(-(w0 + jnp.tanh(wd) @ w_up.astype(f32))) - 0.5
    decay = jnp.exp(-jnp.exp(w_log))
    a = jax.nn.sigmoid(a0 + ad @ a_up.astype(f32))
    heads = lambda t: t.reshape(B, S, RWKV_HEADS, RWKV_HEAD)
    kk = heads(k * k_k)
    kk = kk / jnp.maximum(jnp.sqrt(jnp.sum(kk * kk, axis=-1, keepdims=True)), 1e-12)
    k = k * (1.0 + (a - 1.0) * k_a)
    r_h, w_h, k_h, v_h, a_h = heads(r), heads(decay), heads(k), heads(v), heads(a)
    xs = tuple(jnp.moveaxis(t, 1, 0) for t in (r_h, w_h, k_h, v_h, kk, a_h))
    state0 = jnp.zeros((B, RWKV_HEADS, RWKV_HEAD, RWKV_HEAD), f32)
    _, y = lax.scan(rwkv7_step, state0, xs)
    y = jnp.moveaxis(y, 0, 1)
    mu = jnp.mean(y, axis=-1, keepdims=True)
    var = jnp.mean(jnp.square(y - mu), axis=-1, keepdims=True)
    y = ((y - mu) * lax.rsqrt(var + GN_EPS)).reshape(B, S, RWKV_DIM) * lnx_w + lnx_b
    bonus = jnp.sum(r_h * k_h * r_k.astype(f32), axis=-1, keepdims=True) * v_h
    return y + bonus.reshape(B, S, RWKV_DIM)

def dsa_attention(q, k, v, qi, ki, wi, positions):
    B, S = positions.shape
    k_sel = min(TOPK_MAX, S // 4)
    nb = S // Q_BLOCK
    chunk_id = positions // CHUNK
    kf = ki.astype(jnp.float32)

    def to_blocks(t):
        return jnp.moveaxis(t.reshape((B, nb, Q_BLOCK) + t.shape[2:]), 1, 0)

    def block(args):
        qb, qib, wib, cqb = args
        idx_logits = jnp.einsum('bqhd,bsd->bqhs', qib.astype(jnp.float32), kf) * (IDX_HEAD_DIM ** -0.5)
        score = jnp.einsum('bqh,bqhs->bqs', wib.astype(jnp.float32) * (IDX_HEADS ** -0.5),
                           jax.nn.relu(idx_logits))
        adm = chunk_id[:, None, :] <= cqb[:, :, None]
        score = jnp.where(adm, score, -jnp.inf)
        top_val, top_idx = lax.top_k(score, k_sel)
        valid = jnp.isfinite(top_val)
        kg = jax.vmap(lambda kb, ib: kb[ib])(k, top_idx)
        vg = jax.vmap(lambda vb, ib: vb[ib])(v, top_idx)
        logits = jnp.einsum('bqhd,bqkd->bqhk', qb, kg).astype(jnp.float32) * (ATT_HEAD_DIM ** -0.5)
        logits = jnp.where(valid[:, :, None, :], logits, -jnp.inf)
        p = jax.nn.softmax(logits, axis=-1).astype(v.dtype)
        return jnp.einsum('bqhk,bqkd->bqhd', p, vg)

    o = lax.map(block, (to_blocks(q), to_blocks(qi), to_blocks(wi), to_blocks(chunk_id)))
    return jnp.moveaxis(o, 0, 1).reshape(B, S, ATT_DIM)

def first_inputs(seed: int = 0) -> dict:
    key = jax.random.key(seed)
    ks = jax.random.split(key, 24)
    nrm = lambda k, shape, s: jax.random.normal(k, shape, jnp.float32) * s
    x = nrm(ks[0], (BATCH, SEQ, D_MODEL), 1.0)
    c = nrm(ks[1], (BATCH, D_MODEL), 1.0)
    offsets = jax.random.randint(ks[2], (BATCH,), 0, 64, dtype=jnp.int32) * CHUNK
    positions = offsets[:, None] + jnp.arange(SEQ, dtype=jnp.int32)[None, :]
    ada_w = nrm(ks[3], (DEPTH, D_MODEL, 3 * D_MODEL), 0.5 * D_MODEL ** -0.5)
    ada_b = nrm(ks[4], (DEPTH, 3 * D_MODEL), 0.02)
    norm_g = 1.0 + nrm(ks[5], (DEPTH, D_MODEL), 0.05)
    final_g = 1.0 + nrm(ks[6], (D_MODEL,), 0.05)
    even_w_in = nrm(ks[7], (N_EVEN, D_MODEL, EVEN_COLS), D_MODEL ** -0.5)
    even_w_out = nrm(ks[8], (N_EVEN, EVEN_OUT, D_MODEL), EVEN_OUT ** -0.5)
    conv_w = nrm(ks[9], (N_EVEN, CONV_WIDTH, 1, CONV_DIM), CONV_WIDTH ** -0.5)
    kc = jax.random.split(ks[10], 3)
    conv_vec = jnp.stack([nrm(kc[0], (N_EVEN, CONV_DIM), 0.02),
                          1.0 + nrm(kc[1], (N_EVEN, CONV_DIM), 0.05),
                          nrm(kc[2], (N_EVEN, CONV_DIM), 0.02)], axis=1)
    rwkv_mu_rkv = jax.random.uniform(ks[11], (N_EVEN, 3, RWKV_DIM), jnp.float32)
    rwkv_mu_lora = jax.random.uniform(ks[12], (N_EVEN, 2, LORA_DIM), jnp.float32)
    kv = jax.random.split(ks[13], 6)
    rwkv_vec = jnp.stack([
        jax.random.uniform(kv[0], (N_EVEN, RWKV_DIM), jnp.float32, -4.0, 1.0),
        nrm(kv[1], (N_EVEN, RWKV_DIM), 0.1),
        0.85 + nrm(kv[2], (N_EVEN, RWKV_DIM), 0.05),
        1.0 + nrm(kv[3], (N_EVEN, RWKV_DIM), 0.05),
        1.0 + nrm(kv[4], (N_EVEN, RWKV_DIM), 0.05),
        nrm(kv[5], (N_EVEN, RWKV_DIM), 0.02)], axis=1)
    rwkv_w_up = nrm(ks[14], (N_EVEN, LORA_DIM, RWKV_DIM), 0.5 * LORA_DIM ** -0.5)
    rwkv_a_up = nrm(ks[15], (N_EVEN, LORA_DIM, RWKV_DIM), 0.5 * LORA_DIM ** -0.5)
    rwkv_r_k = nrm(ks[16], (N_EVEN, RWKV_HEADS, RWKV_HEAD), 0.1)
    odd_w_in = nrm(ks[17], (N_ODD, D_MODEL, ODD_COLS), D_MODEL ** -0.5)
    odd_w_out = nrm(ks[18], (N_ODD, ATT_DIM, D_MODEL), ATT_DIM ** -0.5)
    return {"x": x, "c": c, "positions": positions, "ada_w": ada_w, "ada_b": ada_b,
            "norm_g": norm_g, "final_g": final_g, "even_w_in": even_w_in,
            "even_w_out": even_w_out, "conv_w": conv_w, "conv_vec": conv_vec,
            "rwkv_mu_rkv": rwkv_mu_rkv, "rwkv_mu_lora": rwkv_mu_lora, "rwkv_vec": rwkv_vec,
            "rwkv_w_up": rwkv_w_up, "rwkv_a_up": rwkv_a_up, "rwkv_r_k": rwkv_r_k,
            "odd_w_in": odd_w_in, "odd_w_out": odd_w_out}

def first_block(x, c, positions, ada_w, ada_b, norm_g, final_g, even_w_in, even_w_out,
              conv_w, conv_vec, rwkv_mu_rkv, rwkv_mu_lora, rwkv_vec, rwkv_w_up, rwkv_a_up,
              rwkv_r_k, odd_w_in, odd_w_out):
    B, S, _ = x.shape
    cond = jax.nn.silu(c)
    for l in range(DEPTH):
        mod = cond @ ada_w[l] + ada_b[l]
        shift, scale, gate = jnp.split(mod, 3, axis=-1)
        h = rms_norm(x, norm_g[l]) * (1.0 + scale[:, None, :]) + shift[:, None, :]
        j = l // 2
        if l % 2 == 0:
            z = h @ even_w_in[j]
            a_val, a_glu, a_gate, r, k, v, wd, ad, b_gate = split_cols(z, EVEN_SIZES)
            ya = conformer_conv(a_val, a_glu, conv_w[j], conv_vec[j]) * jax.nn.silu(a_gate)
            yb = rwkv7_mix(r, k, v, wd, ad, rwkv_mu_rkv[j], rwkv_mu_lora[j], rwkv_vec[j],
                           rwkv_w_up[j], rwkv_a_up[j], rwkv_r_k[j]).astype(h.dtype)
            yb = yb * jax.nn.silu(b_gate)
            out = jnp.concatenate([ya, yb], axis=-1) @ even_w_out[j]
        else:
            z = h @ odd_w_in[j]
            q, k, v, qi, ki, wi, g = split_cols(z, ODD_SIZES)
            q = rope(q.reshape(B, S, ATT_HEADS, ATT_HEAD_DIM), positions)
            k = rope(k[:, :, None, :], positions)[:, :, 0, :]
            qi = rope(qi.reshape(B, S, IDX_HEADS, IDX_HEAD_DIM), positions)
            ki = rope(ki[:, :, None, :], positions)[:, :, 0, :]
            o = dsa_attention(q, k, v, qi, ki, wi, positions)
            out = (o * jax.nn.silu(g)) @ odd_w_out[j]
        x = x + gate[:, None, :] * out
    return rms_norm(x, final_g)


PLE_DIM = 256
N_EVEN_2 = (DEPTH + 1) // 2
N_ODD_2 = DEPTH // 2

DA_HEADS = 4
DA_HEAD_DIM = 64
DA_V_DIM = 2 * DA_HEAD_DIM
DA_QK_WIDTH = DA_HEADS * 2 * DA_HEAD_DIM
DA_WIDTH = DA_HEADS * DA_V_DIM
ROPE_THETA_2 = 500000.0
ROT_DIM = DA_HEAD_DIM // 4

SC_WIDTH = 512
SC_WIDTH_CONV = 3
EVEN_IN_WIDTH = 3 * DA_QK_WIDTH // 2 * 2 // 2 * 0 + DA_QK_WIDTH * 2 + DA_WIDTH + 3 * SC_WIDTH

GM_WIDTH = D_MODEL
GM_GROUPS = 8
GM_GROUP_CH = GM_WIDTH // GM_GROUPS
GM_CHUNK = 128

D_FF = 2816
N_EXPERTS = 8
TOP_K = 2
MOE_BLOCK = 256

RMS_EPS = 1e-6


def rms_norm_2(x, g):
    xf = x.astype(jnp.float32)
    y = xf * lax.rsqrt(jnp.mean(xf * xf, axis=-1, keepdims=True) + RMS_EPS)
    return (y * g.astype(jnp.float32)).astype(x.dtype)

def layer_norm_2(x, g, b):
    xf = x.astype(jnp.float32)
    mu = jnp.mean(xf, axis=-1, keepdims=True)
    var = jnp.mean(jnp.square(xf - mu), axis=-1, keepdims=True)
    y = (xf - mu) * lax.rsqrt(var + LN_EPS)
    return (y * g.astype(jnp.float32) + b.astype(jnp.float32)).astype(x.dtype)

def rope_partial(t, positions):
    half = ROT_DIM // 2
    inv_freq = ROPE_THETA_2 ** (-jnp.arange(0, ROT_DIM, 2, dtype=jnp.float32) / ROT_DIM)
    ang = positions.astype(jnp.float32)[:, :, None] * inv_freq
    cos = jnp.cos(ang)[:, :, None, None, :].astype(t.dtype)
    sin = jnp.sin(ang)[:, :, None, None, :].astype(t.dtype)
    t1 = t[..., :half]
    t2 = t[..., half:ROT_DIM]
    return jnp.concatenate([t1 * cos - t2 * sin, t2 * cos + t1 * sin, t[..., ROT_DIM:]], axis=-1)

def diff_attention(q, k, v, lam, lambda_init, subln_g):
    bsz, seq = q.shape[0], q.shape[1]
    n_blocks = seq // Q_BLOCK
    q = q * (DA_HEAD_DIM ** -0.5)
    kpos = jnp.arange(seq)

    def one_block(i):
        qb = lax.dynamic_slice_in_dim(q, i * Q_BLOCK, Q_BLOCK, axis=1)
        s = jnp.einsum('bqhcd,bkhcd->bhcqk', qb, k, preferred_element_type=jnp.float32)
        qpos = i * Q_BLOCK + jnp.arange(Q_BLOCK)
        mask = kpos[None, :] <= qpos[:, None]
        pr = jax.nn.softmax(jnp.where(mask, s, -jnp.inf), axis=-1)
        w = pr[:, :, 0] - lam * pr[:, :, 1]
        return jnp.einsum('bhqk,bkhe->bqhe', w.astype(v.dtype), v)

    out = lax.map(one_block, jnp.arange(n_blocks))
    out = jnp.moveaxis(out, 0, 1).reshape(bsz, seq, DA_HEADS, DA_V_DIM)
    out = rms_norm_2(out, subln_g) * (1.0 - lambda_init)
    return out.reshape(bsz, seq, DA_WIDTH)

def causal_short_conv(z, w):
    ch = z.shape[-1]
    rhs = jnp.transpose(w).astype(z.dtype)[:, None, :]
    return lax.conv_general_dilated(z, rhs, window_strides=(1,), padding=[(SC_WIDTH_CONV - 1, 0)],
                                    dimension_numbers=('NWC', 'WIO', 'NWC'), feature_group_count=ch)

def spatial_gating(u, v, w_s, b_s):
    bsz, seq, _ = v.shape
    vr = v.reshape(bsz, seq // GM_CHUNK, GM_CHUNK, GM_GROUPS, GM_GROUP_CH)
    tril = jnp.tril(jnp.ones((GM_CHUNK, GM_CHUNK), dtype=w_s.dtype))
    vs = jnp.einsum('gts,bnsgc->bntgc', w_s * tril, vr)
    vs = vs + jnp.transpose(b_s)[None, None, :, :, None]
    return u * vs.reshape(bsz, seq, GM_WIDTH)

def swiglu(h, w1, w3, w2):
    return (jax.nn.silu(h @ w1) * (h @ w3)) @ w2

def moe_swiglu(h, router_w, w1, w3, w2):
    bsz, seq, dm = h.shape
    n_tok = bsz * seq
    n_assign = n_tok * TOP_K
    n_blocks = -(-(n_assign + N_EXPERTS * (MOE_BLOCK - 1)) // MOE_BLOCK)
    xt = h.reshape(n_tok, dm)
    logits = jnp.einsum('nd,de->ne', xt, router_w, preferred_element_type=jnp.float32)
    top_val, top_idx = lax.top_k(logits, TOP_K)
    gates = jax.nn.softmax(top_val, axis=-1)
    expert_flat = top_idx.reshape(-1)
    token_flat = jnp.arange(n_assign) // TOP_K
    gate_flat = gates.reshape(-1)
    order = jnp.argsort(expert_flat)
    sorted_expert = expert_flat[order]
    sorted_token = token_flat[order]
    counts = jnp.bincount(expert_flat, length=N_EXPERTS)
    starts = jnp.cumsum(counts) - counts
    padded = (counts + MOE_BLOCK - 1) // MOE_BLOCK * MOE_BLOCK
    pad_ends = jnp.cumsum(padded)
    pad_starts = pad_ends - padded
    dest = pad_starts[sorted_expert] + (jnp.arange(n_assign) - starts[sorted_expert])
    rows = jnp.zeros((n_blocks * MOE_BLOCK, dm), h.dtype).at[dest].set(xt[sorted_token])
    block_start = jnp.arange(n_blocks) * MOE_BLOCK
    block_expert = jnp.minimum(jnp.searchsorted(pad_ends, block_start, side='right'), N_EXPERTS - 1)

    def expert_block(args):
        xb, e = args
        return (jax.nn.silu(xb @ w1[e]) * (xb @ w3[e])) @ w2[e]

    y_rows = lax.map(expert_block, (rows.reshape(n_blocks, MOE_BLOCK, dm), block_expert))
    y_sorted = y_rows.reshape(n_blocks * MOE_BLOCK, dm)[dest]
    contrib = y_sorted * gate_flat[order][:, None].astype(h.dtype)
    out = jax.ops.segment_sum(contrib, sorted_token, num_segments=n_tok)
    return out.reshape(bsz, seq, dm)

def second_inputs(seed: int = 0) -> dict:
    key = jax.random.key(seed)
    ks = list(jax.random.split(key, 40))
    cnt = [0]

    def nk():
        cnt[0] += 1
        return ks[cnt[0] - 1]

    def nrm(shape, scale):
        return scale * jax.random.normal(nk(), shape, jnp.float32)

    def gain(shape):
        return 1.0 + nrm(shape, 0.05)

    x = nrm((BATCH, SEQ, D_MODEL), 1.0)
    p = nrm((DEPTH, BATCH, SEQ, PLE_DIM), 1.0)
    positions = (jax.random.randint(nk(), (BATCH, 1), 0, 1024, jnp.int32)
                 + jnp.arange(SEQ, dtype=jnp.int32)[None, :])
    dsc = D_MODEL ** -0.5
    return {
        "x": x,
        "p": p,
        "positions": positions,
        "ln_mix": gain((DEPTH, D_MODEL)),
        "ln_ffn": gain((DEPTH, D_MODEL)),
        "ln_ple": gain((DEPTH, D_MODEL)),
        "a_w_in": nrm((N_EVEN_2, D_MODEL, EVEN_IN_WIDTH), dsc),
        "a_lambda": nrm((N_EVEN_2, 4, DA_HEAD_DIM), 0.1),
        "a_subln": gain((N_EVEN_2, DA_V_DIM)),
        "a_conv_w": nrm((N_EVEN_2, SC_WIDTH, SC_WIDTH_CONV), SC_WIDTH_CONV ** -0.5),
        "a_w_out": nrm((N_EVEN_2, DA_WIDTH + SC_WIDTH, D_MODEL), (DA_WIDTH + SC_WIDTH) ** -0.5),
        "ffn_w1": nrm((N_EVEN_2, D_MODEL, D_FF), dsc),
        "ffn_w3": nrm((N_EVEN_2, D_MODEL, D_FF), dsc),
        "ffn_w2": nrm((N_EVEN_2, D_FF, D_MODEL), D_FF ** -0.5),
        "c_w_in": nrm((N_ODD_2, D_MODEL, 2 * GM_WIDTH), dsc),
        "c_ln_g": gain((N_ODD_2, GM_WIDTH)),
        "c_ln_b": nrm((N_ODD_2, GM_WIDTH), 0.02),
        "c_w_s": nrm((N_ODD_2, GM_GROUPS, GM_CHUNK, GM_CHUNK), GM_CHUNK ** -0.5),
        "c_b_s": 1.0 + nrm((N_ODD_2, GM_GROUPS, GM_CHUNK), 0.1),
        "c_w_out": nrm((N_ODD_2, GM_WIDTH, D_MODEL), GM_WIDTH ** -0.5),
        "router_w": nrm((N_ODD_2, D_MODEL, N_EXPERTS), dsc),
        "moe_w1": nrm((N_ODD_2, N_EXPERTS, D_MODEL, D_FF), dsc),
        "moe_w3": nrm((N_ODD_2, N_EXPERTS, D_MODEL, D_FF), dsc),
        "moe_w2": nrm((N_ODD_2, N_EXPERTS, D_FF, D_MODEL), D_FF ** -0.5),
        "ple_gate": nrm((DEPTH, D_MODEL, D_MODEL), dsc),
        "ple_proj": nrm((DEPTH, PLE_DIM, D_MODEL), PLE_DIM ** -0.5),
        "final_norm": gain((D_MODEL,)),
    }

def second_block(x, p, positions, ln_mix, ln_ffn, ln_ple, a_w_in, a_lambda, a_subln, a_conv_w,
              a_w_out, ffn_w1, ffn_w3, ffn_w2, c_w_in, c_ln_g, c_ln_b, c_w_s, c_b_s, c_w_out,
              router_w, moe_w1, moe_w3, moe_w2, ple_gate, ple_proj, final_norm):
    h = x
    bsz, seq, _ = x.shape
    splits = [DA_QK_WIDTH, 2 * DA_QK_WIDTH, 2 * DA_QK_WIDTH + DA_WIDTH,
              2 * DA_QK_WIDTH + DA_WIDTH + SC_WIDTH, 2 * DA_QK_WIDTH + DA_WIDTH + 2 * SC_WIDTH]
    for i in range(DEPTH):
        j = i // 2
        hn = rms_norm_2(h, ln_mix[i])
        if i % 2 == 0:
            z = hn @ a_w_in[j]
            q, k, v, b_gate, c_gate, hc = jnp.split(z, splits, axis=-1)
            q = rope_partial(q.reshape(bsz, seq, DA_HEADS, 2, DA_HEAD_DIM), positions)
            k = rope_partial(k.reshape(bsz, seq, DA_HEADS, 2, DA_HEAD_DIM), positions)
            v = v.reshape(bsz, seq, DA_HEADS, DA_V_DIM)
            lambda_init = 0.8 - 0.6 * math.exp(-0.3 * i)
            lp = a_lambda[j].astype(jnp.float32)
            lam = jnp.exp(jnp.sum(lp[0] * lp[1])) - jnp.exp(jnp.sum(lp[2] * lp[3])) + lambda_init
            attn = diff_attention(q, k, v, lam, lambda_init, a_subln[j])
            conv = b_gate * causal_short_conv(c_gate * hc, a_conv_w[j])
            h = h + jnp.concatenate([attn, conv], axis=-1) @ a_w_out[j]
            h = h + swiglu(rms_norm_2(h, ln_ffn[i]), ffn_w1[j], ffn_w3[j], ffn_w2[j])
        else:
            z = jax.nn.gelu(hn @ c_w_in[j], approximate=False)
            u, vv = jnp.split(z, 2, axis=-1)
            vv = layer_norm_2(vv, c_ln_g[j], c_ln_b[j])
            h = h + spatial_gating(u, vv, c_w_s[j], c_b_s[j]) @ c_w_out[j]
            h = h + moe_swiglu(rms_norm_2(h, ln_ffn[i]), router_w[j], moe_w1[j], moe_w3[j], moe_w2[j])
        gate = jax.nn.sigmoid(rms_norm_2(h, ln_ple[i]) @ ple_gate[i])
        h = h + gate * (p[i] @ ple_proj[i])
    return rms_norm_2(h, final_norm)


def setup_inputs(seed=0):
    out = dict(first_inputs(seed))
    for name, value in second_inputs(seed + 1).items():
        if name != "x":
            out[name + "_2"] = value
    return out


def reference(
    x, c, positions, ada_w, ada_b, norm_g, final_g, even_w_in, even_w_out, conv_w, conv_vec,
    rwkv_mu_rkv, rwkv_mu_lora, rwkv_vec, rwkv_w_up, rwkv_a_up, rwkv_r_k, odd_w_in, odd_w_out,
    p_2, positions_2, ln_mix_2, ln_ffn_2, ln_ple_2, a_w_in_2, a_lambda_2, a_subln_2, a_conv_w_2,
    a_w_out_2, ffn_w1_2, ffn_w3_2, ffn_w2_2, c_w_in_2, c_ln_g_2, c_ln_b_2, c_w_s_2, c_b_s_2,
    c_w_out_2, router_w_2, moe_w1_2, moe_w3_2, moe_w2_2, ple_gate_2, ple_proj_2, final_norm_2,
):
    x = first_block(
        x, c, positions, ada_w, ada_b, norm_g, final_g, even_w_in, even_w_out, conv_w, conv_vec,
        rwkv_mu_rkv, rwkv_mu_lora, rwkv_vec, rwkv_w_up, rwkv_a_up, rwkv_r_k, odd_w_in,
        odd_w_out,
    )
    return second_block(
        x, p_2, positions_2, ln_mix_2, ln_ffn_2, ln_ple_2, a_w_in_2, a_lambda_2, a_subln_2,
        a_conv_w_2, a_w_out_2, ffn_w1_2, ffn_w3_2, ffn_w2_2, c_w_in_2, c_ln_g_2, c_ln_b_2,
        c_w_s_2, c_b_s_2, c_w_out_2, router_w_2, moe_w1_2, moe_w3_2, moe_w2_2, ple_gate_2,
        ple_proj_2, final_norm_2,
    )


_drawn_inputs = setup_inputs


def setup_inputs(seed=0):
    import zlib

    import numpy as np

    out = dict(_drawn_inputs(seed))
    spreads = {}
    factors = {'ln_ple_2': 4.403, 'c_ln_b_2': 11.91, 'c_ln_g_2': 2.789}
    for name, (base, spread) in spreads.items():
        noise = np.random.default_rng([zlib.crc32(name.encode()), seed]).standard_normal(out[name].shape)
        drawn = base * np.exp(spread * noise) if base else spread * noise
        out[name] = jnp.asarray(drawn.astype(out[name].dtype))
    for name, factor in factors.items():
        out[name] = (out[name] * factor).astype(out[name].dtype)
    return out
```

```python
import numpy as np
import concourse.bass as bass
from concourse import mybir
from contextlib import ExitStack

F32 = mybir.dt.float32
I32 = mybir.dt.int32
ALU = mybir.AluOpType
ACT = mybir.ActivationFunctionType
AX_X = mybir.AxisListType.X

P = 128
T = 256
D = 1024
KT = D // P
TT = T // P
RING = 4
SLOT = 4096
C = 32
NC4 = P // C
NH = 16
HD = 64
NQ = NH
FF = 2816
FT = FF // P
NE = 8
SLOTS = 128
WC = 352
LAM0 = 0.2
BIG = 1.0e30
DECAY = float(np.exp(-0.5))
TOPK = 64
ARENA = 29424

VEC = {}
for _n in ["c", "norm_g0", "norm_g1", "final_g", "ab00", "ab01", "ab02", "ab10", "ab11", "ab12",
           "cv0", "cv1", "cv2", "mu_r", "mu_k", "mu_v"]:
    VEC[_n] = 8 * len(VEC)
for _n in ["w0", "a0", "k_k", "k_a", "lnx_w", "lnx_b", "r_k", "mix0", "mix1", "ffn0", "ffn1", "ple0",
           "ple1", "fnorm", "cln_g", "cln_b"]:
    VEC[_n] = 8 * len(VEC)


class Chain:

    def __init__(self, eng, sem):
        self.eng, self.sem, self.n = eng, sem, 0

    def __call__(self, ins):
        ins.then_inc(self.sem, 1)
        self.n += 1

    def settle(self):
        self.eng.wait_ge(self.sem, self.n)


class Stream:

    def __init__(self):
        self.phases, self.chunks, self.at = {}, [], {}

    def add(self, name, k, cols, n, src, reader="pe", group=4, loop=False):
        c0 = len(self.chunks)
        for _ in range(n):
            self.chunks.append((reader, 1 + sum(1 for r, _ in self.chunks if r == reader)))
        self.phases[name] = dict(c0=c0, k=k, cols=cols, n=n, src=src, loop=loop, group=group)


def build(nc, a, out):
    ctx = ExitStack()
    with ctx, nc.allow_non_contiguous_dma(reason="small parameter columns"):
        def sb(name, shape, dt=F32):
            return ctx.enter_context(nc.sbuf_tensor(name, shape, dt))

        sems = {}

        def sem(name):
            if name not in sems:
                sems[name] = ctx.enter_context(nc.semaphore(name))
            return sems[name]

        ring = sb("ring", [P, RING, SLOT])
        xT = sb("xT", [P, KT, T])
        hT = sb("hT", [P, KT, T])
        ident = sb("ident", [P, P])
        ones = sb("ones", [P, P])
        swap_a = sb("swap_a", [P, P])
        swap_i = sb("swap_i", [P, P])
        swap_d = sb("swap_d", [P, P])
        hsel = sb("hsel", [P, 32])
        bmask = sb("bmask", [P, 2, P])
        segm = sb("segm", [P, T])
        pc = sb("pc", [P, 256])
        cw = sb("cw", [P, T])
        acw = sb("acw", [P, 4, 3])
        small = sb("small", [P, 64])
        mod = sb("mod", [P, 2, 24])
        gs = sb("gs", [P, 16])
        cond = sb("cond", [P, KT])
        nr = sb("nr", [P, T])
        stb = cw[0:16, :]
        hspread = sb("hspread", [16, KT, P])
        pend = sb("pend", [P, KT, 8])
        arena = sb("arena", [P, ARENA])

        def reg(off, *shape):
            n = int(np.prod(shape))
            assert off + n <= ARENA
            v = arena[:, off:off + n]
            if len(shape) == 1:
                return v
            names = " ".join(f"d{i}" for i in range(len(shape)))
            return v.rearrange(f"p ({names}) -> p {names}", **{f"d{i}": s for i, s in enumerate(shape)})

        bank = [ctx.enter_context(nc.psum_tensor(f"bank{i}", [P, 512], F32)) for i in range(8)]

        mulora = small[:, 0:1]
        subln = small[:, 1:2]
        posc_f = small[:, 4:6]
        lam = small[:, 6:7]
        invf = small[:, 8:14]

        def col(name, ct=0):
            return pc[:, VEC[name] + ct:VEC[name] + ct + 1]

        def cols8(name):
            return pc[:, VEC[name]:VEC[name] + 8]

        def hs(ct):
            return hsel[:, 14 - 2 * ct:30 - 2 * ct]

        def he(ct):
            return hspread[:, ct, :]

        VAL = reg(0, KT, T)
        GLU = reg(2048, KT, T)
        AG = reg(4096, KT, T)
        RR = reg(6144, KT, T)
        KK = reg(8192, KT, T)
        VV = reg(10240, KT, T)
        ZE = reg(4096, 32 * T)
        BG = reg(12288, KT, T)
        LO = reg(14336, 512)
        UP = reg(14848, KT, T + 30)
        YY = reg(17136, KT, T)
        X1 = reg(19184, KT, T)
        X2 = reg(21232, KT, T)
        X3 = reg(23280, KT, T)
        AR = reg(25328, KT, 2, T)
        X4 = GLU
        XTOK = reg(19184, TT, D)
        WU = reg(25328, D)
        PROW = reg(26352, 2, P)
        CROW = reg(26608, 2, P)
        ADA = reg(26864, 2, 512)
        A4T = reg(0, NQ, P)
        A3T = reg(4096, NQ, P)
        A2T = reg(19184, NQ, P)
        APT = reg(19184, KT, P)
        UU = reg(20208, NQ * HD)
        TBD = reg(21232, NQ, P)
        BTOK = reg(23280, D)
        VTOK = reg(24304, D)
        KTOK = reg(6144, D)
        ATOK = reg(7168, D)
        WW = reg(14336, NQ * HD)
        SS = reg(15360, KT, HD)
        TTP = reg(15872, C, C)
        LTC = reg(19184, 2 * NQ, C)
        LTP = reg(20208, C, C)
        TMP = reg(21232, 1024)
        YT = hT
        ltd = nc.dram_tensor("lt_scratch", (NC4, C, 2 * NQ, C), F32).ap()
        ttd = nc.dram_tensor("tt_scratch", (P, C * C), F32).ap()

        TOKS = [(lambda ct, t: AR[:, ct, 0, t], ATOK), (lambda ct, t: X4[:, ct, t], BTOK),
                (lambda ct, t: KK[:, ct, t], KTOK), (lambda ct, t: VV[:, ct, t], VTOK)]
        NSQ = [VAL]
        POSI = sb("posi", [P, 2], I32)
        taps = sem("tap_done")

        chunks, phases = [], {}
        count = {"pe": 0, "dve": 0}
        taken = {"act": 0, "dve": 0, "": 0}

        def add(name, k, ncol, n, tiles, src, taker="", reader="pe", loop=False, group=4, **more):
            phases[name] = dict(c0=len(chunks), k=k, ncol=ncol, n=n, tiles=tiles, src=src, loop=loop,
                                group=group, t0=count[reader], taker=taker, taken0=taken[taker], **more)
            taken[taker] += n * tiles
            for _ in range(n):
                count[reader] += tiles
                chunks.append((reader, count[reader]))

        def by_cols(w, width, first=0, k=D // P):
            v = w.rearrange("(k p) n -> p k n", p=P)
            return lambda j, i: v[:, :, bass.ds(first + (j + 4 * i) * width, width)]

        ewi, owi, awi = a["even_w_in"][0], a["odd_w_in"][0], a["a_w_in_2"][0]
        add("ada0", 8, 512, 6, 1, by_cols(a["ada_w"][0], 512), reader="dve")
        add("zA", 8, 512, 4, 4, by_cols(ewi, 512), "act")
        add("zB", 8, 512, 8, 4, by_cols(ewi, 512, 2048), "act", loop=True)
        add("ada1", 8, 512, 6, 1, by_cols(a["ada_w"][1], 512), reader="dve")
        add("zL", 8, 128, 1, 1, by_cols(ewi, 128, 6144), "act")
        add("zG", 8, 512, 2, 4, by_cols(ewi, 512, 6272), "act")
        add("eo", 16, 256, 4, 2, by_cols(a["even_w_out"][0], 256, k=16), "dve")
        M1 = 2048
        add("m1", 8, 512, 1, 4, by_cols(owi, 512, M1), "act")
        add("m2", 8, 328, 1, 4, by_cols(owi, 328, M1 + 512), "act")
        add("q", 8, 512, 4, 4, by_cols(owi, 512), "act")
        add("g", 8, 512, 4, 4, by_cols(owi, 512, M1 + 840), "act")
        add("oo", 16, 256, 4, 2, by_cols(a["odd_w_out"][0], 256, k=16), "dve")
        add("qk", 8, 512, 2, 4, by_cols(awi, 512), "act")
        add("v", 8, 512, 1, 2, by_cols(awi, 512, 1024), "act")
        add("bch", 8, 512, 3, 4, by_cols(awi, 512, 1536), "act")
        add("ao", 8, 512, 2, 4, by_cols(a["a_w_out_2"][0], 512), "dve")
        f1, f3 = (a[f"ffn_{w}_2"][0].rearrange("(k p) n -> p k n", p=P) for w in ("w1", "w3"))
        add("f13", 8, 256, 22, 2, lambda j, i: (f1, f3)[j % 2][:, :, bass.ds((j // 2 + 2 * i) * 256, 256)], loop=True)
        add("f2", FT, 128, 8, 1, by_cols(a["ffn_w2_2"][0], 128, k=FT), "dve", loop=True)
        add("pg0", 8, 512, 2, 4, by_cols(a["ple_gate_2"][0], 512), "act")
        add("pp0", 2, 1024, 1, 8, by_cols(a["ple_proj_2"][0], 1024, k=2), "dve")
        add("cin", 8, 512, 4, 4, by_cols(a["c_w_in_2"][0], 512), "act")
        add("cout", 8, 512, 2, 4, by_cols(a["c_w_out_2"][0], 512), "dve")

        W2F = [3, 3, 3, 3, 3, 3, 2, 2]
        up1, up3 = (a[f"moe_{w}_2"][0].rearrange("e (k p) n -> e p k n", p=P) for w in ("w1", "w3"))
        down = a["moe_w2_2"][0].rearrange("e (f p) n -> e p f n", p=P)
        UPS, DOWNS = 2 * FF // WC, len(W2F)

        def moe_shape(j):
            return (KT, WC) if j < UPS else (W2F[j - UPS], D)

        def moe_src(j, e):
            ex = slice(e, e + 1) if isinstance(e, int) else bass.ds(e, 1)
            if j < UPS:
                v = (up1, up3)[j % 2][ex, :, :, WC * (j // 2):WC * (j // 2) + WC]
            else:
                f = sum(W2F[:j - UPS])
                v = down[ex, :, f:f + W2F[j - UPS], :]
            return v.rearrange("e p k n -> (e p) k n")

        add("moe", 0, 0, NE * (UPS + DOWNS), 1, moe_src, loop=True, group=UPS + DOWNS, shape=moe_shape)
        add("pg1", 8, 512, 2, 4, by_cols(a["ple_gate_2"][1], 512), "act")
        add("pp1", 2, 1024, 1, 8, by_cols(a["ple_proj_2"][1], 1024, k=2), "dve")

        QT = reg(0, NH, T)
        GT = reg(4096, NH, T)
        QI = reg(8192, 4, T)
        KI = reg(9216, 1, T)
        KC = reg(9472, 1, T)
        VTK = reg(9728, TT, P)
        WI = reg(9984, TT, NE)
        ROT = reg(10240, 3, 2, T)
        ANG = reg(11776, 3, T)
        POSB = reg(12544, T)
        CHUNKS = reg(12800, T)
        ADM = reg(13056, TT, T)
        CUR = reg(13568, TT, T)
        RELU = reg(14080, 2, T)
        TOP = reg(14592, TT, 8)
        MASK = reg(14608, TT, T)
        SWP = reg(18000, 2, 2, T)
        LG = reg(15632, 2, 2, T)
        PT = reg(16656, 2, 2 * T)
        MX = reg(17680, 2, 2)
        SM = reg(17684, 2, 2)
        CHC = reg(17690, TT)
        ANG2 = reg(19200, 3, T)
        ANG3 = reg(19968, 3, T)
        POSB2 = reg(20736, T)
        QK = reg(0, KT, T)
        VD = reg(2048, TT, 512)
        BCH = reg(3072, 12, T)
        UC = reg(6144, 4, T + 2)
        CV = reg(7176, 4, T)
        OD = reg(8200, 4, T)
        CMASK = reg(9224, TT, T)
        LAMB = reg(9736, 4, 64)
        RD = reg(12544, 4, T)
        SQD = reg(13568, 4, T)
        FA = reg(17700, FT, T)
        FAF = reg(17700, FT * T)
        PTOK = reg(23400, 2, TT, T)
        PPT = reg(2048, 2, 2, T)
        PG = reg(0, KT, T)
        CU = reg(4096, KT, T)
        CVV = reg(6144, KT, T)
        VTS = reg(8192, TT, D)
        WS = reg(10240, 8, P)
        WST = reg(11264, 8, P)
        BSB = reg(12288, 8, P)
        HTOK = reg(4096, TT, D)
        HG = reg(6144, KT, SLOTS)
        AA = reg(7168, FF)
        AT = reg(9984, FT, SLOTS)
        YS = reg(12800, D)
        GTS = reg(13824, T)
        PSEL = reg(14080, TT, SLOTS)
        GSEL = reg(14336, TT, SLOTS)
        RW = reg(14592, KT, NE)
        RL = reg(14656, TT, NE)
        SEL = reg(14672, TT, NE)
        GATE = reg(14688, TT, NE)
        RANK = reg(14704, TT, NE)
        CNT = reg(14720, 4, NE)
        R64 = reg(14752, 2, TT, NE * NE)
        LOWE = reg(15008, NE, NE)
        IOTA = reg(15072, 2, SLOTS)
        TRI = reg(15328, P)
        ECOL = reg(15456, NE)
        NEG = reg(15464, 8)
        OVER = reg(15472, 4)
        OSLOT = [reg(15500 + 3072 * s, 3072) for s in range(RING)]
        OVERI = sb("overi", [1, 4], I32)
        ROUNDS = (2 * T - 1) // (SLOTS + 1)
        SQ2 = reg(27376, KT, T)
        OT = reg(0, TT, D)
        NSQ += [SQ2] * 9

        ROTS = [(lambda: QI[:, 0:2, :], 1, 2), (lambda: QI[:, 2:4, :], 1, 2), (lambda: KI, 1, 1), (lambda: KC, 0, 1)] + \
            [(lambda j=j: QT[:, 2 * j:2 * j + 2, :], 0, 2) for j in range(8)] + \
            [(lambda j=j: QK[:, 2 * j:2 * j + 2, :], 2, 2) for j in range(4)]
        SWAPS = [swap_a, swap_i, swap_d]
        PI = float(np.float32(np.pi))
        TWO_PI = [float(np.float32(v)) for v in (6.28125, 0.0019350051879882812, 3.0199159819567e-07)]
        assert abs(sum(TWO_PI) - 2 * np.pi) < 1e-10
        MAGIC = 1.5 * 2.0 ** 23

        def over_round(eng, r, body):
            n = eng.value_load(OVERI[0:1, 0:1], min_val=0, max_val=ROUNDS)
            with eng.If(n > r):
                body()

        def finish_sync(sp):
            sp.wait_ge(sem("over_ready"), 1)
            with sp.Fori(0, ROUNDS) as r:
                n = sp.value_load(OVERI[0:1, 0:1], min_val=0, max_val=ROUNDS)
                with sp.If(n > r):
                    e = sp.value_load(OVERI[0:1, bass.ds(r + 1, 1)], min_val=0, max_val=NE - 1)
                    sp.wait_ge(sem("psel_ready"), 4 * (r + NE) + 2)
                    for j in range(UPS + DOWNS):
                        if j >= RING:
                            sp.wait_ge(sem("over_acc"), (UPS + DOWNS) * r + j - RING + 1)
                        k, n_ = moe_shape(j)
                        sp.dma_start(OSLOT[j % RING][:, 0:k * n_].rearrange("p (k n) -> p k n", k=k), moe_src(j, e))\
                            .then_inc(sem(f"over_loaded_{j % RING}"), 16)
            sp.wait_ge(sem("toks_taken"), TK_OUT + 4)
            sp.dma_start(out[0].rearrange("(u p) n -> p u n", p=P), OT[:, :, :]).then_inc(sem("stored"), 16)
            sp.wait_ge(sem("stored"), 16)

        TK_P, TK_V, TK_W, TK_H, TK_OUT = 16, 18, 22, 24, 28

        def more_pool(pool, ch):
            def step(ins):
                ch(ins)
                ch.settle()
            q = sem("late_loaded")
            pool.wait_ge(sem("yb_ready"), 1)
            pool.dma_start(POSB.bitcast(I32), a["positions"][0].partition_broadcast(P)).then_inc(q, 16)
            pool.dma_start(POSB2.bitcast(I32), a["positions_2"][0].partition_broadcast(P)).then_inc(q, 16)
            pool.dma_start(PTOK[:, 0, :, :], a["p_2"][0, 0].rearrange("(u p) n -> p u n", p=P)).then_inc(sem("p_loaded"), 16)
            pool.dma_start(PTOK[:, 1, :, :], a["p_2"][1, 0].rearrange("(u p) n -> p u n", p=P)).then_inc(sem("p_loaded"), 16)
            pool.wait_ge(*took("oo", 8))
            pool.dma_start(LAMB.rearrange("p a b -> p (a b)"), a["a_lambda_2"][0].rearrange("a b -> (a b)").partition_broadcast(P))\
                .then_inc(sem("lam_loaded"), 16)
            step(pool.memset(UC[:, :, 0:2], 0.0))
            step(pool.memset(CMASK[:, :, :], 0.0))
            pool.affine_select(out=CMASK[:, :, :], in_=CMASK[:, :, :], compare_op=ALU.is_ge, fill=-BIG, base=0,
                               pattern=[[P, TT], [-1, T]], channel_multiplier=1).then_inc(sem("cmask_ready"), 1)
            pool.wait_ge(sem("cmask_ready"), 1)
            pool.wait_ge(*took("ao", 8))
            pool.dma_start(WS[:, :, :], a["c_w_s_2"][0].rearrange("g t s -> t g s")).then_inc(sem("ws_loaded"), 16)
            pool.wait_ge(*took("pp0", 8))
            pool.dma_start(BSB[:, :, :].rearrange("p g t -> p (g t)"), a["c_b_s_2"][0].rearrange("g t -> (g t)").partition_broadcast(P))\
                .then_inc(sem("bs_loaded"), 16)
            pool.wait_ge(sem("toks_taken"), TK_W + 2)
            pool.affine_select(out=WST[:, :, :], in_=WST[:, :, :], compare_op=ALU.is_ge, fill=0.0, base=0,
                               pattern=[[0, 8], [1, P]], channel_multiplier=-1).then_inc(sem("ws_masked"), 1)
            pool.wait_ge(sem("ws_masked"), 1)
            pool.wait_ge(*took("cout", 8))
            pool.dma_start(RW[:, :, :], a["router_w_2"][0].rearrange("(k p) e -> p k e", p=P)).then_inc(sem("rw_loaded"), 16)
            step(pool.memset(TRI, 1.0))
            step(pool.affine_select(out=TRI, in_=TRI, compare_op=ALU.is_gt, fill=0.0, base=0, pattern=[[1, P]],
                                    channel_multiplier=-1))
            step(pool.memset(LOWE[:, :, :], 1.0))
            step(pool.affine_select(out=LOWE[:, :, :], in_=LOWE[:, :, :], compare_op=ALU.is_gt, fill=0.0, base=0,
                                    pattern=[[1, NE], [-1, NE]], channel_multiplier=0))
            step(pool.iota(ECOL, [[1, NE]], base=0, channel_multiplier=0, allow_small_or_imprecise_dtypes=True))
            pool.iota(IOTA[:, :, :], [[SLOTS, 2], [1, SLOTS]], base=0, channel_multiplier=0,
                      allow_small_or_imprecise_dtypes=True).then_inc(sem("moe_const"), 1)

        def pe_rest(pe):
            mm = nc.tensor.matmul
            tr = nc.tensor.transpose

            def norm(i, after):
                pe_sum(bank[4][:, 0:T], NSQ[i], [(sem("norm_squares"), 2 * (i + 1))] + after, sem("norm_summed"))

            def rot(lo, hi):
                for i in range(lo, hi):
                    src, table, n = ROTS[i]
                    if i >= 2:
                        pe.wait_ge(sem("rot_done"), i - 1)
                    mm(bank[5 + i % 2][:, 0:n * T], SWAPS[table][:, :], src(), start=True, stop=True)\
                        .then_inc(sem("swapped"), 1)

            def tokens(n0, after, src, n):
                for s, v in after:
                    pe.wait_ge(s, v)
                for b in range(n):
                    if b >= 4:
                        pe.wait_ge(sem("toks_taken"), n0 + b - 3)
                    for j in range(4):
                        s = src(b, j)
                        ins = tr(bank[b % 4][:, j * P:(j + 1) * P], s, ident[:, :])
                    ins.then_inc(sem("toks_ready"), 1)

            norm(1, [took("eo", 8)])
            h = lambda k: hT[:, k, :]

            def values(b, w):
                for tt in range(TT):
                    for k in range(KT):
                        ins = mm(b[:, tt * P:(tt + 1) * P], hT[:, k, tt * P:(tt + 1) * P], w[:, k, P:2 * P],
                                 start=(k == 0), stop=(k == KT - 1))
                return ins

            def index_keys(b, w):
                for half in range(2):
                    for k in range(KT):
                        ins = mm(b[64 * half:64 * half + 64, 0:T], w[:, k, 256:320], hT[:, k, :], start=(k == 0), stop=(k == KT - 1))
                return ins

            def head_weights(b, w):
                for tt in range(TT):
                    for k in range(KT):
                        ins = mm(b[:, tt * NE:(tt + 1) * NE], hT[:, k, tt * P:(tt + 1) * P], w[:, k, 320:328],
                                 start=(k == 0), stop=(k == KT - 1))
                return ins

            pe_gemm("m1", h, [(sem("h_ready"), 2)], special={1: values})
            pe_gemm("m2", h, [took("m1", 4)], special={2: index_keys, 3: head_weights})
            pe.wait_ge(*took("m2", 4))
            rot(0, 4)
            pe.wait_ge(sem("rot_done"), 4)
            for n in range(16):
                tt, hh = n // 8, n % 8
                r = slice(64 * (hh % 2), 64 * (hh % 2) + 64)
                if n >= 2:
                    pe.wait_ge(sem("relu_done"), n - 1)
                mm(bank[7 if hh % 2 == 0 else 4][:, 0:T], QI[r, hh // 2, tt * P:(tt + 1) * P], KI[r, 0, :], start=True, stop=True)\
                    .then_inc(sem("index_ready"), 1)
            pe_gemm("q", h, [])
            pe_gemm("g", h, [took("q", 16)])
            rot(4, 12)
            pe.wait_ge(sem("rot_done"), 12)
            pe.wait_ge(*took("g", 16))
            pe.wait_ge(sem("relu_done"), 16)

            def attend(n0, count, logits, turned, result):
                logits(0)
                for b in range(count):
                    if b + 1 < count:
                        logits(b + 1)
                    pe.wait_ge(sem("weights_ready"), n0 + b + 1)
                    if b >= 2:
                        pe.wait_ge(sem("pt_ready"), n0 + b - 1)
                    turned(b)
                    pe.wait_ge(sem("pt_ready"), n0 + b + 1)
                    if b >= 2:
                        pe.wait_ge(sem("o_taken"), n0 + b - 1)
                    result(b)

            def logits(b):
                tt, hp = b % 2, b // 2
                if b >= 2:
                    pe.wait_ge(sem("logits_taken"), b - 1)
                for j in range(2):
                    ins = mm(bank[4 + b % 2][:, j * T:(j + 1) * T], QT[:, 2 * hp + j, tt * P:(tt + 1) * P], KC[:, 0, :],
                             start=True, stop=True)
                ins.then_inc(sem("logits_ready"), 1)

            def turned(b):
                for sc in range(2):
                    for j in range(2):
                        ins = tr(bank[6 + b % 2][:, (2 * sc + j) * P:(2 * sc + j + 1) * P],
                                 LG[:, b % 2, j, sc * P:(sc + 1) * P], ident[:, :])
                ins.then_inc(sem("turned_ready"), 1)

            def result(b):
                for sc in range(2):
                    ins = mm(bank[b % 2][:, 0:T], VTK[:, sc, :], PT[:, b % 2, sc * T:(sc + 1) * T], start=(sc == 0), stop=(sc == 1))
                ins.then_inc(sem("o_ready"), 1)

            attend(0, 16, logits, turned, result)
            pe_gemm("oo", lambda k: GT[:, k, :], [(sem("o_taken"), 16)])
            norm(2, [took("oo", 8)])
            norm(3, [])

            def values2(tt):
                def f(b, w):
                    for k in range(KT):
                        ins = mm(b[:, :], hT[:, k, tt * P:(tt + 1) * P], w[:, k, :], start=(k == 0), stop=(k == KT - 1))
                    return ins
                return f

            pe_gemm("qk", h, [(sem("h_ready"), 4)])
            pe_gemm("v", h, [took("qk", 8)], special={0: values2(0), 1: values2(1)})
            rot(12, 16)
            pe_gemm("bch", h, [took("v", 2)])
            pe.wait_ge(sem("rot_done"), 16)
            pe.wait_ge(*took("bch", 12))

            def logits2(b):
                tt, hh = b % 2, b // 2
                if b >= 2:
                    pe.wait_ge(sem("logits_taken"), 16 + b - 1)
                for c in range(2):
                    r = slice(64 * c, 64 * c + 64)
                    ins = mm(bank[4 + 2 * (b % 2) + c][:, 0:T], QK[r, hh, tt * P:(tt + 1) * P], QK[r, 4 + hh, :], start=True, stop=True)
                ins.then_inc(sem("logits_ready"), 1)

            def turned2(b):
                for sc in range(2):
                    ins = tr(bank[2 + b % 2][:, sc * P:(sc + 1) * P], LG[:, b % 2, 0, sc * P:(sc + 1) * P], ident[:, :])
                ins.then_inc(sem("turned_ready"), 1)

            def result2(b):
                for sc in range(2):
                    ins = mm(bank[b % 2][:, 0:P], VD[:, sc, (b // 2) * P:(b // 2 + 1) * P], PT[:, b % 2, sc * P:(sc + 1) * P],
                             start=(sc == 0), stop=(sc == 1))
                ins.then_inc(sem("o_ready"), 1)

            attend(16, 8, logits2, turned2, result2)
            pe.wait_ge(sem("squares_ready"), 4)
            for c in range(2):
                ins = mm(bank[4 + c][:, :], ones[:, :], SQD[:, 2 * c:2 * c + 2, :], start=True, stop=True)
            ins.then_inc(sem("o_summed"), 1)
            pe_gemm("ao", lambda k: OD[:, k, :] if k < 4 else CV[:, k - 4, :], [(sem("o_normed"), 1)])
            norm(4, [took("ao", 8)])
            pe.wait_ge(sem("h_ready"), 5)

            def f13(j, i):
                w = wait_chunk(pe, "f13", j, i)
                if j >= 2 or not isinstance(i, int):
                    pe.wait_ge(sem("silu_taken") if j % 2 == 0 else sem("gate_taken"), 2 * (j // 2) + 4 * i)
                for m in range(2):
                    for k in range(KT):
                        ins = mm(bank[2 * (j % 2) + m][:, 0:T], w[:, k, m * P:(m + 1) * P], hT[:, k, :], start=(k == 0), stop=(k == KT - 1))
                    ins.then_inc(acc_ready, 1)

            each_chunk(pe, "f13", f13, first=1)
            pe_gemm("f2", lambda k: FA[:, k, :], [(sem("gate_taken"), FT)])

            def embed(i):
                pe.wait_ge(sem("p_loaded"), 32)
                for c in range(2):
                    for tt in range(TT):
                        ins = tr(bank[7][:, c * T + tt * P:c * T + (tt + 1) * P], PTOK[:, i, tt, c * P:(c + 1) * P], ident[:, :])
                ins.then_inc(sem("toks_ready"), 1)

            def ple(i, nrm, before):
                norm(nrm, [before])
                pe_gemm(f"pg{i}", h, [(sem("h_ready"), nrm + 1)])
                pe_gemm(f"pp{i}", lambda k: PPT[:, i, k, :], [took(f"pg{i}", 8), (sem("toks_taken"), TK_P + 2)])

            embed(0)
            pe.wait_ge(sem("toks_taken"), TK_P + 1)
            embed(1)
            ple(0, 5, took("f2", 8))
            norm(6, [took("pp0", 8), (sem("embedded"), 1)])
            pe_gemm("cin", h, [(sem("h_ready"), 7)])
            pe_sum(bank[4][:, 0:T], CVV, [took("cin", 16)], sem("mean_summed"))
            pe_sum(bank[5][:, 0:T], SQ2, [(sem("squares_ready"), 5)], sem("var_summed"))
            tokens(TK_V, [(sem("cln_done"), 1)], lambda b, j: CVV[:, 4 * (b % 2) + j, (b // 2) * P:(b // 2 + 1) * P], 4)
            pe.wait_ge(sem("ws_loaded"), 16)
            for b in range(2):
                for j in range(4):
                    ins = tr(bank[6 + b][:, j * P:(j + 1) * P], WS[:, 4 * b + j, :], ident[:, :])
                ins.then_inc(sem("toks_ready"), 1)
            pe.wait_ge(sem("toks_taken"), TK_V + 4)
            pe.wait_ge(sem("ws_masked"), 1)
            for g in range(8):
                for tt in range(TT):
                    ins = mm(bank[g // 2][:, (g % 2) * T + tt * P:(g % 2) * T + (tt + 1) * P], VTS[:, tt, g * P:(g + 1) * P], WST[:, g, :],
                             start=True, stop=True)
                if g % 2 == 1:
                    ins.then_inc(sem("spatial_ready"), 1)
            pe_gemm("cout", lambda k: CU[:, k, :], [(sem("spatial_taken"), 4)])
            norm(7, [took("cout", 8)])
            tokens(TK_H, [(sem("h_ready"), 8)], lambda b, j: hT[:, 4 * (b % 2) + j, (b // 2) * P:(b // 2 + 1) * P], 4)
            pe.wait_ge(sem("rw_loaded"), 16)
            for tt in range(TT):
                for k in range(KT):
                    ins = mm(bank[5][:, tt * NE:(tt + 1) * NE], hT[:, k, tt * P:(tt + 1) * P], RW[:, k, :], start=(k == 0), stop=(k == KT - 1))
            ins.then_inc(sem("router_ready"), 1)
            pe.wait_ge(sem("sel_ready"), 1)
            mm(bank[6][:, 0:NE], TRI, SEL[:, 0, :], start=True, stop=True)
            mm(bank[6][:, NE:2 * NE], ones[:, :], SEL[:, 0, :], start=True, stop=False)
            mm(bank[6][:, NE:2 * NE], TRI, SEL[:, 1, :], start=False, stop=True)
            mm(bank[6][:, 2 * NE:3 * NE], ones[:, :], SEL[:, 0, :], start=True, stop=False)
            mm(bank[6][:, 2 * NE:3 * NE], ones[:, :], SEL[:, 1, :], start=False, stop=True).then_inc(sem("rank_ready"), 1)
            pe.wait_ge(sem("toks_taken"), TK_H + 4)
            pe.wait_ge(sem("rank_taken"), 1)

            def expert(i, acc, acc0, weights):
                pe.wait_ge(sem("psel_ready"), 4 * i + 2)
                for ct in range(KT):
                    for tt in range(TT):
                        ins = mm(bank[4 + ct // 4][:, (ct % 4) * P:(ct % 4 + 1) * P], HTOK[:, tt, ct * P:(ct + 1) * P], PSEL[:, tt, :],
                                 start=(tt == 0), stop=(tt == 1))
                    if ct % 4 == 3:
                        ins.then_inc(sem("gather_ready"), 1)
                pe.wait_ge(sem("psel_ready"), 4 * i + 4)
                for tt in range(TT):
                    ins = tr(bank[6][:, tt * P:(tt + 1) * P], GSEL[:, tt, :], ident[:, :])
                ins.then_inc(sem("gsel_turned"), 1)
                pe.wait_ge(sem("hg_taken"), 2 * i + 2)
                for j in range(UPS):
                    w = weights(j)
                    if j >= 4:
                        pe.wait_ge(sem("moe_silu") if j % 2 == 0 else sem("moe_gated"), (UPS // 2) * i + j // 2 - 1)
                    for k in range(KT):
                        ins = mm(bank[2 * (j % 2) + (j // 2) % 2][:, 0:WC], HG[:, k, :], w[:, k, :], start=(k == 0), stop=(k == KT - 1))
                    ins.then_inc(acc, 1)
                pe.wait_ge(sem("moe_gated"), (UPS // 2) * (i + 1))
                pe.wait_ge(sem("gs_taken"), i + 1)
                for g in range(6):
                    if g >= 4:
                        pe.wait_ge(sem("at_taken"), 6 * i + g - 3)
                    for f in range(4 * g, min(4 * g + 4, FT)):
                        ins = tr(bank[4 + g % 4][:, (f % 4) * P:(f % 4 + 1) * P], AA[:, f * P:(f + 1) * P], ident[:, :])
                    ins.then_inc(sem("at_ready"), 1)
                for m in range(DOWNS):
                    w = weights(UPS + m)
                    f0 = sum(W2F[:m])
                    for f in range(f0, f0 + W2F[m]):
                        if f % 4 == 0:
                            pe.wait_ge(sem("at_taken"), 6 * i + f // 4 + 1)
                        for half in range(2):
                            ins = mm(bank[half][:, :], AT[:, f, :], w[:, f - f0, 512 * half:512 * half + 512], start=(f == 0), stop=(f == FT - 1))
                    ins.then_inc(acc, 1)
                pe.wait_ge(sem("ys_taken"), 2 * i + 2)
                for ct in range(KT):
                    ins = mm(bank[2 + ct // 2][:, (ct % 2) * T:(ct % 2 + 1) * T], YS[:, ct * P:(ct + 1) * P], GTS, start=True, stop=True)
                    if ct % 2 == 1:
                        ins.then_inc(sem("scat_ready"), 1)

            ph = phases["moe"]
            with pe.Fori(0, NE) as e:
                expert(e, acc_ready, ph["t0"], lambda j: wait_chunk(pe, "moe", j, e))
            pe.wait_ge(sem("over_ready"), 1)
            with pe.Fori(0, ROUNDS) as r:
                n = pe.value_load(OVERI[0:1, 0:1], min_val=0, max_val=ROUNDS)
                with pe.If(n > r):
                    def over_weights(j):
                        pe.wait_ge(sem(f"over_loaded_{j % RING}"), 16 * (j // RING + 1) + 16 * ((UPS + DOWNS) // RING) * r)
                        k, n_ = moe_shape(j)
                        return OSLOT[j % RING][:, 0:k * n_].rearrange("p (k n) -> p k n", k=k)
                    expert(r + NE, sem("over_acc"), 0, over_weights)
            ple(1, 8, (sem("moe_done"), 1))
            norm(9, [took("pp1", 8), (sem("embedded"), 2)])
            tokens(TK_OUT, [(sem("h_ready"), 10)], lambda b, j: hT[:, 4 * (b % 2) + j, (b // 2) * P:(b // 2 + 1) * P], 4)


        def act_rest(act, ch, A, norm):
            act.wait_ge(sem("angles_ready"), 1)
            for k in range(3):
                A(ROT[:, k, 1, :], ANG[:, k, :], ACT.Sin, scale=small[:, 11 + k:12 + k]).then_inc(sem("rot_tables"), 1)
            A(ROT[:, :, 0, :], ANG2[:, :, :], ACT.Sin).then_inc(sem("rot_tables"), 1)
            norm(1, [took("eo", 8)])

            def take_m1(q, lin, b):
                if q == 0:
                    return A(KC[:, 0, :], b, ACT.Copy)
                if q == 1:
                    return A(VTK[:, :, :], b.rearrange("p (u v) -> p u v", u=TT), ACT.Copy)
                return A(QI[:, q - 2, :], b, ACT.Copy)

            def take_m2(q, lin, b):
                if q < 2:
                    return A(QI[:, 2 + q, :], b, ACT.Copy)
                if q == 2:
                    return A(KI[:, 0, :], b, ACT.Copy)
                return A(WI[:, :, :], b[:, 0:TT * NE].rearrange("p (u e) -> p u e", u=TT), ACT.Copy, scale=NE ** -0.5)

            take_gemm(act, "m1", take_m1)
            take_gemm(act, "m2", take_m2)
            for n in range(16):
                act.wait_ge(sem("index_ready"), n + 1)
                if n >= 2:
                    act.wait_ge(sem("score_added"), n - 1)
                A(RELU[:, n % 2, :], bank[7 if n % 2 == 0 else 4][:, 0:T], ACT.Relu, scale=HD ** -0.5).then_inc(sem("relu_done"), 1)
            take_gemm(act, "q", lambda q, lin, b: A(QT[:, q, :], b, ACT.Copy))
            take_gemm(act, "g", lambda q, lin, b: A(GT[:, q, :], b, ACT.Silu))

            def attend(n0, count, banks, width):
                def exps(b):
                    act.wait_ge(sem("max_ready"), n0 + b + 1)
                    for j in range(2):
                        A(LG[:, b % 2, j, :], LG[:, b % 2, j, :], ACT.Exp, bias=MX[:, b % 2, j:j + 1],
                          accum_out=SM[:, b % 2, j:j + 1]).then_inc(sem("exps_ready"), 1)
                exps(0)
                for b in range(count):
                    if b + 1 < count:
                        exps(b + 1)
                    act.wait_ge(sem("turned_ready"), n0 + b + 1)
                    if b >= 2:
                        act.wait_ge(sem("o_ready"), n0 + b - 1)
                    A(PT[:, b % 2, 0:width], bank[banks + b % 2][:, 0:width], ACT.Copy).then_inc(sem("pt_ready"), 1)

            attend(0, 16, 6, 2 * T)
            norm(2, [took("oo", 8)])
            norm(3, [(sem("h_ready"), 3)])
            take_gemm(act, "qk", lambda q, lin, b: A(QK[:, q, :], b, ACT.Copy))
            take_gemm(act, "v", lambda q, lin, b: A(VD[:, q, :], bank[q][:, :], ACT.Copy))
            take_gemm(act, "bch", lambda q, lin, b: A(BCH[:, q, :], b, ACT.Copy))
            act.wait_ge(sem("lam_sums"), 1)
            A(small[:, 14:16], small[:, 14:16], ACT.Exp).then_inc(sem("lam_exps"), 1)
            attend(16, 8, 2, T)
            act.wait_ge(sem("o_taken"), 24)
            A(SQD[:, :, :], OD[:, :, :], ACT.Square).then_inc(sem("squares_ready"), 1)
            act.wait_ge(sem("o_summed"), 1)
            for c in range(2):
                A(RD[:, 2 * c:2 * c + 2, :], bank[4 + c][:, :].rearrange("p (h t) -> p h t", h=2), ACT.Sqrt, bias=1e-6, scale=1.0 / P)\
                    .then_inc(sem("rooted"), 1)
            norm(4, [took("ao", 8)])

            def silu(j, i):
                if j % 2 == 0:
                    for m in range(2):
                        act.wait_ge(acc_ready, phases["f13"]["t0"] + 2 * j + m + 1 + 8 * i)
                        f = j + m + 4 * i
                        A(FAF[:, bass.ds(f * T, T)], bank[m][:, 0:T], ACT.Silu).then_inc(sem("silu_taken"), 1)

            each_chunk(act, "f13", silu)
            for i in range(2):
                act.wait_ge(sem("toks_ready"), TK_P + 1 + i)
                A(PPT[:, i, :, :], bank[7][:, :].rearrange("p (c t) -> p c t", c=2), ACT.Copy).then_inc(sem("toks_taken"), 1)
            norm(5, [took("f2", 8)])
            take_gemm(act, "pg0", lambda q, lin, b: A(PG[:, q, :], b, ACT.Sigmoid))
            norm(6, [(sem("embedded"), 1)])
            take_gemm(act, "cin", lambda q, lin, b: A(CU[:, q, :] if q < KT else CVV[:, q - KT, :], b, ACT.Gelu))
            act.wait_ge(sem("centred"), 6)
            A(SQ2[:, :, :], CVV[:, :, :], ACT.Square).then_inc(sem("squares_ready"), 1)
            act.wait_ge(sem("var_summed"), 3)
            A(nr[:, :], bank[5][:, 0:T], ACT.Sqrt, bias=1e-5, scale=1.0 / D).then_inc(sem("rooted"), 1)

            def tokens(n0, dst):
                for b in range(4):
                    act.wait_ge(sem("toks_ready"), n0 + b + 1)
                    A(dst[:, b // 2, 512 * (b % 2):512 * (b % 2) + 512], bank[b][:, :], ACT.Copy).then_inc(sem("toks_taken"), 1)

            tokens(TK_V, VTS)
            for b in range(2):
                act.wait_ge(sem("toks_ready"), TK_W + b + 1)
                A(WST[:, 4 * b:4 * b + 4, :], bank[6 + b][:, :].rearrange("p (g t) -> p g t", g=4), ACT.Copy).then_inc(sem("toks_taken"), 1)
            norm(7, [took("cout", 8)])
            tokens(TK_H, HTOK)
            act.wait_ge(sem("gates_centred"), 1)
            A(GATE[:, :, :], GATE[:, :, :], ACT.Exp).then_inc(sem("gate_exps"), 1)

            def expert(i, acc, acc0):
                for g in range(2):
                    act.wait_ge(sem("gather_ready"), 2 * i + (g + 1))
                    A(HG[:, 4 * g:4 * g + 4, :], bank[4 + g][:, :].rearrange("p (k s) -> p k s", k=4), ACT.Copy).then_inc(sem("hg_taken"), 1)
                act.wait_ge(sem("gsel_turned"), i + 1)
                A(GTS, bank[6][:, 0:T], ACT.Copy).then_inc(sem("gs_taken"), 1)
                for j in range(0, UPS, 2):
                    act.wait_ge(acc, acc0 + (j + 1))
                    A(AA[:, WC * (j // 2):WC * (j // 2) + WC], bank[(j // 2) % 2][:, 0:WC], ACT.Silu).then_inc(sem("moe_silu"), 1)
                for g in range(6):
                    n = min(4, FT - 4 * g)
                    act.wait_ge(sem("at_ready"), 6 * i + (g + 1))
                    A(AT[:, 4 * g:4 * g + n, :], bank[4 + g % 4][:, 0:n * P].rearrange("p (k s) -> p k s", k=n), ACT.Copy)\
                        .then_inc(sem("at_taken"), 1)
                for half in range(2):
                    act.wait_ge(acc, acc0 + (UPS + DOWNS))
                    A(YS[:, 512 * half:512 * half + 512], bank[half][:, :], ACT.Copy).then_inc(sem("ys_taken"), 1)

            with act.Fori(0, NE) as e:
                expert(e, acc_ready, (UPS + DOWNS) * e + phases["moe"]["t0"])
            act.wait_ge(sem("over_ready"), 1)
            with act.Fori(0, ROUNDS) as r:
                over_round(act, r, lambda: expert(r + NE, sem("over_acc"), (UPS + DOWNS) * r))
            norm(8, [(sem("moe_done"), 1)])
            take_gemm(act, "pg1", lambda q, lin, b: A(PG[:, q, :], b, ACT.Sigmoid))
            norm(9, [(sem("embedded"), 2)])
            tokens(TK_OUT, OT)

        def dve_rest(dve, V, ch, step, norm):
            add_to_x = lambda q, lin, b: V.tensor_tensor(xT[:, q, :], b, xT[:, q, :], ALU.add)
            norm(1, lambda ct: gs[:, 8 + ct:9 + ct], lambda ct: mod[:, 1, ct:ct + 1])
            step(V.tensor_scalar(ANG3.bitcast(I32)[:, 2, :], POSB.bitcast(I32), 6, None, ALU.arith_shift_right))
            ch(V.tensor_copy(CHUNKS, ANG3.bitcast(I32)[:, 2, :]))
            step(V.tensor_scalar(POSI[:, :], POSI[:, :], 6, None, ALU.arith_shift_right))
            step(V.tensor_copy(CHC, POSI[:, :]))

            dve.wait_ge(sem("rot_tables"), 4)

            def rotate(lo, hi):
                for i in range(lo, hi):
                    src, table, n = ROTS[i]
                    z = src()
                    dve.wait_ge(sem("swapped"), i + 1)
                    if i >= 2:
                        dve.wait_ge(sem("rot_done"), i - 1)
                    ch(V.tensor_tensor(SWP[:, i % 2, 0:n, :], bank[5 + i % 2][:, 0:n * T].rearrange("p (n t) -> p n t", n=n),
                                       ROT[:, table, 1, :].unsqueeze(1).to_broadcast([P, n, T]), ALU.mult))
                    step(V.tensor_tensor(z, z, ROT[:, table, 0, :].unsqueeze(1).to_broadcast([P, n, T]), ALU.mult))
                    V.tensor_tensor(z, z, SWP[:, i % 2, 0:n, :], ALU.add).then_inc(sem("rot_done"), 1)

            rotate(0, 4)
            dve.wait_ge(*took("m2", 4))
            for n in range(16):
                tt, hh = n // 8, n % 8
                dve.wait_ge(sem("relu_done"), n + 1)
                if hh == 0:
                    ins = V.tensor_scalar(CUR[:, tt, :], RELU[:, n % 2, :], WI[:, tt, 0:1], None, ALU.mult)
                else:
                    dve.wait_ge(sem("score_added"), n)
                    ins = V.scalar_tensor_tensor(CUR[:, tt, :], RELU[:, n % 2, :], WI[:, tt, hh:hh + 1], CUR[:, tt, :], ALU.mult, ALU.add)
                ins.then_inc(sem("score_added"), 1)
            dve.wait_ge(sem("score_added"), 16)
            for tt in range(TT):
                ch(V.tensor_scalar(ADM[:, tt, :], CHUNKS, CHC[:, tt:tt + 1], None, ALU.is_le))
            ch.settle()
            ch(V.tensor_tensor(CUR[:, :, :], CUR[:, :, :], ADM[:, :, :], ALU.mult))
            step(V.tensor_scalar(MASK[:, :, :], ADM[:, :, :], BIG, -BIG, ALU.mult, ALU.add))
            step(V.tensor_tensor(CUR[:, :, :], CUR[:, :, :], MASK[:, :, :], ALU.add))
            for n in range(TOPK // 8):
                for tt in range(TT):
                    ch(V.max(TOP[:, tt, :], CUR[:, tt, :]))
                ch.settle()
                for tt in range(TT):
                    ch(V.match_replace(CUR[:, tt, :], TOP[:, tt, :], CUR[:, tt, :], -3.0e38))
                ch.settle()
            step(V.scalar_tensor_tensor(CUR[:, :, :], CUR[:, :, :], -2.0e38, ADM[:, :, :], ALU.is_le, ALU.mult))
            step(V.tensor_scalar(MASK[:, :, :], CUR[:, :, :], BIG, -BIG, ALU.mult, ALU.add))
            rotate(4, 12)

            def attend(n0, count, scores, weights, result):
                scores(0)
                for b in range(count):
                    if b + 1 < count:
                        if b >= 1:
                            dve.wait_ge(sem("turned_ready"), n0 + b)
                        scores(b + 1)
                    dve.wait_ge(sem("exps_ready"), 2 * (n0 + b + 1))
                    weights(b)
                    if b >= 1:
                        dve.wait_ge(sem("o_ready"), n0 + b)
                        result(b - 1)
                dve.wait_ge(sem("o_ready"), n0 + count)
                result(count - 1)

            def largest(b):
                ch.settle()
                V.tensor_reduce(MX[:, b % 2, :], LG[:, b % 2, :, :], AX_X, ALU.max, negate=True).then_inc(sem("max_ready"), 1)

            def scores(b):
                dve.wait_ge(sem("logits_ready"), b + 1)
                m = MASK[:, b % 2, :].unsqueeze(1).to_broadcast([P, 2, T])
                V.scalar_tensor_tensor(LG[:, b % 2, :, :], bank[4 + b % 2][:, :].rearrange("p (j s) -> p j s", j=2), P ** -0.5, m,
                                       ALU.mult, ALU.add).then_inc(sem("logits_taken"), 1)
                dve.wait_ge(sem("logits_taken"), b + 1)
                largest(b)

            def weights(b):
                step(V.reciprocal(SM[:, b % 2, :], SM[:, b % 2, :]))
                V.tensor_tensor(LG[:, b % 2, :, :], LG[:, b % 2, :, :], SM[:, b % 2, :].unsqueeze(2).to_broadcast([P, 2, T]), ALU.mult)\
                    .then_inc(sem("weights_ready"), 1)

            def result(b):
                tt, hp = b % 2, b // 2
                o = GT[:, 2 * hp:2 * hp + 2, tt * P:(tt + 1) * P]
                V.tensor_tensor(o, o, bank[b % 2][:, 0:T].rearrange("p (j t) -> p j t", j=2), ALU.mult).then_inc(sem("o_taken"), 1)

            attend(0, 16, scores, weights, result)
            take_gemm(dve, "oo", lambda q, lin, b: V.scalar_tensor_tensor(
                xT[:, q, :], b, mod[:, 1, 16 + q:17 + q], xT[:, q, :], ALU.mult, ALU.add))
            norm(2, lambda ct: col("final_g", ct), dst=xT)
            dve.wait_ge(sem("h_ready"), 3)
            norm(3, lambda ct: col("mix0", ct))

            rotate(12, 16)
            dve.wait_ge(sem("lam_loaded"), 16)
            step(V.tensor_tensor(LAMB[:, 0:4:2, :], LAMB[:, 0:4:2, :], LAMB[:, 1:4:2, :], ALU.mult))
            V.tensor_reduce(small[:, 14:16], LAMB[:, 0:4:2, :], AX_X, ALU.add).then_inc(sem("lam_sums"), 1)
            dve.wait_ge(sem("cmask_ready"), 1)
            dve.wait_ge(*took("bch", 12))
            step(V.tensor_tensor(UC[:, :, 2:2 + T], BCH[:, 4:8, :], BCH[:, 8:12, :], ALU.mult))
            for ct in range(4):
                ch(V.tensor_scalar(CV[:, ct, :], UC[:, ct, 0:T], acw[:, ct, 0:1], None, ALU.mult))
            ch.settle()
            for j in (1, 2):
                for ct in range(4):
                    ch(V.scalar_tensor_tensor(CV[:, ct, :], UC[:, ct, j:j + T], acw[:, ct, j:j + 1], CV[:, ct, :], ALU.mult, ALU.add))
                ch.settle()
            ch(V.tensor_tensor(CV[:, :, :], CV[:, :, :], BCH[:, 0:4, :], ALU.mult))
            dve.wait_ge(sem("lam_exps"), 1)
            nlam = small[:, 7:8]
            step(V.tensor_scalar(nlam, small[:, 15:16], small[:, 14:15], LAM0, ALU.subtract, ALU.subtract))

            def scores2(b):
                dve.wait_ge(sem("logits_ready"), 16 + b + 1)
                for c in range(2):
                    ins = V.scalar_tensor_tensor(LG[:, b % 2, c, :], bank[4 + 2 * (b % 2) + c][:, 0:T], HD ** -0.5, CMASK[:, b % 2, :],
                                                 ALU.mult, ALU.add)
                    if c == 0:
                        ch(ins)
                ins.then_inc(sem("logits_taken"), 1)
                dve.wait_ge(sem("logits_taken"), 16 + b + 1)
                largest(b)

            def weights2(b):
                step(V.reciprocal(SM[:, b % 2, :], SM[:, b % 2, :]))
                ch(V.tensor_tensor(SM[:, b % 2, 1:2], SM[:, b % 2, 1:2], nlam, ALU.mult))
                step(V.tensor_scalar(LG[:, b % 2, 0, :], LG[:, b % 2, 0, :], SM[:, b % 2, 0:1], None, ALU.mult))
                V.scalar_tensor_tensor(LG[:, b % 2, 0, :], LG[:, b % 2, 1, :], SM[:, b % 2, 1:2], LG[:, b % 2, 0, :], ALU.mult, ALU.add)\
                    .then_inc(sem("weights_ready"), 1)

            def result2(b):
                V.tensor_copy(OD[:, b // 2, (b % 2) * P:(b % 2 + 1) * P], bank[b % 2][:, 0:P]).then_inc(sem("o_taken"), 1)

            attend(16, 8, scores2, weights2, result2)
            dve.wait_ge(sem("rooted"), 5)
            ch(V.tensor_scalar(OD[:, :, :], OD[:, :, :], subln, 1.0 - LAM0, ALU.mult, ALU.mult))
            step(V.reciprocal(RD[:, :, :], RD[:, :, :]))
            V.tensor_tensor(OD[:, :, :], OD[:, :, :], RD[:, :, :], ALU.mult).then_inc(sem("o_normed"), 1)
            take_gemm(dve, "ao", add_to_x)
            norm(4, lambda ct: col("ffn0", ct))

            def gated(j, i):
                if j % 2 == 1:
                    for m in range(2):
                        f = j - 1 + m + 4 * i
                        dve.wait_ge(acc_ready, phases["f13"]["t0"] + 2 * j + m + 1 + 8 * i)
                        dve.wait_ge(sem("silu_taken"), j + m + 4 * i)
                        V.tensor_tensor(FAF[:, bass.ds(f * T, T)], FAF[:, bass.ds(f * T, T)], bank[2 + m][:, 0:T], ALU.mult)\
                            .then_inc(sem("gate_taken"), 1)

            each_chunk(dve, "f13", gated)
            xF = xT[:, :, :].rearrange("p k t -> p (k t)")

            def take_f2(q, lin, b):
                x = xF[:, bass.ds((q + lin) * T, T)]
                return V.tensor_tensor(x, b, x, ALU.add)

            take_gemm(dve, "f2", take_f2)

            def ple(i, nrm):
                norm(nrm, lambda ct: col(f"ple{i}", ct))
                take_gemm(dve, f"pp{i}", lambda q, lin, b: V.tensor_tensor(PG[:, q, :], PG[:, q, :], b, ALU.mult))
                dve.wait_ge(*took(f"pp{i}", 8))
                V.tensor_tensor(xT[:, :, :], xT[:, :, :], PG[:, :, :], ALU.add).then_inc(sem("embedded"), 1)

            ple(0, 5)
            dve.wait_ge(sem("embedded"), 1)
            norm(6, lambda ct: col("mix1", ct))
            dve.wait_ge(sem("mean_summed"), 3)
            mean = bank[4][:, 0:T].unsqueeze(1).to_broadcast([P, KT, T])
            V.scalar_tensor_tensor(CVV[:, :, :], mean, -1.0 / D, CVV[:, :, :], ALU.mult, ALU.add).then_inc(sem("centred"), 1)
            dve.wait_ge(sem("rooted"), 6)
            step(V.reciprocal(nr[:, :], nr[:, :]))
            for ct in range(KT):
                ch(V.scalar_tensor_tensor(CVV[:, ct, :], CVV[:, ct, :], col("cln_g", ct), nr[:, :], ALU.mult, ALU.mult))
            ch.settle()
            for ct in range(KT):
                ins = V.tensor_scalar(CVV[:, ct, :], CVV[:, ct, :], col("cln_b", ct), None, ALU.add)
                if ct < KT - 1:
                    ch(ins)
            ins.then_inc(sem("cln_done"), 1)
            dve.wait_ge(sem("bs_loaded"), 16)
            for b in range(4):
                dve.wait_ge(sem("spatial_ready"), b + 1)
                v = bank[b][:, :].rearrange("p (g u t) -> p g u t", g=2, u=TT)
                bs = BSB[:, 2 * b:2 * b + 2, :].unsqueeze(2).to_broadcast([P, 2, TT, P])
                sp_ = VTS[:, b // 2, 512 * (b % 2):512 * (b % 2) + 512].rearrange("p (g u t) -> p g u t", g=2, u=TT)
                u = CU[:, 2 * b:2 * b + 2, :].rearrange("p g (u t) -> p g u t", u=TT)
                if b == 0:
                    dve.wait_ge(sem("spatial_ready"), 4)
                step(V.tensor_tensor(sp_, v, bs, ALU.add))
                V.tensor_tensor(u, u, sp_, ALU.mult).then_inc(sem("spatial_taken"), 1)
            take_gemm(dve, "cout", add_to_x)
            norm(7, lambda ct: col("ffn1", ct))
            dve.wait_ge(sem("router_ready"), 1)
            step(V.tensor_copy(RL[:, :, :], bank[5][:, 0:TT * NE].rearrange("p (u e) -> p u e", u=TT)))
            dve.wait_ge(sem("moe_const"), 1)
            big = [R64[:, m, :, :].rearrange("p u (e f) -> p u e f", e=NE) for m in range(2)]
            own = RL[:, :, :].unsqueeze(3).to_broadcast([P, TT, NE, NE])
            other = RL[:, :, :].unsqueeze(2).to_broadcast([P, TT, NE, NE])
            ch(V.tensor_tensor(big[0], other, own, ALU.is_gt))
            step(V.tensor_tensor(big[1], other, own, ALU.is_equal))
            step(V.tensor_tensor(big[1], big[1], LOWE[:, :, :].unsqueeze(1).to_broadcast([P, TT, NE, NE]), ALU.mult))
            step(V.tensor_tensor(big[0], big[0], big[1], ALU.add))
            ch(V.tensor_reduce(SEL[:, :, :], big[0], AX_X, ALU.add))
            step(V.tensor_reduce(NEG[:, 0:TT], RL[:, :, :], AX_X, ALU.max))
            ch(V.tensor_scalar(SEL[:, :, :], SEL[:, :, :], 1.5, None, ALU.is_lt))
            V.tensor_tensor(GATE[:, :, :], RL[:, :, :], NEG[:, 0:TT].unsqueeze(2).to_broadcast([P, TT, NE]), ALU.subtract)\
                .then_inc(sem("gates_centred"), 1)
            dve.wait_ge(sem("gate_exps"), 1)
            ch.settle()
            step(V.tensor_tensor(GATE[:, :, :], GATE[:, :, :], SEL[:, :, :], ALU.mult))
            step(V.tensor_reduce(NEG[:, 0:TT], GATE[:, :, :], AX_X, ALU.add))
            step(V.reciprocal(NEG[:, 0:TT], NEG[:, 0:TT]))
            V.tensor_tensor(GATE[:, :, :], GATE[:, :, :], NEG[:, 0:TT].unsqueeze(2).to_broadcast([P, TT, NE]), ALU.mult)\
                .then_inc(sem("sel_ready"), 1)
            dve.wait_ge(sem("sel_ready"), 1)
            dve.wait_ge(sem("rank_ready"), 1)
            ch(V.tensor_copy(RANK[:, :, :], bank[6][:, 0:TT * NE].rearrange("p (u e) -> p u e", u=TT)))
            V.tensor_copy(CNT[:, 0, :], bank[6][:, 2 * NE:3 * NE]).then_inc(sem("rank_taken"), 1)
            dve.wait_ge(sem("rank_taken"), 1)
            step(V.tensor_scalar(CNT[:, 1, :], CNT[:, 0, :], float(SLOTS), None, ALU.is_gt))
            ch(V.tensor_reduce(OVER[:, 0:1], CNT[:, 1, :], AX_X, ALU.add))
            step(V.tensor_tensor(big[0][:, 0], LOWE[:, :, :], CNT[:, 1, :].unsqueeze(1).to_broadcast([P, NE, NE]), ALU.mult))
            step(V.tensor_reduce(CNT[:, 2, :], big[0][:, 0], AX_X, ALU.add))
            ch(V.tensor_tensor(CNT[:, 3, :], CNT[:, 1, :], ECOL, ALU.mult))
            for r in range(ROUNDS):
                ch.settle()
                step(V.scalar_tensor_tensor(CNT[:, 0, :], CNT[:, 2, :], float(r), CNT[:, 3, :], ALU.is_equal, ALU.mult))
                ch(V.tensor_reduce(OVER[:, r + 1:r + 2], CNT[:, 0, :], AX_X, ALU.add))
            ch.settle()
            V.tensor_copy(OVERI[0:1, :], OVER[0:1, :]).then_inc(sem("over_ready"), 1)

            def expert(i, e, which, acc, acc0):
                for tt in range(TT):
                    V.tensor_scalar(PSEL[:, tt, :], IOTA[:, which, :], RANK[:, tt, bass.ds(e, 1)], SEL[:, tt, bass.ds(e, 1)],
                                    ALU.is_equal, ALU.mult).then_inc(sem("psel_ready"), 1)
                for tt in range(TT):
                    dve.wait_ge(sem("psel_ready"), 4 * i + (tt + 1))
                    V.tensor_scalar(GSEL[:, tt, :], PSEL[:, tt, :], GATE[:, tt, bass.ds(e, 1)], None, ALU.mult)\
                        .then_inc(sem("psel_ready"), 1)
                for j in range(1, UPS, 2):
                    dve.wait_ge(acc, acc0 + (j + 1))
                    dve.wait_ge(sem("moe_silu"), (UPS // 2) * i + (j // 2 + 1))
                    aa = AA[:, WC * (j // 2):WC * (j // 2) + WC]
                    V.tensor_tensor(aa, aa, bank[2 + (j // 2) % 2][:, 0:WC], ALU.mult).then_inc(sem("moe_gated"), 1)
                for g in range(4):
                    dve.wait_ge(sem("scat_ready"), 4 * i + (g + 1))
                    x = xT[:, 2 * g:2 * g + 2, :]
                    V.tensor_tensor(x, bank[2 + g][:, :].rearrange("p (k t) -> p k t", k=2), x, ALU.add).then_inc(sem("scat_taken"), 1)
                dve.wait_ge(sem("scat_taken"), 4 * i + 4)
                V.memset(NEG[:, 0:1], 0.0)

            with dve.Fori(0, NE) as e:
                expert(e, e, 0, acc_ready, (UPS + DOWNS) * e + phases["moe"]["t0"])

            def over(r):
                e = dve.value_load(OVERI[0:1, bass.ds(r + 1, 1)], min_val=0, max_val=NE - 1)
                expert(r + NE, e, 1, sem("over_acc"), (UPS + DOWNS) * r)

            dve.wait_ge(sem("over_ready"), 1)
            with dve.Fori(0, ROUNDS) as r:
                over_round(dve, r, lambda: over(r))
            V.memset(NEG[:, 1:2], 0.0).then_inc(sem("moe_done"), 1)
            dve.wait_ge(sem("moe_done"), 1)
            ple(1, 8)
            dve.wait_ge(sem("embedded"), 2)
            norm(9, lambda ct: col("fnorm", ct), dst=hT)

        def dve_angles(dve, V, ch, step):
            dve.wait_ge(sem("late_loaded"), 32)
            ch(V.tensor_copy(ANG3[:, 0, :], POSB.bitcast(I32)))
            step(V.tensor_copy(ANG3[:, 1, :], POSB2.bitcast(I32)))
            for k in range(3):
                ch(V.tensor_scalar(ANG[:, k, :], ANG3[:, k // 2, :], invf[:, k:k + 1], None, ALU.mult))
            ch.settle()
            step(V.tensor_scalar(ANG2[:, :, :], ANG[:, :, :], 1.0 / (2 * np.pi), MAGIC, ALU.mult, ALU.add))
            step(V.tensor_scalar(ANG2[:, :, :], ANG2[:, :, :], MAGIC, None, ALU.subtract))
            for c in TWO_PI:
                step(V.scalar_tensor_tensor(ANG[:, :, :], ANG2[:, :, :], -c, ANG[:, :, :], ALU.mult, ALU.add))
            step(V.tensor_scalar(ANG[:, :, :], ANG[:, :, :], PI, -PI, ALU.min, ALU.max))
            step(V.tensor_scalar(ANG3[:, :, :], ANG[:, :, :], PI / 2, -2 * PI, ALU.is_gt, ALU.mult))
            step(V.scalar_tensor_tensor(ANG2[:, :, :], ANG[:, :, :], PI / 2, ANG3[:, :, :], ALU.add, ALU.add))
            V.tensor_scalar(ANG2[:, :, :], ANG2[:, :, :], PI, -PI, ALU.min, ALU.max).then_inc(sem("angles_ready"), 1)

        def view(ph, j):
            k, n = ph["shape"](j) if "shape" in ph else (ph["k"], ph["ncol"])
            return ring[:, (ph["c0"] + j) % RING, 0:k * n].rearrange("p (k n) -> p k n", k=k)

        loaded = [sem(f"weights_loaded_{s}") for s in range(RING)]
        used = {"pe": sem("acc_ready"), "dve": sem("ada_used")}
        acc_ready = used["pe"]

        def each_chunk(eng, name, body, first=0):
            ph = phases[name]
            g = ph["group"]
            if ph["loop"]:
                for j in range(g * first):
                    body(j, 0)
                with eng.Fori(first, ph["n"] // g) as i:
                    for j in range(g):
                        body(j, i)
                for j in range(ph["n"] - ph["n"] % g, ph["n"]):
                    body(j, 0)
            else:
                for j in range(ph["n"]):
                    body(j, 0)

        def wait_chunk(eng, name, j, i):
            ph = phases[name]
            c = ph["c0"] + j
            eng.wait_ge(loaded[c % RING], 16 * (c // RING + 1) + (16 * (ph["group"] // RING) * i if ph["loop"] else 0))
            return view(ph, j)

        acc_taken = {"act": sem("acc_taken_act"), "dve": sem("acc_taken_dve")}

        def took(name, n):
            ph = phases[name]
            return acc_taken[ph["taker"]], ph["taken0"] + n

        def pe_gemm(name, rhs, after, special=()):
            ph = phases[name]
            n = ph["tiles"]
            for s, v in after:
                nc.tensor.wait_ge(s, v)
            per = ph["group"] * ph["tiles"]

            def body(j, i):
                w = wait_chunk(nc.tensor, name, j, i)
                for m in range(n):
                    q = j * ph["tiles"] + m
                    if q == 0 and ph["loop"]:
                        nc.tensor.wait_ge(took(name, 0)[0], took(name, 0)[1] + per * i)
                    elif q >= 4:
                        nc.tensor.wait_ge(took(name, 0)[0], took(name, q - 3)[1] + per * i)
                    if q in special:
                        special[q](bank[q % 4], w).then_inc(acc_ready, 1)
                        continue
                    width = min(P, ph["ncol"] - m * P)
                    for k in range(ph["k"]):
                        mm = nc.tensor.matmul(bank[q % 4][0:width, 0:T], w[:, k, m * P:m * P + width], rhs(k),
                                              start=(k == 0), stop=(k == ph["k"] - 1))
                    mm.then_inc(acc_ready, 1)

            each_chunk(nc.tensor, name, body)

        def take_gemm(eng, name, op):
            ph = phases[name]
            n = ph["tiles"]
            per = ph["group"] * ph["tiles"]

            def body(j, i):
                for m in range(n):
                    q = j * ph["tiles"] + m
                    lin = per * i
                    eng.wait_ge(acc_ready, ph["t0"] + q + 1 + lin)
                    op(q, lin, bank[q % 4][:, 0:T]).then_inc(acc_taken[ph["taker"]], 1)

            each_chunk(eng, name, body)

        def pe_sum(dst, src, after, done):
            for s, v in after:
                nc.tensor.wait_ge(s, v)
            for k in range(KT):
                mm = nc.tensor.matmul(dst, ones[:, :], src[:, k, :], start=(k == 0), stop=(k == KT - 1))
            mm.then_inc(done, 1)

        def pe_head_sum(dst, src, after, done):
            for s, v in after:
                nc.tensor.wait_ge(s, v)
            for k in range(KT):
                mm = nc.tensor.matmul(dst, hs(k), src[:, k, :], start=(k == 0), stop=(k == KT - 1))
            mm.then_inc(done, 1)

        def pe_head_spread(src, after, done):
            for s, v in after:
                nc.tensor.wait_ge(s, v)
            for k in range(KT):
                mm = nc.tensor.matmul(bank[4 + k // 2][:, (k % 2) * T:(k % 2 + 1) * T], he(k), src,
                                      start=True, stop=True)
            mm.then_inc(done, 1)

        def spread(k2):
            return bank[4 + k2][:, :].rearrange("p (k t) -> p k t", k=2)

        block = ctx.enter_context(nc.Block())

        @block.sync
        def _(sp):
            for name, ph in phases.items():
                g, n = ph["group"], ph["n"]

                def fetch(j, i):
                    c = ph["c0"] + j
                    if c >= RING:
                        reader, v = chunks[c - RING]
                        sp.wait_ge(used[reader], v + ph["tiles"] * g * i)
                    sp.dma_start(view(ph, j), ph["src"](j, i)).then_inc(loaded[c % RING], 16)

                for j in range(n if not ph["loop"] else g):
                    fetch(j, 0)
                if ph["loop"]:
                    with sp.Fori(0, n // g - 1) as i:
                        for j in range(g, 2 * g):
                            c = ph["c0"] + j
                            sp.wait_ge(used["pe"], chunks[c - RING][1] + ph["tiles"] * g * i)
                            sp.dma_start(view(ph, j - g), ph["src"](j - g, i + 1)).then_inc(loaded[c % RING], 16)
                    for j in range(n - n % g, n):
                        fetch(j, 0)
            finish_sync(sp)

        @block.gpsimd
        def _(pool):
            ch = Chain(pool, sem("pool_step"))

            def step(ins):
                ch(ins)
                ch.settle()

            q = sem("pool_params_loaded")
            pool.dma_start(CROW[0:124, 0, :], a["conv_w"][0, 0:31, 0, :].rearrange("j (c p) -> (j c) p", p=P)[0:124, :]).then_inc(q, 16)
            pool.dma_start(CROW[0:124, 1, :], a["conv_w"][0, 0:31, 0, :].rearrange("j (c p) -> (j c) p", p=P)[124:248, :]).then_inc(q, 16)
            pool.dma_start(WU[0:64, :], a["rwkv_w_up"][0]).then_inc(q, 16)
            pool.dma_start(WU[64:128, :], a["rwkv_a_up"][0]).then_inc(q, 16)
            step(pool.memset(ident[:, :], 0.0))
            pool.affine_select(out=ident[:, :], in_=ident[:, :], compare_op=ALU.not_equal, fill=1.0, base=0,
                               pattern=[[-1, P]], channel_multiplier=1).then_inc(sem("ident_ready"), 1)
            pool.wait_ge(sem("ident_ready"), 1)
            step(pool.memset(ones[:, :], 1.0))
            for m in (swap_a, swap_i, swap_d, hsel, bmask):
                step(pool.memset(m[:, :] if m is not bmask else m[:, :, :], 0.0))
            step(pool.memset(hsel[0:64, 14:15], 1.0))
            step(pool.memset(hsel[64:128, 15:16], 1.0))
            for b in range(NC4):
                step(pool.memset(bmask[C * b:C * b + C, :, C * b:C * b + C], 1.0))
            step(pool.affine_select(out=bmask[:, 0, :], in_=bmask[:, 0, :], compare_op=ALU.is_gt, fill=0.0, base=0,
                                  pattern=[[1, P]], channel_multiplier=-1))
            step(pool.affine_select(out=bmask[:, 1, :], in_=bmask[:, 1, :], compare_op=ALU.is_ge, fill=0.0, base=0,
                                  pattern=[[1, P]], channel_multiplier=-1))
            step(pool.memset(segm[:, :], 1.0))
            step(pool.memset(segm[:, 0:T:C], 0.0))
            for m, half, blk in ((swap_a, 64, 128), (swap_i, 32, 64), (swap_d, 8, 64)):
                for h, base in ((0, -half), (1, 0)):
                    v = m[:, :].rearrange("p (b x) -> p b x", x=blk)[:, :, h * half:(h + 1) * half]
                    step(pool.affine_select(out=v, in_=v, compare_op=ALU.not_equal, fill=1.0, base=base,
                                          pattern=[[-blk, P // blk], [-1, half]], channel_multiplier=1))
            step(pool.memset(hspread[:, :, :], 1.0))
            step(pool.affine_select(out=hspread[:, :, :], in_=hspread[:, :, :], compare_op=ALU.is_ge, fill=0.0, base=0,
                                  pattern=[[P, KT], [1, P]], channel_multiplier=-64))
            step(pool.affine_select(out=hspread[:, :, :], in_=hspread[:, :, :], compare_op=ALU.is_ge, fill=0.0, base=63,
                                  pattern=[[-P, KT], [-1, P]], channel_multiplier=64))
            pool.memset(UP[:, :, 0:30], 0.0).then_inc(sem("const_ready"), 1)
            pool.wait_ge(sem("lt_ready"), 8)
            for n in range(NC4):
                pool.dma_start(ltd[n], LTC[C * n:C * n + C, :, :]).then_inc(sem("lt_stored"), 16)
            pool.wait_ge(sem("lt_stored"), 16 * NC4)
            for n in range(NC4):
                pool.dma_start(LTP[C * n:C * n + C, :, :], ltd[n].rearrange("s q t -> q s t")).then_inc(sem("lt_pairs"), 16)
            pool.wait_ge(sem("inverse_ready"), 1)
            pool.dma_start(ttd, TTP[:, :, :].rearrange("p a b -> p (a b)")).then_inc(sem("tt_stored"), 16)
            pool.wait_ge(sem("tt_stored"), 16)
            for tt in range(TT):
                if tt == 0:
                    pool.wait_ge(sem("tbd_cleared"), 1)
                else:
                    pool.wait_ge(sem("u_ready"), 4)
                for n in range(NC4):
                    src = ttd.rearrange("(n u q) (c t) -> n u c q t", n=NC4, u=TT, c=C)[n, tt]
                    pool.dma_start(TBD[C * n:C * n + C, :, C * n:C * n + C], src).then_inc(sem("tbd_ready"), 16)
            more_pool(pool, ch)

        NPAR = 20

        def chunk_ends(tt):
            return pend[:, :, NC4 * tt:NC4 * tt + NC4]

        @block.tensor
        def _(pe):
            mm = nc.tensor.matmul

            pe.wait_ge(sem("ident_ready"), 1)
            pe.wait_ge(sem("x_loaded"), 16)
            for ct in range(KT):
                for tt in range(TT):
                    ins = nc.tensor.transpose(bank[ct][:, tt * P:(tt + 1) * P], XTOK[:, tt, ct * P:(ct + 1) * P], ident[:, :])
                ins.then_inc(sem("x_turned"), 1)
            pe.wait_ge(sem("params_loaded"), 16 * NPAR)
            pe.wait_ge(sem("pool_params_loaded"), 64)
            pe.wait_ge(sem("x_taken"), 1)
            nc.tensor.transpose(bank[0][:, 0:P], PROW[:, 0, :], ident[:, :])
            nc.tensor.transpose(bank[0][:, P:2 * P], PROW[:, 1, :], ident[:, :])
            nc.tensor.transpose(bank[0][:, 256:380], CROW[0:124, 0, :], ident[0:124, 0:124])
            nc.tensor.transpose(bank[0][:, 380:504], CROW[0:124, 1, :], ident[0:124, 0:124]).then_inc(sem("params_turned"), 1)
            pe.wait_ge(sem("const_ready"), 1)

            def ada(layer):
                ph = phases[f"ada{layer}"]
                for m in range(6):
                    pe.wait_ge(sem("ada_used"), ph["t0"] + m + 1)
                    for j in range(4):
                        ins = mm(bank[5][:, 4 * m + j:4 * m + j + 1], ADA[:, m % 2, j * P:(j + 1) * P], ones[:, 0:1],
                                 start=True, stop=True)
                    ins.then_inc(sem("ada_summed"), 1)

            def norm(i, after):
                pe_sum(bank[4][:, 0:T], NSQ[i], [(sem("norm_squares"), 2 * (i + 1))] + after, sem("norm_summed"))

            norm(0, [])
            ada(0)
            pe_gemm("zA", lambda k: hT[:, k, :], [(sem("h_ready"), 1), (sem("params_taken"), 2)])
            pe_gemm("zB", lambda k: hT[:, k, :], [took("zA", 16)])
            ada(1)
            pe_gemm("zL", lambda k: hT[:, k, :], [took("zB", 32)])
            for part, (lo, done) in enumerate(((0, "wup_ready"), (64, "aup_ready"))):
                pe.wait_ge(sem("lora_ready"), 1)
                for ct in range(KT):
                    if part == 1 and ct % 2 == 0:
                        pe.wait_ge(sem("wup_taken"), ct + 2)
                    ins = mm(bank[4 + ct // 2][:, (ct % 2) * T:(ct % 2 + 1) * T], WU[lo:lo + 64, ct * P:(ct + 1) * P],
                             LO[lo:lo + 64, 0:T], start=True, stop=True)
                    if ct % 2 == 1:
                        ins.then_inc(sem(done), 1)
            pe_gemm("zG", lambda k: hT[:, k, :], [took("zL", 1)])
            pe_sum(bank[4][:, 0:T], YY, [(taps, 248), (sem("aup_taken"), 8)], sem("mean_summed"))
            pe_sum(bank[5][:, 0:T], VAL, [(sem("squares_ready"), 1)], sem("var_summed"))
            pe_head_sum(bank[6][0:16, 0:T], VAL, [(sem("squares_ready"), 2)], sem("key_sum"))
            pe_head_spread(nr[0:16, :], [(sem("key_norm"), 1)], sem("key_spread"))
            pe_head_sum(bank[0][0:16, 0:T], X1, [(sem("rk_ready"), 1), took("zG", 8)], sem("bonus_sum"))

            pe.wait_ge(sem("rwkv_ready"), 1)
            for g in range(8):
                tt = g // 4
                if g >= 4:
                    pe.wait_ge(sem("lt_ready"), g - 3)
                else:
                    pe.wait_ge(sem("key_applied"), 4)
                for j in range(4):
                    h = 8 * (g % 4 // 2) + 2 * j + g % 2
                    r = slice(64 * (h % 2), 64 * (h % 2) + 64)
                    t = slice(tt * P, tt * P + P)
                    ins = mm(bank[4 + g % 4][:, j * P:(j + 1) * P], X4[r, h // 2, t], AR[r, h // 2, 0, t], start=True, stop=True)
                ins.then_inc(sem("lt_banks"), 1)

            for tt in range(TT):
                t = slice(tt * P, tt * P + P)
                for m, (src, _) in enumerate(TOKS):
                    for half in range(2):
                        b = (2 * m + half) % 4
                        n = 8 * tt + 2 * m + half
                        if n >= 4:
                            pe.wait_ge(sem("toks_taken"), n - 3)
                        else:
                            pe.wait_ge(sem("bonus_taken"), 1)
                        if tt == 1 and m == 0 and half == 0:
                            pe.wait_ge(sem("y_ready"), 2)
                        for j in range(4):
                            ins = nc.tensor.transpose(bank[b][:, j * P:(j + 1) * P], src(4 * half + j, t), ident[:, :])
                        ins.then_inc(sem("toks_ready"), 1)
                for g in range(8):
                    n = 8 * tt + g
                    if n >= 4:
                        pe.wait_ge(sem("kar_taken"), n - 3)
                    else:
                        pe.wait_ge(sem("lt_ready"), 8)
                    if tt == 1 and g == 0:
                        pe.wait_ge(sem("state_ready"), NC4 + 1)
                        pe.wait_ge(sem("ycarry_taken"), 4)
                    for j in range(2):
                        h = 4 * (g // 2) + 2 * j + g % 2
                        r = slice(64 * (h % 2), 64 * (h % 2) + 64)
                        ins = mm(bank[4 + g % 4][:, j * 256:(j + 1) * 256].rearrange("p (a t) -> p a t", a=2),
                                 KK[r, h // 2, t], AR[r, h // 2, :, t], start=True, stop=True)
                    ins.then_inc(sem("kar_ready"), 1)
                pe.wait_ge(sem("toks_taken"), 8 * tt + 8)
                for g in range(4):
                    for j in range(4):
                        h = 8 * (g // 2) + 2 * j + g % 2
                        r = slice(64 * (h % 2), 64 * (h % 2) + 64)
                        ins = mm(bank[g][:, j * P:(j + 1) * P], X4[r, h // 2, t], AR[r, h // 2, 1, t], start=True, stop=True)
                    ins.then_inc(sem("br_ready"), 1)
                for g in range(4):
                    pe.wait_ge(sem("kar_taken"), 8 * tt + 8)
                    for j in range(4):
                        h = 4 * g + j
                        ins = mm(bank[4 + g][:, j * P:(j + 1) * P], A2T[:, h, :], VTOK[:, (h // 2) * P:(h // 2 + 1) * P],
                                 start=True, stop=True)
                    ins.then_inc(sem("w_ready"), 1)
                pe.wait_ge(sem("tbd_ready"), 64 * (tt + 1))
                pe.wait_ge(sem("br_taken"), 4 * (tt + 1))
                for g in range(2):
                    for j in range(8):
                        h = 8 * g + j
                        ins = mm(bank[g][64 * (h % 2):64 * (h % 2) + 64, (j // 2) * P:(j // 2 + 1) * P],
                                 ATOK[:, h * HD:(h + 1) * HD], TBD[:, h, :], start=True, stop=True)
                    ins.then_inc(sem("apt_ready"), 1)
                for g in range(4):
                    if g == 0:
                        pe.wait_ge(sem("w_taken"), 8 * (tt + 1))
                    for j in range(4):
                        h = 4 * g + j
                        ins = mm(bank[2 + g][:, j * P:(j + 1) * P], TBD[:, h, :], WW[:, (h // 2) * P:(h // 2 + 1) * P],
                                 start=True, stop=True)
                    ins.then_inc(sem("u_ready"), 1)
                for n in range(NC4):
                    i = NC4 * tt + n
                    rows = slice(C * n, C * n + C)
                    tc = slice(tt * P + C * n, tt * P + C * n + C)
                    if n == 0:
                        pe.wait_ge(sem("apt_taken"), 2 * (tt + 1))
                        pe.wait_ge(sem("u_taken"), 8 * (tt + 1))
                    pe.wait_ge(sem("state_ready"), i + 1)
                    for h in range(NH):
                        r = slice(64 * (h % 2), 64 * (h % 2) + 64)
                        ins = mm(bank[4 + h % 2][rows, (h // 2) * HD:(h // 2 + 1) * HD],
                                 APT[r, h // 2, rows], SS[r, h // 2, :], start=True, stop=True)
                    ins.then_inc(sem("as_ready"), 1)
                    for h in range(NH):
                        r = slice(64 * (h % 2), 64 * (h % 2) + 64)
                        mm(bank[7][r, (h // 2) * HD:(h // 2 + 1) * HD], KTOK[rows, h * HD:(h + 1) * HD],
                           VTOK[rows, h * HD:(h + 1) * HD], start=(h < 2), stop=False, skip_group_check=True)
                    if i >= 1:
                        pe.wait_ge(sem("ycarry_taken"), i)
                    for h in range(NH):
                        r = slice(64 * (h % 2), 64 * (h % 2) + 64)
                        ins = mm(bank[6][r, (h // 2) * C:(h // 2 + 1) * C], SS[r, h // 2, :], AR[r, h // 2, 1, tc],
                                 start=True, stop=True)
                    ins.then_inc(sem("ycarry_ready"), 1)
                    pe.wait_ge(sem("sa_ready"), 2 * i + 2)
                    for h in range(NH):
                        r = slice(64 * (h % 2), 64 * (h % 2) + 64)
                        ins = mm(bank[7][r, (h // 2) * HD:(h // 2 + 1) * HD], BTOK[rows, h * HD:(h + 1) * HD],
                                 UU[rows, h * HD:(h + 1) * HD], start=False, stop=True, skip_group_check=True)
                    ins.then_inc(sem("update_ready"), 1)
                for g in range(2):
                    for j in range(8):
                        h = 8 * g + j
                        o = bank[g][64 * (h % 2):64 * (h % 2) + 64, (j // 2) * P:(j // 2 + 1) * P]
                        mm(o, UU[:, h * HD:(h + 1) * HD], A3T[:, h, :], start=True, stop=False)
                        ins = mm(o, VTOK[:, h * HD:(h + 1) * HD], A4T[:, h, :], start=False, stop=True)
                    ins.then_inc(sem("yin_ready"), 1)

            pe_head_sum(bank[4][0:16, 0:T], YT, [(sem("y_ready"), 4)], sem("mean_summed"))
            pe_head_spread(nr[0:16, :], [(sem("gn_mean_ready"), 1)], sem("gn_mean_spread"))
            pe_head_sum(bank[0][0:16, 0:T], X1, [(sem("squares_ready"), 3)], sem("var_summed"))
            pe_head_spread(nr[0:16, :], [(sem("gn_rstd"), 1), (sem("centred"), 5)], sem("gn_rstd_spread"))
            pe_head_spread(stb[:, :], [(sem("gn_scaled"), 4)], sem("bonus_spread"))
            pe_gemm("eo", lambda k: YY[:, k, :] if k < 8 else YT[:, k - 8, :], [(sem("yb_ready"), 1)])
            pe_rest(pe)

        @block.scalar
        def _(act):
            ch = Chain(act, sem("act_step"))
            A = nc.scalar.activation
            act.dma_start(XTOK[:, :, :], a["x"][0].rearrange("(u p) n -> p u n", p=P)).then_inc(sem("x_loaded"), 16)
            q = sem("params_loaded")
            sent = [0]

            def par(dst, src):
                act.dma_start(dst, src).then_inc(q, 16)
                sent[0] += 1

            def rows(name, src):
                v = VEC[name]
                n = 1
                for s in src.shape:
                    n *= s
                n //= P
                flat = src
                if len(src.shape) == 2:
                    flat = src.rearrange("a b -> (a b)")
                elif len(src.shape) == 3:
                    flat = src.rearrange("a b c -> (a b c)")
                par(PROW[v % P:v % P + n, v // P, :], flat.rearrange("(r p) -> r p", p=P))

            rows("c", a["c"])
            rows("norm_g0", a["norm_g"])
            rows("final_g", a["final_g"])
            rows("ab00", a["ada_b"])
            rows("cv0", a["conv_vec"])
            rows("mu_r", a["rwkv_mu_rkv"])
            rows("w0", a["rwkv_vec"])
            rows("r_k", a["rwkv_r_k"])
            rows("mix0", a["ln_mix_2"])
            rows("ffn0", a["ln_ffn_2"])
            rows("ple0", a["ln_ple_2"])
            rows("fnorm", a["final_norm_2"])
            rows("cln_g", a["c_ln_g_2"])
            rows("cln_b", a["c_ln_b_2"])
            par(acw[:, :, :], a["a_conv_w_2"][0].rearrange("(c p) j -> p c j", p=P))
            par(mulora, a["rwkv_mu_lora"][0].rearrange("a b -> (a b)").unsqueeze(1))
            par(subln, a["a_subln_2"][0].unsqueeze(1))
            par(invf, a["inv_freq"])
            par(POSI[:, 0:1], a["positions"][0, 0:P].unsqueeze(1))
            par(POSI[:, 1:2], a["positions"][0, P:T].unsqueeze(1))
            assert sent[0] == NPAR, sent

            for ct in range(4, 8):
                act.wait_ge(sem("x_turned"), ct + 1)
                A(xT[:, ct, :], bank[ct][:, 0:T], ACT.Copy).then_inc(sem("x_taken_act"), 1)
            act.wait_ge(sem("params_turned"), 1)
            A(pc[:, :], bank[0][:, 0:256], ACT.Copy).then_inc(sem("params_taken"), 1)
            A(cw[:, 0:248], bank[0][:, 256:504], ACT.Copy).then_inc(sem("params_taken"), 1)
            act.wait_ge(sem("params_taken"), 2)
            A(cond[:, :], cols8("c"), ACT.Silu).then_inc(sem("cond_ready"), 1)

            def norm(i, after):
                for s, v in after:
                    act.wait_ge(s, v)
                for half in range(2):
                    k = slice(4 * half, 4 * half + 4)
                    A(NSQ[i][:, k, :], xT[:, k, :], ACT.Square).then_inc(sem("norm_squares"), 1)
                act.wait_ge(sem("norm_summed"), i + 1)
                A(nr[:, :], bank[4][:, 0:T], ACT.Sqrt, bias=1e-6, scale=1.0 / D).then_inc(sem("norm_rooted"), 1)

            norm(0, [(sem("x_taken"), 4), (sem("x_taken_act"), 4)])

            def take_a(q, lin, b):
                return A(UP[:, q, 30:30 + T], b, ACT.Copy) if q < 8 else A(GLU[:, q - 8, :], b, ACT.Sigmoid)

            take_gemm(act, "zA", take_a)
            take_gemm(act, "zB", lambda q, lin, b: A(ZE[:, bass.ds(q * T + lin * T, T)], b, ACT.Copy))
            take_gemm(act, "zL", lambda q, lin, b: A(LO[:, 0:T], b, ACT.Copy))
            act.wait_ge(sem("lora_lerped"), 1)
            A(LO[0:64, 0:T], LO[0:64, 0:T], ACT.Tanh).then_inc(sem("lora_ready"), 1)
            for ct in range(KT):
                act.wait_ge(sem("wup_ready"), ct // 2 + 1)
                A(X1[:, ct, :], bank[4 + ct // 2][:, (ct % 2) * T:(ct % 2 + 1) * T], ACT.Sigmoid,
                  bias=col("w0", ct)).then_inc(sem("wup_taken"), 1)
            for ct in range(KT):
                act.wait_ge(sem("aup_ready"), ct // 2 + 1)
                A(X2[:, ct, :], bank[4 + ct // 2][:, (ct % 2) * T:(ct % 2 + 1) * T], ACT.Sigmoid,
                  bias=col("a0", ct)).then_inc(sem("aup_taken"), 1)
            take_gemm(act, "zG", lambda q, lin, b: A(BG[:, q, :], b, ACT.Silu))
            act.wait_ge(sem("centred"), 1)
            A(VAL[:, :, :], YY[:, :, :], ACT.Square).then_inc(sem("squares_ready"), 1)
            A(AG[:, :, :], AG[:, :, :], ACT.Silu).then_inc(sem("agate_ready"), 1)
            act.wait_ge(sem("var_summed"), 1)
            A(nr[:, :], bank[5][:, 0:T], ACT.Sqrt, bias=1e-5, scale=1.0 / D).then_inc(sem("rooted"), 1)
            act.wait_ge(sem("conv_scaled"), 1)
            for ct in range(KT):
                ins = A(YY[:, ct, :], YY[:, ct, :], ACT.Silu, bias=col("cv2", ct), scale=col("cv1", ct))
            ins.then_inc(sem("conv_silu"), 1)
            act.wait_ge(sem("keys_scaled"), 1)
            A(VAL[:, :, :], X4[:, :, :], ACT.Square).then_inc(sem("squares_ready"), 1)
            act.wait_ge(sem("key_sum"), 1)
            A(nr[0:16, :], bank[6][0:16, 0:T], ACT.Sqrt).then_inc(sem("rooted"), 1)
            act.wait_ge(sem("decay_sums"), 1)
            A(AR[:, :, 1, :], X3[:, :, :], ACT.Exp, scale=-DECAY).then_inc(sem("decays"), 1)
            act.wait_ge(sem("decay_before"), 1)
            A(AR[:, :, 0, :], X1[:, :, :], ACT.Exp, scale=-DECAY).then_inc(sem("decays"), 1)
            A(X3[:, :, :], X3[:, :, :], ACT.Exp, scale=DECAY).then_inc(sem("decays"), 1)
            act.wait_ge(sem("bonus_sum"), 1)
            A(stb[:, :], bank[0][0:16, 0:T], ACT.Copy).then_inc(sem("bonus_taken"), 1)

            for tt in range(TT):
                for m, (_, dst) in enumerate(TOKS):
                    for half in range(2):
                        n = 8 * tt + 2 * m + half
                        act.wait_ge(sem("toks_ready"), n + 1)
                        if tt == 1 and m == 0 and half == 0:
                            act.wait_ge(sem("yin_ready"), 2)
                        A(dst[:, 512 * half:512 * half + 512], bank[(2 * m + half) % 4][:, :], ACT.Copy)\
                            .then_inc(sem("toks_taken"), 1)
                for g in range(4):
                    act.wait_ge(sem("w_ready"), 4 * tt + g + 1)
                    for h in range(2):
                        src = bank[4 + g][:, :].rearrange("p (c h v) -> p c h v", c=2, h=2)[:, :, h, h * HD:(h + 1) * HD]
                        dst = WW[:, 256 * g:256 * g + 256].rearrange("p (c h v) -> p c h v", c=2, h=2)[:, :, h, :]
                        A(dst, src, ACT.Copy).then_inc(sem("w_taken"), 1)
                for g in range(2):
                    act.wait_ge(sem("apt_ready"), 2 * tt + g + 1)
                    A(APT[:, 4 * g:4 * g + 4, :], bank[g][:, :].rearrange("p (c t) -> p c t", c=4), ACT.Copy)\
                        .then_inc(sem("apt_taken"), 1)
                for n in range(NC4):
                    i = NC4 * tt + n
                    act.wait_ge(sem("ycarry_ready"), i + 1)
                    A(YT[:, :, tt * P + C * n:tt * P + C * n + C], bank[6][:, 0:T].rearrange("p (c t) -> p c t", c=KT), ACT.Copy)\
                        .then_inc(sem("ycarry_taken"), 1)

            act.wait_ge(sem("mean_summed"), 2)
            A(nr[0:16, :], bank[4][0:16, 0:T], ACT.Copy, scale=1.0 / HD).then_inc(sem("gn_mean_ready"), 1)
            act.wait_ge(sem("centred"), 5)
            A(X1[:, :, :], YT[:, :, :], ACT.Square).then_inc(sem("squares_ready"), 1)
            act.wait_ge(sem("var_summed"), 2)
            A(nr[0:16, :], bank[0][0:16, 0:T], ACT.Sqrt, bias=64e-5, scale=1.0 / HD).then_inc(sem("rooted"), 1)
            act_rest(act, ch, A, norm)

        @block.vector
        def _(dve):
            V = nc.vector
            ch = Chain(dve, sem("dve_step"))

            def step(ins):
                ch(ins)
                ch.settle()

            for ct in range(4):
                dve.wait_ge(sem("x_turned"), ct + 1)
                V.tensor_copy(xT[:, ct, :], bank[ct][:, 0:T]).then_inc(sem("x_taken"), 1)
            dve.wait_ge(sem("x_taken_act"), 4)

            def ada(layer):
                ph = phases[f"ada{layer}"]
                for m in range(6):
                    w = wait_chunk(dve, f"ada{layer}", m, 0)
                    if 6 * layer + m >= 2:
                        dve.wait_ge(sem("ada_summed"), 6 * layer + m - 1)
                    acc = ADA[:, m % 2, :]
                    step(V.tensor_scalar(acc, w[:, 0, :], cond[:, 0:1], None, ALU.mult))
                    for k in range(1, KT):
                        ins = V.scalar_tensor_tensor(acc, w[:, k, :], cond[:, k:k + 1], acc, ALU.mult, ALU.add)
                        if k < KT - 1:
                            step(ins)
                    ins.then_inc(sem("ada_used"), 1)
                dve.wait_ge(sem("ada_summed"), 6 * (layer + 1))
                b = VEC[f"ab{layer}0"]
                step(V.tensor_tensor(mod[:, layer, :], bank[5][:, 0:24], pc[:, b:b + 24], ALU.add))
                step(V.tensor_scalar(gs[:, 8 * layer:8 * layer + 8], mod[:, layer, 8:16], 1.0, None, ALU.add))
                V.tensor_tensor(gs[:, 8 * layer:8 * layer + 8], gs[:, 8 * layer:8 * layer + 8],
                                cols8(f"norm_g{layer}"), ALU.mult).then_inc(sem("mod_ready"), 1)
                dve.wait_ge(sem("mod_ready"), layer + 1)

            def norm(i, gain, shift=None, dst=None):
                dst = hT if dst is None else dst
                dve.wait_ge(sem("norm_rooted"), i + 1)
                step(V.reciprocal(nr[:, :], nr[:, :]))
                for ct in range(KT):
                    ins = V.scalar_tensor_tensor(dst[:, ct, :], xT[:, ct, :], gain(ct), nr[:, :], ALU.mult, ALU.mult)
                    if shift is not None or ct < KT - 1:
                        ch(ins)
                if shift is not None:
                    ch.settle()
                    for ct in range(KT):
                        ins = V.tensor_scalar(dst[:, ct, :], dst[:, ct, :], shift(ct), None, ALU.add)
                        if ct < KT - 1:
                            ch(ins)
                ins.then_inc(sem("h_ready"), 1)

            dve.wait_ge(sem("cond_ready"), 1)
            ada(0)
            norm(0, lambda ct: gs[:, ct:ct + 1], lambda ct: mod[:, 0, ct:ct + 1])

            dve.wait_ge(*took("zA", 16))
            dve.wait_ge(sem("const_ready"), 1)
            step(V.tensor_tensor(UP[:, :, 30:30 + T], UP[:, :, 30:30 + T], GLU[:, :, :], ALU.mult))
            for ct in range(KT):
                V.tensor_scalar(YY[:, ct, :], UP[:, ct, 0:T], cw[:, ct:ct + 1], col("cv0", ct), ALU.mult, ALU.add)\
                    .then_inc(taps, 1)
            with dve.Fori(1, 31) as j:
                for ct in range(KT):
                    dve.wait_ge(taps, 8 * j - 8 + ct + 1)
                    V.scalar_tensor_tensor(YY[:, ct, :], UP[:, ct, bass.ds(j, T)], cw[:, bass.ds(8 * j + ct, 1)],
                                           YY[:, ct, :], ALU.mult, ALU.add).then_inc(taps, 1)
            dve.wait_ge(taps, 248)
            ada(1)

            def lerp(z, d, mu, done):
                ch(V.tensor_tensor(d[:, :, 1:T], z[:, :, 0:T - 1], z[:, :, 1:T], ALU.subtract))
                step(V.tensor_scalar(d[:, :, 0:1], z[:, :, 0:1], -1.0, None, ALU.mult))
                for ct in range(z.shape[1]):
                    ins = V.scalar_tensor_tensor(z[:, ct, :], d[:, ct, :], mu(ct), z[:, ct, :], ALU.mult, ALU.add)
                    if ct < z.shape[1] - 1:
                        ch(ins)
                ins.then_inc(done, 1)

            dve.wait_ge(*took("zL", 1))
            lo = LO[:, :].rearrange("p (a t) -> p a t", a=2)
            lerp(lo[:, 0:1, :], lo[:, 1:2, :], lambda ct: mulora, sem("lora_lerped"))
            dve.wait_ge(*took("zB", 32))
            for n, (z, name) in enumerate(((KK, "mu_k"), (RR, "mu_r"), (VV, "mu_v"))):
                lerp(z, VAL, lambda ct, name=name: col(name, ct), sem("rkv_lerped"))
                dve.wait_ge(sem("rkv_lerped"), n + 1)
            dve.wait_ge(sem("mean_summed"), 1)
            mean = bank[4][:, 0:T].unsqueeze(1).to_broadcast([P, KT, T])
            V.scalar_tensor_tensor(YY[:, :, :], mean, -1.0 / D, YY[:, :, :], ALU.mult, ALU.add).then_inc(sem("centred"), 1)
            for ct in range(KT):
                ins = V.tensor_scalar(X4[:, ct, :], KK[:, ct, :], col("k_k", ct), None, ALU.mult)
                if ct < KT - 1:
                    ch(ins)
            ins.then_inc(sem("keys_scaled"), 1)
            dve.wait_ge(sem("keys_scaled"), 1)
            dve.wait_ge(sem("rooted"), 1)
            step(V.reciprocal(nr[:, :], nr[:, :]))
            nrb = nr[:, :].unsqueeze(1).to_broadcast([P, KT, T])
            V.tensor_tensor(YY[:, :, :], YY[:, :, :], nrb, ALU.mult).then_inc(sem("conv_scaled"), 1)
            dve.wait_ge(sem("wup_taken"), 8)
            for ct in range(KT):
                ins = V.tensor_tensor_scan(X3[:, ct, :], segm[:, :], X1[:, ct, :], 0.0, ALU.mult, ALU.add)
                if ct < KT - 1:
                    ch(ins)
            ins.then_inc(sem("decay_sums"), 1)
            dve.wait_ge(sem("decay_sums"), 1)
            V.tensor_tensor(X1[:, :, :], X3[:, :, :], X1[:, :, :], ALU.subtract).then_inc(sem("decay_before"), 1)
            dve.wait_ge(sem("rooted"), 2)
            step(V.tensor_scalar(nr[0:16, :], nr[0:16, :], 1e-12, None, ALU.max))
            V.reciprocal(nr[0:16, :], nr[0:16, :]).then_inc(sem("key_norm"), 1)
            dve.wait_ge(sem("conv_silu"), 1)
            dve.wait_ge(sem("agate_ready"), 1)
            V.tensor_tensor(YY[:, :, :], YY[:, :, :], AG[:, :, :], ALU.mult).then_inc(sem("conv_normed"), 1)
            dve.wait_ge(sem("key_spread"), 1)
            for g in range(4):
                V.tensor_tensor(X4[:, 2 * g:2 * g + 2, :], X4[:, 2 * g:2 * g + 2, :], spread(g), ALU.mult)\
                    .then_inc(sem("key_applied"), 1)
            dve.wait_ge(sem("key_applied"), 4)
            dve.wait_ge(sem("aup_taken"), 8)
            dve.wait_ge(sem("decays"), 3)
            step(V.scalar_tensor_tensor(AR[:, :, 0, :], X4[:, :, :], -1.0, AR[:, :, 0, :], ALU.mult, ALU.mult))
            step(V.tensor_tensor(X4[:, :, :], X4[:, :, :], X2[:, :, :], ALU.mult))
            step(V.tensor_tensor(X4[:, :, :], X4[:, :, :], X3[:, :, :], ALU.mult))
            for ct in range(KT):
                ch(V.tensor_scalar(X2[:, ct, :], X2[:, ct, :], col("k_a", ct), col("k_a", ct), ALU.mult, ALU.subtract))
            ch.settle()
            step(V.scalar_tensor_tensor(KK[:, :, :], X2[:, :, :], 1.0, KK[:, :, :], ALU.add, ALU.mult))
            step(V.tensor_tensor(X1[:, :, :], RR[:, :, :], KK[:, :, :], ALU.mult))
            for ct in range(KT):
                ins = V.tensor_scalar(X1[:, ct, :], X1[:, ct, :], col("r_k", ct), None, ALU.mult)
                if ct < KT - 1:
                    ch(ins)
            ins.then_inc(sem("rk_ready"), 1)
            step(V.tensor_copy(pend[:, :, :], AR[:, :, 1, C - 1:T:C]))
            ch(V.tensor_tensor(AR[:, :, 1, :], AR[:, :, 1, :], RR[:, :, :], ALU.mult))
            ch(V.memset(SS[:, :, :], 0.0))
            ch(V.memset(TTP[:, :, :], 0.0))
            ch.settle()
            V.tensor_tensor(KK[:, :, :], KK[:, :, :], X3[:, :, :], ALU.mult).then_inc(sem("rwkv_ready"), 1)
            V.memset(TTP[:, :, :].rearrange("p a b -> p (a b)")[:, 0:C * C:C + 1], 1.0).then_inc(sem("state_ready"), 1)

            dve.wait_ge(sem("bonus_sum"), 1)
            for g in range(8):
                dve.wait_ge(sem("lt_banks"), g + 1)
                b = bank[4 + g % 4][:, :].rearrange("p (q t) -> p q t", q=4)
                for n in range(NC4):
                    r = slice(C * n, C * n + C)
                    m = bmask[r, 0, r].unsqueeze(1).to_broadcast([C, 4, C])
                    q = 16 * (g // 4) + 8 * (g % 4 // 2) + g % 2
                    ins = V.tensor_tensor(LTC[r, q:q + 7:2, :], b[r, :, r], m, ALU.mult)
                ins.then_inc(sem("lt_ready"), 1)
            dve.wait_ge(sem("lt_pairs"), 16 * NC4)
            dve.wait_ge(sem("state_ready"), 1)
            for t in range(1, C):
                prod = TMP[:, 0:t * t].rearrange("p (c s) -> p c s", c=t)
                l = LTP[:, 0:t, t].unsqueeze(1).to_broadcast([P, t, t])
                step(V.tensor_tensor(prod, TTP[:, 0:t, 0:t], l, ALU.mult))
                ins = V.tensor_reduce(TTP[:, 0:t, t:t + 1], prod, AX_X, ALU.add)
                if t < C - 1:
                    step(ins)
            ins.then_inc(sem("inverse_ready"), 1)
            dve.wait_ge(sem("inverse_ready"), 1)
            V.memset(TBD[:, :, :], 0.0).then_inc(sem("tbd_cleared"), 1)

            m0 = bmask[:, 0, :].unsqueeze(1)
            m1 = bmask[:, 1, :].unsqueeze(1)
            for tt in range(TT):
                for g in range(8):
                    dve.wait_ge(sem("kar_ready"), 8 * tt + g + 1)
                    if tt == 1 and g == 0:
                        dve.wait_ge(sem("yin_ready"), 2)
                    b = bank[4 + g % 4][:, :].rearrange("p (h a t) -> p h a t", h=2, a=2)
                    q = slice(4 * (g // 2) + g % 2, 4 * (g // 2) + g % 2 + 3, 2)
                    ch(V.tensor_tensor(A2T[:, q, :], b[:, :, 0, :], m0.to_broadcast([P, 2, P]), ALU.mult))
                    V.tensor_tensor(A4T[:, q, :], b[:, :, 1, :], m1.to_broadcast([P, 2, P]), ALU.mult)\
                        .then_inc(sem("kar_taken"), 1)
                for g in range(4):
                    dve.wait_ge(sem("br_ready"), 4 * tt + g + 1)
                    b = bank[g][:, :].rearrange("p (h t) -> p h t", h=4)
                    q = slice(8 * (g // 2) + g % 2, 8 * (g // 2) + g % 2 + 7, 2)
                    V.tensor_tensor(A3T[:, q, :], b, m1.to_broadcast([P, 4, P]), ALU.mult)\
                        .then_inc(sem("br_taken"), 1)
                for g in range(4):
                    dve.wait_ge(sem("u_ready"), 4 * tt + g + 1)
                    for h in range(2):
                        src = bank[2 + g][:, :].rearrange("p (c h v) -> p c h v", c=2, h=2)[:, :, h, h * HD:(h + 1) * HD]
                        dst = UU[:, 256 * g:256 * g + 256].rearrange("p (c h v) -> p c h v", c=2, h=2)[:, :, h, :]
                        V.tensor_copy(dst, src).then_inc(sem("u_taken"), 1)
                dve.wait_ge(sem("u_taken"), 8 * (tt + 1))
                for n in range(NC4):
                    i = NC4 * tt + n
                    rows = slice(C * n, C * n + C)
                    dve.wait_ge(sem("as_ready"), i + 1)
                    for half in range(2):
                        u = UU[rows, :].rearrange("p (c h v) -> p c h v", c=KT, h=2)[:, :, half, :]
                        V.tensor_tensor(u, bank[4 + half][rows, :].rearrange("p (c v) -> p c v", c=KT), u, ALU.add).then_inc(sem("sa_ready"), 1)
                    dve.wait_ge(sem("update_ready"), i + 1)
                    step(V.tensor_tensor(SS[:, :, :], bank[7][:, :].rearrange("p (c v) -> p c v", c=KT), SS[:, :, :], ALU.add))
                    pe_ = pend[:, :, i:i + 1].to_broadcast([P, KT, HD])
                    V.tensor_tensor(SS[:, :, :], SS[:, :, :], pe_, ALU.mult).then_inc(sem("state_ready"), 1)
                    dve.wait_ge(sem("state_ready"), i + 2)
                dve.wait_ge(sem("ycarry_taken"), 4 * (tt + 1))
                for g in range(2):
                    dve.wait_ge(sem("yin_ready"), 2 * tt + g + 1)
                    o = YT[:, 4 * g:4 * g + 4, tt * P:(tt + 1) * P]
                    V.tensor_tensor(o, bank[g][:, :].rearrange("p (c t) -> p c t", c=4), o, ALU.add).then_inc(sem("y_ready"), 1)

            dve.wait_ge(sem("y_ready"), 4)
            dve.wait_ge(sem("gn_mean_spread"), 1)
            for g in range(4):
                o = YT[:, 2 * g:2 * g + 2, :]
                V.scalar_tensor_tensor(o, spread(g), -1.0, o, ALU.mult, ALU.add).then_inc(sem("centred"), 1)
            dve.wait_ge(sem("rooted"), 3)
            V.reciprocal(nr[0:16, :], nr[0:16, :]).then_inc(sem("gn_rstd"), 1)
            dve.wait_ge(sem("gn_rstd_spread"), 1)
            for g in range(4):
                o = YT[:, 2 * g:2 * g + 2, :]
                V.tensor_tensor(o, o, spread(g), ALU.mult).then_inc(sem("gn_scaled"), 1)
            dve.wait_ge(sem("gn_scaled"), 4)
            for ct in range(KT):
                ch(V.tensor_scalar(YT[:, ct, :], YT[:, ct, :], col("lnx_w", ct), col("lnx_b", ct), ALU.mult, ALU.add))
            dve.wait_ge(sem("bonus_spread"), 1)
            for g in range(4):
                ch(V.tensor_tensor(X2[:, 2 * g:2 * g + 2, :], VV[:, 2 * g:2 * g + 2, :], spread(g), ALU.mult))
            ch.settle()
            step(V.tensor_tensor(YT[:, :, :], YT[:, :, :], X2[:, :, :], ALU.add))
            V.tensor_tensor(YT[:, :, :], YT[:, :, :], BG[:, :, :], ALU.mult).then_inc(sem("yb_ready"), 1)
            dve_angles(dve, V, ch, step)
            take_gemm(dve, "eo", lambda q, lin, b: V.scalar_tensor_tensor(
                xT[:, q, :], b, mod[:, 0, 16 + q:17 + q], xT[:, q, :], ALU.mult, ALU.add))
            dve_rest(dve, V, ch, step, norm)


def kernel(**inputs):
    import numpy as _np
    import concourse.bacc as _bacc
    from concourse import mybir as _mybir
    from concourse.bass_utils import run_bass_kernel_spmd as _run

    nc = _bacc.Bacc("TRN2", target_bir_lowering=False, num_devices=1)
    arrays, args = {}, {}
    for name, value in inputs.items():
        v = _np.ascontiguousarray(value)
        arrays[f"in_{name}_dram"] = v
        args[name] = nc.dram_tensor(f"in_{name}_dram", v.shape, _mybir.dt.from_np(v.dtype), kind="ExternalInput").ap()
    inv = _np.zeros((128, 6), _np.float32)
    p = _np.arange(128)
    inv[:, 0] = (10000.0 ** (-(2 * (p % 64)) / 128)).astype(_np.float32)
    inv[:, 1] = (10000.0 ** (-(2 * (p % 32)) / 64)).astype(_np.float32)
    inv[:, 2] = _np.where(p % 64 < 16, 500000.0 ** (-(2 * (p % 8)) / 16), 0).astype(_np.float32)
    inv[:, 3] = _np.where(p < 64, -1, 1)
    inv[:, 4] = _np.where(p % 64 < 32, -1, 1)
    inv[:, 5] = _np.where(p % 64 < 8, -1, 1)
    arrays["inv_freq_dram"] = inv
    args["inv_freq"] = nc.dram_tensor("inv_freq_dram", inv.shape, _mybir.dt.float32, kind="ExternalInput").ap()
    out = nc.dram_tensor("out_dram", (1, 256, 1024), _mybir.dt.float32, kind="ExternalOutput").ap()
    build(nc, args, out)
    r = _run(nc, [arrays], core_ids=[0])
    return r.results[0]["out_dram"]
```

```python
import numpy as np
import concourse.bass as bass
from concourse import mybir
from contextlib import ExitStack

F32 = mybir.dt.float32
I32 = mybir.dt.int32
F32R = mybir.dt.float32r
ALU = mybir.AluOpType
ACT = mybir.ActivationFunctionType
AX_X = mybir.AxisListType.X

P = 128
T = 256
D = 1024
KT = D // P
TT = T // P
RING = 4
SLOT = 4096
C = 32
NC4 = P // C
NH = 16
HD = 64
NQ = NH
FF = 2816
FT = FF // P
NE = 8
SLOTS = 128
WC = 352
LAM0 = 0.2
BIG = 1.0e30
DECAY = float(np.exp(-0.5))
TOPK = 64
ARENA = 29424

VEC = {}
for _n in ["c", "norm_g0", "norm_g1", "final_g", "ab00", "ab01", "ab02", "ab10", "ab11", "ab12",
           "cv0", "cv1", "cv2", "mu_r", "mu_k", "mu_v"]:
    VEC[_n] = 8 * len(VEC)
for _n in ["w0", "a0", "k_k", "k_a", "lnx_w", "lnx_b", "r_k", "mix0", "mix1", "ffn0", "ffn1", "ple0",
           "ple1", "fnorm", "cln_g", "cln_b"]:
    VEC[_n] = 8 * len(VEC)


class Chain:

    def __init__(self, eng, sem):
        self.eng, self.sem, self.n = eng, sem, 0

    def __call__(self, ins):
        ins.then_inc(self.sem, 1)
        self.n += 1

    def settle(self):
        self.eng.wait_ge(self.sem, self.n)


def build(nc, a, out):
    ctx = ExitStack()
    with ctx, nc.allow_non_contiguous_dma(reason="small parameter columns"):
        def sb(name, shape, dt=F32):
            return ctx.enter_context(nc.sbuf_tensor(name, shape, dt))

        sems = {}

        def sem(name):
            if name not in sems:
                sems[name] = ctx.enter_context(nc.semaphore(name))
            return sems[name]

        with nc.sbuf_tensor("ring_r", [P, RING, SLOT], F32R) as ring_r:
            pass
        ring = sb("ring", [P, RING, SLOT])
        xT = sb("xT", [P, KT, T])
        hT = sb("hT", [P, KT, T])
        ident = sb("ident", [P, P])
        ones = sb("ones", [P, P])
        swap_a = sb("swap_a", [P, P])
        swap_i = sb("swap_i", [P, P])
        swap_d = sb("swap_d", [P, P])
        hsel = sb("hsel", [P, 32])
        bmask = sb("bmask", [P, 2, P])
        segm = sb("segm", [P, T])
        pc = sb("pc", [P, 256])
        cw = sb("cw", [P, T])
        acw = sb("acw", [P, 4, 3])
        small = sb("small", [P, 64])
        mod = sb("mod", [P, 2, 24])
        gs = sb("gs", [P, 16])
        cond = sb("cond", [P, KT])
        nr = sb("nr", [P, T])
        stb = cw[0:16, :]
        hspread = sb("hspread", [16, KT, P])
        pend = sb("pend", [P, KT, 8])

        def sb_r(name, off, *shape):
            with nc.sbuf_tensor(f"{name}_before", [P, max(off, 1)], F32) as before:
                if off:
                    with nc.sbuf_tensor(name, [P, *shape], F32R) as t:
                        return t
            with nc.sbuf_tensor(name, [P, *shape], F32R) as t:
                return t

        hg_r = sb_r("hg_r", 0, 2, KT, SLOTS)
        his_r = sb_r("his_r", 15480, RING - 1, 3072)
        at_hi_r = sb_r("at_hi_r", 24696, FT, SLOTS)
        ffn_r = sb_r("ffn_r", 0, RING, 2048)
        h_r = sb_r("h_r", 8192, 2, KT, T)
        fa_hi_r = sb_r("fa_hi_r", 12288, FT, T)
        fa_lo_r = sb_r("fa_lo_r", 17920, FT, T)
        f2_r = sb_r("f2_r", 0, RING, FT * P)
        at_lo_r = sb_r("at_lo_r", 9984, FT, SLOTS)
        arena = sb("arena", [P, ARENA])

        def reg(off, *shape):
            n = int(np.prod(shape))
            assert off + n <= ARENA
            v = arena[:, off:off + n]
            if len(shape) == 1:
                return v
            names = " ".join(f"d{i}" for i in range(len(shape)))
            return v.rearrange(f"p ({names}) -> p {names}", **{f"d{i}": s for i, s in enumerate(shape)})

        bank = [ctx.enter_context(nc.psum_tensor(f"bank{i}", [P, 512], F32)) for i in range(8)]

        mulora = small[:, 0:1]
        subln = small[:, 1:2]
        posc_f = small[:, 4:6]
        lam = small[:, 6:7]
        invf = small[:, 8:14]

        def col(name, ct=0):
            return pc[:, VEC[name] + ct:VEC[name] + ct + 1]

        def cols8(name):
            return pc[:, VEC[name]:VEC[name] + 8]

        def hs(ct):
            return hsel[:, 14 - 2 * ct:30 - 2 * ct]

        def he(ct):
            return hspread[:, ct, :]

        VAL = reg(0, KT, T)
        GLU = reg(2048, KT, T)
        AG = reg(4096, KT, T)
        RR = reg(6144, KT, T)
        KK = reg(8192, KT, T)
        VV = reg(10240, KT, T)
        ZE = reg(4096, 32 * T)
        BG = reg(12288, KT, T)
        LO = reg(14336, 512)
        UP = reg(14848, KT, T + 30)
        YY = reg(17136, KT, T)
        X1 = reg(19184, KT, T)
        X2 = reg(21232, KT, T)
        X3 = reg(23280, KT, T)
        AR = reg(25328, KT, 2, T)
        X4 = GLU
        XTOK = reg(19184, TT, D)
        WU = reg(25328, D)
        PROW = reg(26352, 2, P)
        CROW = reg(26608, 2, P)
        ADA = reg(26864, 2, 512)
        A4T = reg(0, NQ, P)
        A3T = reg(4096, NQ, P)
        A2T = reg(19184, NQ, P)
        APT = reg(19184, KT, P)
        UU = reg(20208, NQ * HD)
        TBD = reg(21232, NQ, P)
        BTOK = reg(23280, D)
        VTOK = reg(24304, D)
        KTOK = reg(6144, D)
        ATOK = reg(7168, D)
        WW = reg(14336, NQ * HD)
        SS = reg(15360, KT, HD)
        TTP = reg(15872, C, C)
        LTC = reg(19184, 2 * NQ, C)
        LTP = reg(20208, C, C)
        TMP = reg(21232, 1024)
        YT = hT
        ltd = nc.dram_tensor("lt_scratch", (NC4, C, 2 * NQ, C), F32).ap()
        ttd = nc.dram_tensor("tt_scratch", (P, C * C), F32).ap()

        TOKS = [(lambda ct, t: AR[:, ct, 0, t], ATOK), (lambda ct, t: X4[:, ct, t], BTOK),
                (lambda ct, t: KK[:, ct, t], KTOK), (lambda ct, t: VV[:, ct, t], VTOK)]
        NSQ = [VAL]
        POSI = sb("posi", [P, 2], I32)
        taps = sem("tap_done")

        chunks, phases = [], {}
        count = {"pe": 0, "dve": 0}
        taken = {"act": 0, "dve": 0, "": 0}

        def add(name, k, ncol, n, tiles, src, taker="", reader="pe", loop=False, group=4, **more):
            phases[name] = dict(at=[len(chunks) + j for j in range(n)], k=k, ncol=ncol, n=n, tiles=tiles, src=src, loop=loop,
                                group=group, t0=count[reader], taker=taker, taken0=taken[taker], **more)
            taken[taker] += n * tiles
            for _ in range(n):
                count[reader] += tiles
                chunks.append((reader, count[reader]))

        def by_cols(w, width, first=0, k=D // P):
            v = w.rearrange("(k p) n -> p k n", p=P)
            return lambda j, i: v[:, :, bass.ds(first + (j + 4 * i) * width, width)]

        ewi, owi, awi = a["even_w_in"][0], a["odd_w_in"][0], a["a_w_in_2"][0]
        add("ada0", 8, 512, 6, 1, by_cols(a["ada_w"][0], 512), reader="dve")
        add("zA", 8, 512, 4, 4, by_cols(ewi, 512), "act")
        add("ada1", 8, 512, 6, 1, by_cols(a["ada_w"][1], 512), reader="dve")
        first = phases["zA"]["at"][0]
        merged = [("zA", 0), ("ada1", 0), ("ada1", 1), ("zA", 1), ("ada1", 2), ("ada1", 3), ("zA", 2), ("ada1", 4), ("ada1", 5),
                  ("zA", 3)]
        chunks[first:] = [chunks[phases[name]["at"][j]] for name, j in merged]
        for m, (name, j) in enumerate(merged):
            phases[name]["at"][j] = first + m
        add("zB", 8, 512, 8, 4, by_cols(ewi, 512, 2048), "act", loop=True)
        add("zL", 8, 128, 1, 1, by_cols(ewi, 128, 6144), "act")
        add("zG", 8, 512, 2, 4, by_cols(ewi, 512, 6272), "act")
        add("eo", 16, 256, 4, 2, by_cols(a["even_w_out"][0], 256, k=16), "dve")
        M1 = 2048
        add("m1", 8, 512, 1, 4, by_cols(owi, 512, M1), "act")
        add("m2", 8, 328, 1, 4, by_cols(owi, 328, M1 + 512), "act")
        add("q", 8, 512, 4, 4, by_cols(owi, 512), "act")
        add("g", 8, 512, 4, 4, by_cols(owi, 512, M1 + 840), "act")
        add("oo", 16, 256, 4, 2, by_cols(a["odd_w_out"][0], 256, k=16), "dve")
        add("qk", 8, 512, 2, 4, by_cols(awi, 512), "act")
        add("v", 8, 512, 1, 2, by_cols(awi, 512, 1024), "act")
        add("bch", 8, 512, 3, 4, by_cols(awi, 512, 1536), "act")
        add("ao", 8, 512, 2, 4, by_cols(a["a_w_out_2"][0], 512), "dve")
        f1, f3 = (a[f"ffn_{w}_2"][0].rearrange("(k p) n -> p k n", p=P) for w in ("w1", "w3"))
        add("f13", 8, 256, 22, 2, lambda j, i: (f1, f3)[j % 2][:, :, bass.ds((j // 2 + 2 * i) * 256, 256)], loop=True)
        add("f2", FT, 128, 8, 1, by_cols(a["ffn_w2_2"][0], 128, k=FT), "dve")
        add("pg0", 8, 512, 2, 4, by_cols(a["ple_gate_2"][0], 512), "act")
        add("pp0", 2, 1024, 1, 8, by_cols(a["ple_proj_2"][0], 1024, k=2), "dve")
        add("cin", 8, 512, 4, 4, by_cols(a["c_w_in_2"][0], 512), "act")
        add("cout", 8, 512, 2, 4, by_cols(a["c_w_out_2"][0], 512), "dve")

        W2F = [3, 3, 3, 3, 3, 3, 2, 2]
        up1, up3 = (a[f"moe_{w}_2"][0].rearrange("e (k p) n -> e p k n", p=P) for w in ("w1", "w3"))
        down = a["moe_w2_2"][0].rearrange("e (f p) n -> e p f n", p=P)
        UPS, DOWNS = 2 * FF // WC, len(W2F)

        def is_split(j):
            return j % 4 < 3

        def down_tiles(j):
            f = sum(W2F[:j - UPS])
            return range(f, f + W2F[j - UPS])

        def tiles_split(g):
            return [f for j in range(UPS, UPS + DOWNS) if is_split(j) for f in down_tiles(j) if f // 4 == g]

        def split_no(j):
            return sum(is_split(m) for m in range(j + 1))

        SPLITS = split_no(UPS + DOWNS - 1)

        def moe_shape(j):
            return (KT, WC) if j < UPS else (W2F[j - UPS], D)

        def moe_src(j, e):
            ex = slice(e, e + 1) if isinstance(e, int) else bass.ds(e, 1)
            if j < UPS:
                v = (up1, up3)[j % 2][ex, :, :, WC * (j // 2):WC * (j // 2) + WC]
            else:
                f = sum(W2F[:j - UPS])
                v = down[ex, :, f:f + W2F[j - UPS], :]
            return v.rearrange("e p k n -> (e p) k n")

        add("moe", 0, 0, NE * (UPS + DOWNS), 1, moe_src, loop=True, group=UPS + DOWNS, shape=moe_shape)
        add("pg1", 8, 512, 2, 4, by_cols(a["ple_gate_2"][1], 512), "act")
        add("pp1", 2, 1024, 1, 8, by_cols(a["ple_proj_2"][1], 1024, k=2), "dve")

        QT = reg(0, NH, T)
        GT = reg(4096, NH, T)
        QI = reg(8192, 4, T)
        KI = reg(9216, 1, T)
        KC = reg(9472, 1, T)
        VTK = reg(9728, TT, P)
        WI = reg(9984, TT, NE)
        ROT = reg(10240, 3, 2, T)
        ANG = reg(11776, 3, T)
        POSB = reg(12544, T)
        CHUNKS = reg(12800, T)
        ADM = reg(13056, TT, T)
        CUR = reg(13568, TT, T)
        RELU = reg(14080, 2, T)
        TOP = reg(14592, TT, 8)
        MASK = reg(14608, TT, T)
        SWP = reg(18000, 2, 2, T)
        LG = reg(15120, 3, 2, T)
        PT = reg(16656, 2, 2 * T)
        MX = reg(17680, 3, 2)
        SM = reg(17688, 3, 2)
        CHC = reg(17686, TT)
        ANG2 = reg(19200, 3, T)
        ANG3 = reg(19968, 3, T)
        POSB2 = reg(20736, T)
        QK = reg(0, KT, T)
        VD = reg(2048, TT, 512)
        BCH = reg(3072, 12, T)
        UC = reg(6144, 4, T + 2)
        CV = reg(7176, 4, T)
        OD = reg(8200, 4, T)
        CMASK = reg(9224, TT, T)
        LAMB = reg(9736, 4, 64)
        RD = reg(12544, 4, T)
        SQD = reg(13568, 4, T)
        FA = reg(17920, FT, T)
        FAF = reg(17920, FT * T)
        PTOK = reg(23552, 2, TT, T)
        PPT = reg(2048, 2, 2, T)
        PG = reg(0, KT, T)
        CU = reg(4096, KT, T)
        CVV = reg(6144, KT, T)
        VTS = reg(8192, TT, D)
        WS = reg(10240, 8, P)
        WST = reg(11264, 8, P)
        BSB = reg(12288, 8, P)
        HTOK = reg(4096, TT, D)
        HG = reg(6144, KT, SLOTS)
        HG_HI = hg_r[:, 0]
        HG_LO = hg_r[:, 1]
        HIS = [his_r[:, s] for s in range(RING - 1)]
        AT_HI = at_hi_r
        AT_LO = at_lo_r
        AA = reg(7168, FF)
        AT = reg(9984, FT, SLOTS)
        YS = reg(12800, D)
        GTS = reg(13824, T)
        PSEL = reg(14080, TT, SLOTS)
        GSEL = reg(14336, TT, SLOTS)
        RW = reg(14592, KT, NE)
        RL = reg(14656, TT, NE)
        SEL = reg(14672, TT, NE)
        GATE = reg(14688, TT, NE)
        RANK = reg(14704, TT, NE)
        CNT = reg(14720, 4, NE)
        R64 = reg(14752, 2, TT, NE * NE)
        LOWE = reg(15008, NE, NE)
        IOTA = reg(15072, 2, SLOTS)
        TRI = reg(15328, P)
        ECOL = reg(15456, NE)
        NEG = reg(15464, 8)
        OVER = reg(15472, 4)
        OSLOT = [reg(15480 + 3072 * s, 3072) for s in range(RING)]
        OVERI = sb("overi", [1, 4], I32)
        ROUNDS = (2 * T - 1) // (SLOTS + 1)
        SQ2 = reg(27376, KT, T)
        OT = reg(0, TT, D)
        NSQ += [SQ2] * 9

        ROTS = [(lambda: QI[:, 0:2, :], 1, 2), (lambda: QI[:, 2:4, :], 1, 2), (lambda: KI, 1, 1), (lambda: KC, 0, 1)] + \
            [(lambda j=j: QT[:, 2 * j:2 * j + 2, :], 0, 2) for j in range(8)] + \
            [(lambda j=j: QK[:, 2 * j:2 * j + 2, :], 2, 2) for j in range(4)]
        def f2_hi(j):
            return f2_r[:, phases["f2"]["at"][j] % RING].rearrange("p (k n) -> p k n", k=FT)

        LOGITS = [4, 5, 2]
        def ffn_hi(j):
            return ffn_r[:, phases["f13"]["at"][j] % RING].rearrange("p (k n) -> p k n", k=KT)

        SWAPS = [swap_a, swap_i, swap_d]
        PI = float(np.float32(np.pi))
        TWO_PI = [float(np.float32(v)) for v in (6.28125, 0.0019350051879882812, 3.0199159819567e-07)]
        assert abs(sum(TWO_PI) - 2 * np.pi) < 1e-10
        MAGIC = 1.5 * 2.0 ** 23

        def over_round(eng, r, body):
            n = eng.value_load(OVERI[0:1, 0:1], min_val=0, max_val=ROUNDS)
            with eng.If(n > r):
                body()

        def finish_sync(sp):
            sp.wait_ge(sem("over_ready"), 1)
            with sp.Fori(0, ROUNDS) as r:
                n = sp.value_load(OVERI[0:1, 0:1], min_val=0, max_val=ROUNDS)
                with sp.If(n > r):
                    e = sp.value_load(OVERI[0:1, bass.ds(r + 1, 1)], min_val=0, max_val=NE - 1)
                    sp.wait_ge(sem("psel_ready"), 4 * (r + NE) + 2)
                    for j in range(UPS + DOWNS):
                        if j >= RING:
                            sp.wait_ge(sem("over_acc"), (UPS + DOWNS) * r + j - RING + 1)
                        k, n_ = moe_shape(j)
                        sp.dma_start(OSLOT[j % RING][:, 0:k * n_].rearrange("p (k n) -> p k n", k=k), moe_src(j, e))\
                            .then_inc(sem(f"over_loaded_{j % RING}"), 16)
            sp.wait_ge(sem("toks_taken"), TK_OUT + 4)
            sp.dma_start(out[0].rearrange("(u p) n -> p u n", p=P), OT[:, :, :]).then_inc(sem("stored"), 16)
            sp.wait_ge(sem("stored"), 16)

        TK_P, TK_V, TK_W, TK_H, TK_OUT = 16, 18, 22, 24, 28

        def more_pool(pool, ch):
            def step(ins):
                ch(ins)
                ch.settle()
            q = sem("late_loaded")
            pool.wait_ge(sem("yb_ready"), 1)
            pool.dma_start(POSB.bitcast(I32), a["positions"][0].partition_broadcast(P)).then_inc(q, 16)
            pool.dma_start(POSB2.bitcast(I32), a["positions_2"][0].partition_broadcast(P)).then_inc(q, 16)
            pool.dma_start(PTOK[:, 0, :, :], a["p_2"][0, 0].rearrange("(u p) n -> p u n", p=P)).then_inc(sem("p_loaded"), 16)
            pool.dma_start(PTOK[:, 1, :, :], a["p_2"][1, 0].rearrange("(u p) n -> p u n", p=P)).then_inc(sem("p_loaded"), 16)
            pool.wait_ge(*took("oo", 8))
            pool.dma_start(LAMB.rearrange("p a b -> p (a b)"), a["a_lambda_2"][0].rearrange("a b -> (a b)").partition_broadcast(P))\
                .then_inc(sem("lam_loaded"), 16)
            step(pool.memset(UC[:, :, 0:2], 0.0))
            step(pool.memset(CMASK[:, :, :], 0.0))
            pool.affine_select(out=CMASK[:, :, :], in_=CMASK[:, :, :], compare_op=ALU.is_ge, fill=-BIG, base=0,
                               pattern=[[P, TT], [-1, T]], channel_multiplier=1).then_inc(sem("cmask_ready"), 1)
            pool.wait_ge(sem("cmask_ready"), 1)
            pool.wait_ge(*took("f2", 8))
            pool.dma_start(WS[:, :, :], a["c_w_s_2"][0].rearrange("g t s -> t g s")).then_inc(sem("ws_loaded"), 16)
            pool.wait_ge(*took("pp0", 8))
            pool.dma_start(BSB[:, :, :].rearrange("p g t -> p (g t)"), a["c_b_s_2"][0].rearrange("g t -> (g t)").partition_broadcast(P))\
                .then_inc(sem("bs_loaded"), 16)
            pool.wait_ge(sem("toks_taken"), TK_W + 2)
            pool.affine_select(out=WST[:, :, :], in_=WST[:, :, :], compare_op=ALU.is_ge, fill=0.0, base=0,
                               pattern=[[0, 8], [1, P]], channel_multiplier=-1).then_inc(sem("ws_masked"), 1)
            pool.wait_ge(sem("ws_masked"), 1)
            pool.wait_ge(*took("cout", 8))
            pool.dma_start(RW[:, :, :], a["router_w_2"][0].rearrange("(k p) e -> p k e", p=P)).then_inc(sem("rw_loaded"), 16)
            step(pool.memset(TRI, 1.0))
            step(pool.affine_select(out=TRI, in_=TRI, compare_op=ALU.is_gt, fill=0.0, base=0, pattern=[[1, P]],
                                    channel_multiplier=-1))
            step(pool.memset(LOWE[:, :, :], 1.0))
            step(pool.affine_select(out=LOWE[:, :, :], in_=LOWE[:, :, :], compare_op=ALU.is_gt, fill=0.0, base=0,
                                    pattern=[[1, NE], [-1, NE]], channel_multiplier=0))
            step(pool.iota(ECOL, [[1, NE]], base=0, channel_multiplier=0, allow_small_or_imprecise_dtypes=True))
            pool.iota(IOTA[:, :, :], [[SLOTS, 2], [1, SLOTS]], base=0, channel_multiplier=0,
                      allow_small_or_imprecise_dtypes=True).then_inc(sem("moe_const"), 1)

        def pe_rest(pe):
            mm = nc.tensor.matmul
            tr = nc.tensor.transpose

            def norm(i, after):
                pe_sum(bank[4][:, 0:T], NSQ[i], [(sem("norm_squares"), 2 * (i + 1))] + after, sem("norm_summed"))

            def parts(b, x_lo, x_hi, w_lo, w_hi):
                terms = [(x, w, k) for x, w in ((x_hi, w_lo), (x_lo, w_hi), (x_hi, w_hi)) for k in range(x_hi.shape[1])]
                for n, (x, w, k) in enumerate(terms):
                    ins = mm(b, x[:, k, :], w[:, k, :], start=(n == 0), stop=(n == len(terms) - 1))
                return ins

            def rot(lo, hi):
                for i in range(lo, hi):
                    src, table, n = ROTS[i]
                    if i >= 2:
                        pe.wait_ge(sem("rot_done"), i - 1)
                    mm(bank[5 + i % 2][:, 0:n * T], SWAPS[table][:, :], src(), start=True, stop=True)\
                        .then_inc(sem("swapped"), 1)

            def tokens(n0, after, src, n):
                for s, v in after:
                    pe.wait_ge(s, v)
                for b in range(n):
                    if b >= 4:
                        pe.wait_ge(sem("toks_taken"), n0 + b - 3)
                    for j in range(4):
                        s = src(b, j)
                        ins = tr(bank[b % 4][:, j * P:(j + 1) * P], s, ident[:, :])
                    ins.then_inc(sem("toks_ready"), 1)

            norm(1, [took("eo", 8)])
            h = lambda k: hT[:, k, :]

            def values(b, w):
                for tt in range(TT):
                    for k in range(KT):
                        ins = mm(b[:, tt * P:(tt + 1) * P], hT[:, k, tt * P:(tt + 1) * P], w[:, k, P:2 * P],
                                 start=(k == 0), stop=(k == KT - 1))
                return ins

            def index_keys(b, w):
                for half in range(2):
                    for k in range(KT):
                        ins = mm(b[64 * half:64 * half + 64, 0:T], w[:, k, 256:320], hT[:, k, :], start=(k == 0), stop=(k == KT - 1))
                return ins

            def head_weights(b, w):
                for tt in range(TT):
                    for k in range(KT):
                        ins = mm(b[:, tt * NE:(tt + 1) * NE], hT[:, k, tt * P:(tt + 1) * P], w[:, k, 320:328],
                                 start=(k == 0), stop=(k == KT - 1))
                return ins

            pe_gemm("m1", h, [(sem("h_ready"), 2)], special={1: values})
            pe_gemm("m2", h, [took("m1", 4)], special={2: index_keys, 3: head_weights})
            pe.wait_ge(*took("m2", 4))
            rot(0, 4)
            pe.wait_ge(sem("rot_done"), 4)
            for n in range(16):
                tt, hh = n // 8, n % 8
                r = slice(64 * (hh % 2), 64 * (hh % 2) + 64)
                if n >= 2:
                    pe.wait_ge(sem("relu_done"), n - 1)
                mm(bank[7 if hh % 2 == 0 else 4][:, 0:T], QI[r, hh // 2, tt * P:(tt + 1) * P], KI[r, 0, :], start=True, stop=True)\
                    .then_inc(sem("index_ready"), 1)
            pe_gemm("q", h, [])
            pe_gemm("g", h, [took("q", 16)])
            rot(4, 12)
            pe.wait_ge(sem("rot_done"), 12)
            pe.wait_ge(*took("g", 16))
            pe.wait_ge(sem("relu_done"), 16)

            def attend(n0, count, ahead, logits, turned, result):
                for b in range(ahead):
                    logits(b)
                for b in range(count + 1):
                    if b + ahead < count:
                        logits(b + ahead)
                    if b < count:
                        pe.wait_ge(sem("weights_ready"), n0 + b + 1)
                        if b >= 2:
                            pe.wait_ge(sem("pt_ready"), n0 + b - 1)
                        turned(b)
                    if b >= 1:
                        pe.wait_ge(sem("pt_ready"), n0 + b)
                        if b >= 3:
                            pe.wait_ge(sem("o_taken"), n0 + b - 2)
                        result(b - 1)

            def logits(b):
                tt, hp = b % 2, b // 2
                if b >= 3:
                    pe.wait_ge(sem("logits_taken"), b - 2)
                for j in range(2):
                    ins = mm(bank[LOGITS[b % 3]][:, j * T:(j + 1) * T], QT[:, 2 * hp + j, tt * P:(tt + 1) * P], KC[:, 0, :],
                             start=True, stop=True)
                ins.then_inc(sem("logits_ready"), 1)

            def turned(b):
                for sc in range(2):
                    for j in range(2):
                        ins = tr(bank[6 + b % 2][:, (2 * sc + j) * P:(2 * sc + j + 1) * P],
                                 LG[:, b % 3, j, sc * P:(sc + 1) * P], ident[:, :])
                ins.then_inc(sem("turned_ready"), 1)

            def result(b):
                for sc in range(2):
                    ins = mm(bank[b % 2][:, 0:T], VTK[:, sc, :], PT[:, b % 2, sc * T:(sc + 1) * T], start=(sc == 0), stop=(sc == 1))
                ins.then_inc(sem("o_ready"), 1)

            attend(0, 16, 2, logits, turned, result)
            pe_gemm("oo", lambda k: GT[:, k, :], [(sem("o_taken"), 16)])
            norm(2, [took("oo", 8)])
            norm(3, [])

            def values2(tt):
                def f(b, w):
                    for k in range(KT):
                        ins = mm(b[:, :], hT[:, k, tt * P:(tt + 1) * P], w[:, k, :], start=(k == 0), stop=(k == KT - 1))
                    return ins
                return f

            pe_gemm("qk", h, [(sem("h_ready"), 4)])
            pe_gemm("v", h, [took("qk", 8)], special={0: values2(0), 1: values2(1)})
            rot(12, 16)
            pe_gemm("bch", h, [took("v", 2)])
            pe.wait_ge(sem("rot_done"), 16)
            pe.wait_ge(*took("bch", 12))

            def logits2(b):
                tt, hh = b % 2, b // 2
                if b >= 2:
                    pe.wait_ge(sem("logits_taken"), 16 + b - 1)
                for c in range(2):
                    r = slice(64 * c, 64 * c + 64)
                    ins = mm(bank[4 + 2 * (b % 2) + c][:, 0:T], QK[r, hh, tt * P:(tt + 1) * P], QK[r, 4 + hh, :], start=True, stop=True)
                ins.then_inc(sem("logits_ready"), 1)

            def turned2(b):
                for sc in range(2):
                    ins = tr(bank[2 + b % 2][:, sc * P:(sc + 1) * P], LG[:, b % 2, 0, sc * P:(sc + 1) * P], ident[:, :])
                ins.then_inc(sem("turned_ready"), 1)

            def result2(b):
                for sc in range(2):
                    ins = mm(bank[b % 2][:, 0:P], VD[:, sc, (b // 2) * P:(b // 2 + 1) * P], PT[:, b % 2, sc * P:(sc + 1) * P],
                             start=(sc == 0), stop=(sc == 1))
                ins.then_inc(sem("o_ready"), 1)

            attend(16, 8, 1, logits2, turned2, result2)
            pe.wait_ge(sem("squares_ready"), 4)
            for c in range(2):
                ins = mm(bank[4 + c][:, :], ones[:, :], SQD[:, 2 * c:2 * c + 2, :], start=True, stop=True)
            ins.then_inc(sem("o_summed"), 1)
            pe_gemm("ao", lambda k: OD[:, k, :] if k < 4 else CV[:, k - 4, :], [(sem("o_normed"), 1)])
            norm(4, [took("ao", 8)])
            pe.wait_ge(sem("x_split"), 2)

            def f13(j, i):
                pe.wait_ge(sem("lo_ready"), 4 * i + (j + 1))
                lo, hi = view(phases["f13"], j, ring_r), ffn_hi(j)
                if j >= 2 or not isinstance(i, int):
                    pe.wait_ge(sem("silu_taken") if j % 2 == 0 else sem("gate_taken"), 2 * (j // 2) + 4 * i)
                for m in range(2):
                    c = slice(m * P, m * P + P)
                    parts(bank[2 * (j % 2) + m][:, 0:T], lo[:, :, c], hi[:, :, c], h_r[:, 1], h_r[:, 0]).then_inc(acc_ready, 1)

            each_chunk(pe, "f13", f13, first=1)
            pe.wait_ge(sem("x_split"), 2 + 2 * FT)
            for j in range(KT):
                pe.wait_ge(sem("lo_ready"), FT + j + 1)
                if j >= 4:
                    pe.wait_ge(*took("f2", j - 3))
                parts(bank[j % 4][:, 0:T], view(phases["f2"], j, ring_r), f2_hi(j), fa_lo_r, fa_hi_r).then_inc(acc_ready, 1)

            def embed(i):
                pe.wait_ge(sem("p_loaded"), 32)
                for c in range(2):
                    for tt in range(TT):
                        ins = tr(bank[7][:, c * T + tt * P:c * T + (tt + 1) * P], PTOK[:, i, tt, c * P:(c + 1) * P], ident[:, :])
                ins.then_inc(sem("toks_ready"), 1)

            def ple(i, nrm, before):
                norm(nrm, [before])
                pe_gemm(f"pg{i}", h, [(sem("h_ready"), nrm + 1)])
                pe_gemm(f"pp{i}", lambda k: PPT[:, i, k, :], [took(f"pg{i}", 8), (sem("toks_taken"), TK_P + 2)])

            embed(0)
            pe.wait_ge(sem("toks_taken"), TK_P + 1)
            embed(1)
            ple(0, 5, took("f2", 8))
            norm(6, [took("pp0", 8), (sem("embedded"), 1)])
            pe_gemm("cin", h, [(sem("h_ready"), 7)])
            pe_sum(bank[4][:, 0:T], CVV, [took("cin", 16)], sem("mean_summed"))
            pe_sum(bank[5][:, 0:T], SQ2, [(sem("squares_ready"), 5)], sem("var_summed"))
            tokens(TK_V, [(sem("cln_done"), 1)], lambda b, j: CVV[:, 4 * (b % 2) + j, (b // 2) * P:(b // 2 + 1) * P], 4)
            pe.wait_ge(sem("ws_loaded"), 16)
            for b in range(2):
                for j in range(4):
                    ins = tr(bank[6 + b][:, j * P:(j + 1) * P], WS[:, 4 * b + j, :], ident[:, :])
                ins.then_inc(sem("toks_ready"), 1)
            pe.wait_ge(sem("toks_taken"), TK_V + 4)
            pe.wait_ge(sem("ws_masked"), 1)
            for g in range(8):
                for tt in range(TT):
                    ins = mm(bank[g // 2][:, (g % 2) * T + tt * P:(g % 2) * T + (tt + 1) * P], VTS[:, tt, g * P:(g + 1) * P], WST[:, g, :],
                             start=True, stop=True)
                if g % 2 == 1:
                    ins.then_inc(sem("spatial_ready"), 1)
            pe_gemm("cout", lambda k: CU[:, k, :], [(sem("spatial_taken"), 4)])
            norm(7, [took("cout", 8)])
            tokens(TK_H, [(sem("h_ready"), 8)], lambda b, j: hT[:, 4 * (b % 2) + j, (b // 2) * P:(b // 2 + 1) * P], 4)
            pe.wait_ge(sem("rw_loaded"), 16)
            for tt in range(TT):
                for k in range(KT):
                    ins = mm(bank[5][:, tt * NE:(tt + 1) * NE], hT[:, k, tt * P:(tt + 1) * P], RW[:, k, :], start=(k == 0), stop=(k == KT - 1))
            ins.then_inc(sem("router_ready"), 1)
            pe.wait_ge(sem("sel_ready"), 1)
            mm(bank[6][:, 0:NE], TRI, SEL[:, 0, :], start=True, stop=True)
            mm(bank[6][:, NE:2 * NE], ones[:, :], SEL[:, 0, :], start=True, stop=False)
            mm(bank[6][:, NE:2 * NE], TRI, SEL[:, 1, :], start=False, stop=True)
            mm(bank[6][:, 2 * NE:3 * NE], ones[:, :], SEL[:, 0, :], start=True, stop=False)
            mm(bank[6][:, 2 * NE:3 * NE], ones[:, :], SEL[:, 1, :], start=False, stop=True).then_inc(sem("rank_ready"), 1)
            pe.wait_ge(sem("toks_taken"), TK_H + 4)
            pe.wait_ge(sem("rank_taken"), 1)

            def gather(i):
                pe.wait_ge(sem("psel_ready"), 4 * i + 2)
                for ct in range(KT):
                    for tt in range(TT):
                        ins = mm(bank[6 + ct // 4][:, (ct % 4) * P:(ct % 4 + 1) * P], HTOK[:, tt, ct * P:(ct + 1) * P], PSEL[:, tt, :],
                                 start=(tt == 0), stop=(tt == 1))
                    if ct % 4 == 3:
                        ins.then_inc(sem("gather_ready"), 1)

            def expert(i, acc, weights, split, following):
                def chunk(j):
                    if not (split and is_split(j)):
                        return weights(j), None
                    pe.wait_ge(sem("lo_ready"), SPLITS * i + (FT + KT + split_no(j)))
                    k, n = moe_shape(j)
                    return view(phases["moe"], j, ring_r), HIS[j % RING][:, 0:k * n].rearrange("p (k n) -> p k n", k=k)

                pe.wait_ge(sem("hg_taken"), 2 * i + 2)
                pe.wait_ge(sem("psel_ready"), 4 * i + 4)
                for tt in range(TT):
                    ins = tr(bank[6][:, tt * P:(tt + 1) * P], GSEL[:, tt, :], ident[:, :])
                ins.then_inc(sem("gsel_turned"), 1)
                if split:
                    pe.wait_ge(sem("x_split"), 2 * i + (2 * FT + 4))
                for j in range(UPS):
                    w, hi = chunk(j)
                    if j >= 4:
                        pe.wait_ge(sem("moe_silu") if j % 2 == 0 else sem("moe_gated"), (UPS // 2) * i + j // 2 - 1)
                    b = bank[2 * (j % 2) + (j // 2) % 2][:, 0:WC]
                    if hi is not None:
                        ins = parts(b, HG_LO, HG_HI, w, hi)
                    else:
                        for k in range(KT):
                            ins = mm(b, HG[:, k, :], w[:, k, :], start=(k == 0), stop=(k == KT - 1))
                    ins.then_inc(acc, 1)
                pe.wait_ge(sem("moe_gated"), (UPS // 2) * (i + 1))
                pe.wait_ge(sem("gs_taken"), i + 1)
                for g in range(6):
                    if g >= 4:
                        pe.wait_ge(sem("at_taken"), 6 * i + g - 3)
                    for f in range(4 * g, min(4 * g + 4, FT)):
                        ins = tr(bank[4 + g % 4][:, (f % 4) * P:(f % 4 + 1) * P], AA[:, f * P:(f + 1) * P], ident[:, :])
                    ins.then_inc(sem("at_ready"), 1)
                for j in range(UPS, UPS + DOWNS):
                    w, hi = chunk(j)
                    for n, f in enumerate(down_tiles(j)):
                        if f % 4 == 0 or n == 0:
                            pe.wait_ge(sem("at_taken"), 6 * i + (f // 4 + 1))
                            if hi is not None:
                                pe.wait_ge(sem("at_split"), 10 * i + 2 * (f // 4 + 1))
                        for half in range(2):
                            c = slice(512 * half, 512 * half + 512)
                            if hi is None:
                                terms = [(AT[:, f, :], w[:, n, c])]
                            else:
                                terms = [(x[:, f, :], y[:, n, c]) for x, y in ((AT_HI, w), (AT_LO, hi), (AT_HI, hi))]
                            for m, (x, y) in enumerate(terms):
                                ins = mm(bank[half][:, :], x, y, start=(f == 0 and m == 0), stop=(f == FT - 1))
                    ins.then_inc(acc, 1)
                if following:
                    gather(i + 1)
                pe.wait_ge(sem("ys_taken"), 2 * i + 2)
                for ct in range(KT):
                    ins = mm(bank[2 + ct // 2][:, (ct % 2) * T:(ct % 2 + 1) * T], YS[:, ct * P:(ct + 1) * P], GTS, start=True, stop=True)
                    if ct % 2 == 1:
                        ins.then_inc(sem("scat_ready"), 1)

            gather(0)
            with pe.Fori(0, NE - 1) as e:
                expert(e, acc_ready, lambda j: wait_chunk(pe, "moe", j, e), True, True)
            expert(NE - 1, acc_ready, lambda j: wait_chunk(pe, "moe", j, NE - 1), True, False)
            pe.wait_ge(sem("over_ready"), 1)
            with pe.Fori(0, ROUNDS) as r:
                n = pe.value_load(OVERI[0:1, 0:1], min_val=0, max_val=ROUNDS)
                with pe.If(n > r):
                    def over_weights(j):
                        pe.wait_ge(sem(f"over_loaded_{j % RING}"), 16 * (j // RING + 1) + 16 * ((UPS + DOWNS) // RING) * r)
                        k, n_ = moe_shape(j)
                        return OSLOT[j % RING][:, 0:k * n_].rearrange("p (k n) -> p k n", k=k)
                    gather(r + NE)
                    expert(r + NE, sem("over_acc"), over_weights, False, False)
            ple(1, 8, (sem("moe_done"), 1))
            norm(9, [took("pp1", 8), (sem("embedded"), 2)])
            tokens(TK_OUT, [(sem("h_ready"), 10)], lambda b, j: hT[:, 4 * (b % 2) + j, (b // 2) * P:(b // 2 + 1) * P], 4)


        def act_rest(act, ch, A, norm):
            act.wait_ge(sem("angles_ready"), 1)
            for k in range(3):
                A(ROT[:, k, 1, :], ANG[:, k, :], ACT.Sin, scale=small[:, 11 + k:12 + k]).then_inc(sem("rot_tables"), 1)
            A(ROT[:, :, 0, :], ANG2[:, :, :], ACT.Sin).then_inc(sem("rot_tables"), 1)
            norm(1, [took("eo", 8)])

            def take_m1(q, lin, b):
                if q == 0:
                    return A(KC[:, 0, :], b, ACT.Copy)
                if q == 1:
                    return A(VTK[:, :, :], b.rearrange("p (u v) -> p u v", u=TT), ACT.Copy)
                return A(QI[:, q - 2, :], b, ACT.Copy)

            def take_m2(q, lin, b):
                if q < 2:
                    return A(QI[:, 2 + q, :], b, ACT.Copy)
                if q == 2:
                    return A(KI[:, 0, :], b, ACT.Copy)
                return A(WI[:, :, :], b[:, 0:TT * NE].rearrange("p (u e) -> p u e", u=TT), ACT.Copy, scale=NE ** -0.5)

            take_gemm(act, "m1", take_m1)
            take_gemm(act, "m2", take_m2)
            for n in range(16):
                act.wait_ge(sem("index_ready"), n + 1)
                if n >= 2:
                    act.wait_ge(sem("score_added"), n - 1)
                A(RELU[:, n % 2, :], bank[7 if n % 2 == 0 else 4][:, 0:T], ACT.Relu, scale=HD ** -0.5).then_inc(sem("relu_done"), 1)
            take_gemm(act, "q", lambda q, lin, b: A(QT[:, q, :], b, ACT.Copy))
            take_gemm(act, "g", lambda q, lin, b: A(GT[:, q, :], b, ACT.Silu))

            def attend(n0, count, ahead, banks, width):
                def exps(b):
                    act.wait_ge(sem("max_ready"), n0 + b + 1)
                    m = b % (ahead + 1)
                    for j in range(2):
                        A(LG[:, m, j, :], LG[:, m, j, :], ACT.Exp, bias=MX[:, m, j:j + 1],
                          accum_out=SM[:, m, j:j + 1]).then_inc(sem("exps_ready"), 1)
                for b in range(ahead):
                    exps(b)
                for b in range(count):
                    if b + ahead < count:
                        exps(b + ahead)
                    act.wait_ge(sem("turned_ready"), n0 + b + 1)
                    if b >= 2:
                        act.wait_ge(sem("o_ready"), n0 + b - 1)
                    A(PT[:, b % 2, 0:width], bank[banks + b % 2][:, 0:width], ACT.Copy).then_inc(sem("pt_ready"), 1)

            attend(0, 16, 2, 6, 2 * T)
            norm(2, [took("oo", 8)])
            norm(3, [(sem("h_ready"), 3)])
            take_gemm(act, "qk", lambda q, lin, b: A(QK[:, q, :], b, ACT.Copy))
            take_gemm(act, "v", lambda q, lin, b: A(VD[:, q, :], bank[q][:, :], ACT.Copy))
            take_gemm(act, "bch", lambda q, lin, b: A(BCH[:, q, :], b, ACT.Copy))
            act.wait_ge(sem("lam_sums"), 1)
            A(small[:, 14:16], small[:, 14:16], ACT.Exp).then_inc(sem("lam_exps"), 1)
            attend(16, 8, 1, 2, T)
            act.wait_ge(sem("o_taken"), 24)
            A(SQD[:, :, :], OD[:, :, :], ACT.Square).then_inc(sem("squares_ready"), 1)
            act.wait_ge(sem("o_summed"), 1)
            for c in range(2):
                A(RD[:, 2 * c:2 * c + 2, :], bank[4 + c][:, :].rearrange("p (h t) -> p h t", h=2), ACT.Sqrt, bias=1e-6, scale=1.0 / P)\
                    .then_inc(sem("rooted"), 1)
            norm(4, [took("ao", 8)])

            def silu(j, i):
                if j % 2 == 0:
                    for m in range(2):
                        act.wait_ge(acc_ready, phases["f13"]["t0"] + 2 * j + m + 1 + 8 * i)
                        f = j + m + 4 * i
                        A(FAF[:, bass.ds(f * T, T)], bank[m][:, 0:T], ACT.Silu).then_inc(sem("silu_taken"), 1)

            each_chunk(act, "f13", silu)
            for i in range(2):
                act.wait_ge(sem("toks_ready"), TK_P + 1 + i)
                A(PPT[:, i, :, :], bank[7][:, :].rearrange("p (c t) -> p c t", c=2), ACT.Copy).then_inc(sem("toks_taken"), 1)
            norm(5, [took("f2", 8)])
            take_gemm(act, "pg0", lambda q, lin, b: A(PG[:, q, :], b, ACT.Sigmoid))
            norm(6, [(sem("embedded"), 1)])
            take_gemm(act, "cin", lambda q, lin, b: A(CU[:, q, :] if q < KT else CVV[:, q - KT, :], b, ACT.Gelu))
            act.wait_ge(sem("centred"), 6)
            A(SQ2[:, :, :], CVV[:, :, :], ACT.Square).then_inc(sem("squares_ready"), 1)
            act.wait_ge(sem("var_summed"), 3)
            A(nr[:, :], bank[5][:, 0:T], ACT.Sqrt, bias=1e-5, scale=1.0 / D).then_inc(sem("rooted"), 1)

            def tokens(n0, dst):
                for b in range(4):
                    act.wait_ge(sem("toks_ready"), n0 + b + 1)
                    A(dst[:, b // 2, 512 * (b % 2):512 * (b % 2) + 512], bank[b][:, :], ACT.Copy).then_inc(sem("toks_taken"), 1)

            tokens(TK_V, VTS)
            for b in range(2):
                act.wait_ge(sem("toks_ready"), TK_W + b + 1)
                A(WST[:, 4 * b:4 * b + 4, :], bank[6 + b][:, :].rearrange("p (g t) -> p g t", g=4), ACT.Copy).then_inc(sem("toks_taken"), 1)
            norm(7, [took("cout", 8)])
            tokens(TK_H, HTOK)
            act.wait_ge(sem("gates_centred"), 1)
            A(GATE[:, :, :], GATE[:, :, :], ACT.Exp).then_inc(sem("gate_exps"), 1)

            def gathered(i):
                for g in range(2):
                    act.wait_ge(sem("gather_ready"), 2 * i + (g + 1))
                    A(HG[:, 4 * g:4 * g + 4, :], bank[6 + g][:, :].rearrange("p (k s) -> p k s", k=4), ACT.Copy).then_inc(sem("hg_taken"), 1)

            def expert(i, acc, acc0, following):
                act.wait_ge(sem("gsel_turned"), i + 1)
                A(GTS, bank[6][:, 0:T], ACT.Copy).then_inc(sem("gs_taken"), 1)
                for j in range(0, UPS, 2):
                    act.wait_ge(acc, acc0 + (j + 1))
                    A(AA[:, WC * (j // 2):WC * (j // 2) + WC], bank[(j // 2) % 2][:, 0:WC], ACT.Silu).then_inc(sem("moe_silu"), 1)
                for g in range(6):
                    n = min(4, FT - 4 * g)
                    act.wait_ge(sem("at_ready"), 6 * i + (g + 1))
                    A(AT[:, 4 * g:4 * g + n, :], bank[4 + g % 4][:, 0:n * P].rearrange("p (k s) -> p k s", k=n), ACT.Copy)\
                        .then_inc(sem("at_taken"), 1)
                for half in range(2):
                    act.wait_ge(acc, acc0 + (UPS + DOWNS))
                    A(YS[:, 512 * half:512 * half + 512], bank[half][:, :], ACT.Copy).then_inc(sem("ys_taken"), 1)
                if following:
                    gathered(i + 1)

            t0, per = phases["moe"]["t0"], UPS + DOWNS
            gathered(0)
            with act.Fori(0, NE - 1) as e:
                expert(e, acc_ready, per * e + t0, True)
            expert(NE - 1, acc_ready, per * (NE - 1) + t0, False)

            def over(r):
                gathered(r + NE)
                expert(r + NE, sem("over_acc"), per * r, False)

            act.wait_ge(sem("over_ready"), 1)
            with act.Fori(0, ROUNDS) as r:
                over_round(act, r, lambda: over(r))
            norm(8, [(sem("moe_done"), 1)])
            take_gemm(act, "pg1", lambda q, lin, b: A(PG[:, q, :], b, ACT.Sigmoid))
            norm(9, [(sem("embedded"), 2)])
            tokens(TK_OUT, OT)

        def dve_rest(dve, V, ch, step, norm):
            add_to_x = lambda q, lin, b: V.tensor_tensor(xT[:, q, :], b, xT[:, q, :], ALU.add)
            norm(1, lambda ct: gs[:, 8 + ct:9 + ct], lambda ct: mod[:, 1, ct:ct + 1])
            step(V.tensor_scalar(ANG3.bitcast(I32)[:, 2, :], POSB.bitcast(I32), 6, None, ALU.arith_shift_right))
            ch(V.tensor_copy(CHUNKS, ANG3.bitcast(I32)[:, 2, :]))
            step(V.tensor_scalar(POSI[:, :], POSI[:, :], 6, None, ALU.arith_shift_right))
            step(V.tensor_copy(CHC, POSI[:, :]))

            dve.wait_ge(sem("rot_tables"), 4)

            def rotate(lo, hi):
                for i in range(lo, hi):
                    src, table, n = ROTS[i]
                    z = src()
                    dve.wait_ge(sem("swapped"), i + 1)
                    if i >= 2:
                        dve.wait_ge(sem("rot_done"), i - 1)
                    ch(V.tensor_tensor(SWP[:, i % 2, 0:n, :], bank[5 + i % 2][:, 0:n * T].rearrange("p (n t) -> p n t", n=n),
                                       ROT[:, table, 1, :].unsqueeze(1).to_broadcast([P, n, T]), ALU.mult))
                    step(V.tensor_tensor(z, z, ROT[:, table, 0, :].unsqueeze(1).to_broadcast([P, n, T]), ALU.mult))
                    V.tensor_tensor(z, z, SWP[:, i % 2, 0:n, :], ALU.add).then_inc(sem("rot_done"), 1)

            rotate(0, 4)
            dve.wait_ge(*took("m2", 4))
            for n in range(16):
                tt, hh = n // 8, n % 8
                dve.wait_ge(sem("relu_done"), n + 1)
                if hh == 0:
                    ins = V.tensor_scalar(CUR[:, tt, :], RELU[:, n % 2, :], WI[:, tt, 0:1], None, ALU.mult)
                else:
                    dve.wait_ge(sem("score_added"), n)
                    ins = V.scalar_tensor_tensor(CUR[:, tt, :], RELU[:, n % 2, :], WI[:, tt, hh:hh + 1], CUR[:, tt, :], ALU.mult, ALU.add)
                ins.then_inc(sem("score_added"), 1)
            dve.wait_ge(sem("score_added"), 16)
            for tt in range(TT):
                ch(V.tensor_scalar(ADM[:, tt, :], CHUNKS, CHC[:, tt:tt + 1], None, ALU.is_le))
            ch.settle()
            ch(V.tensor_tensor(CUR[:, :, :], CUR[:, :, :], ADM[:, :, :], ALU.mult))
            step(V.tensor_scalar(MASK[:, :, :], ADM[:, :, :], BIG, -BIG, ALU.mult, ALU.add))
            step(V.tensor_tensor(CUR[:, :, :], CUR[:, :, :], MASK[:, :, :], ALU.add))
            for n in range(TOPK // 8):
                for tt in range(TT):
                    ch(V.max(TOP[:, tt, :], CUR[:, tt, :]))
                ch.settle()
                for tt in range(TT):
                    ch(V.match_replace(CUR[:, tt, :], TOP[:, tt, :], CUR[:, tt, :], -3.0e38))
                ch.settle()
            step(V.scalar_tensor_tensor(CUR[:, :, :], CUR[:, :, :], -2.0e38, ADM[:, :, :], ALU.is_le, ALU.mult))
            step(V.tensor_scalar(MASK[:, :, :], CUR[:, :, :], BIG, -BIG, ALU.mult, ALU.add))
            rotate(4, 12)

            def attend(n0, count, ahead, scores, weights, result):
                for b in range(ahead):
                    scores(b)
                for b in range(count + 2):
                    if b + ahead < count:
                        if b >= 1:
                            dve.wait_ge(sem("turned_ready"), n0 + b)
                        scores(b + ahead)
                    if b < count:
                        dve.wait_ge(sem("exps_ready"), 2 * (n0 + b + 1))
                        weights(b)
                    if b >= 2:
                        dve.wait_ge(sem("o_ready"), n0 + b - 1)
                        result(b - 2)

            def largest(m):
                ch.settle()
                V.tensor_reduce(MX[:, m, :], LG[:, m, :, :], AX_X, ALU.max, negate=True).then_inc(sem("max_ready"), 1)

            def scores(b):
                dve.wait_ge(sem("logits_ready"), b + 1)
                m = MASK[:, b % 2, :].unsqueeze(1).to_broadcast([P, 2, T])
                V.scalar_tensor_tensor(LG[:, b % 3, :, :], bank[LOGITS[b % 3]][:, :].rearrange("p (j s) -> p j s", j=2), P ** -0.5, m,
                                       ALU.mult, ALU.add).then_inc(sem("logits_taken"), 1)
                dve.wait_ge(sem("logits_taken"), b + 1)
                largest(b % 3)

            def weights(b):
                m = b % 3
                step(V.reciprocal(SM[:, m, :], SM[:, m, :]))
                V.tensor_tensor(LG[:, m, :, :], LG[:, m, :, :], SM[:, m, :].unsqueeze(2).to_broadcast([P, 2, T]), ALU.mult)\
                    .then_inc(sem("weights_ready"), 1)

            def result(b):
                tt, hp = b % 2, b // 2
                o = GT[:, 2 * hp:2 * hp + 2, tt * P:(tt + 1) * P]
                V.tensor_tensor(o, o, bank[b % 2][:, 0:T].rearrange("p (j t) -> p j t", j=2), ALU.mult).then_inc(sem("o_taken"), 1)

            attend(0, 16, 2, scores, weights, result)
            take_gemm(dve, "oo", lambda q, lin, b: V.scalar_tensor_tensor(
                xT[:, q, :], b, mod[:, 1, 16 + q:17 + q], xT[:, q, :], ALU.mult, ALU.add))
            norm(2, lambda ct: col("final_g", ct), dst=xT)
            dve.wait_ge(sem("h_ready"), 3)
            norm(3, lambda ct: col("mix0", ct))

            rotate(12, 16)
            dve.wait_ge(sem("lam_loaded"), 16)
            step(V.tensor_tensor(LAMB[:, 0:4:2, :], LAMB[:, 0:4:2, :], LAMB[:, 1:4:2, :], ALU.mult))
            V.tensor_reduce(small[:, 14:16], LAMB[:, 0:4:2, :], AX_X, ALU.add).then_inc(sem("lam_sums"), 1)
            dve.wait_ge(sem("cmask_ready"), 1)
            dve.wait_ge(*took("bch", 12))
            step(V.tensor_tensor(UC[:, :, 2:2 + T], BCH[:, 4:8, :], BCH[:, 8:12, :], ALU.mult))
            for ct in range(4):
                ch(V.tensor_scalar(CV[:, ct, :], UC[:, ct, 0:T], acw[:, ct, 0:1], None, ALU.mult))
            ch.settle()
            for j in (1, 2):
                for ct in range(4):
                    ch(V.scalar_tensor_tensor(CV[:, ct, :], UC[:, ct, j:j + T], acw[:, ct, j:j + 1], CV[:, ct, :], ALU.mult, ALU.add))
                ch.settle()
            ch(V.tensor_tensor(CV[:, :, :], CV[:, :, :], BCH[:, 0:4, :], ALU.mult))
            dve.wait_ge(sem("lam_exps"), 1)
            nlam = small[:, 7:8]
            step(V.tensor_scalar(nlam, small[:, 15:16], small[:, 14:15], LAM0, ALU.subtract, ALU.subtract))

            def scores2(b):
                dve.wait_ge(sem("logits_ready"), 16 + b + 1)
                for c in range(2):
                    ins = V.scalar_tensor_tensor(LG[:, b % 2, c, :], bank[4 + 2 * (b % 2) + c][:, 0:T], HD ** -0.5, CMASK[:, b % 2, :],
                                                 ALU.mult, ALU.add)
                    if c == 0:
                        ch(ins)
                ins.then_inc(sem("logits_taken"), 1)
                dve.wait_ge(sem("logits_taken"), 16 + b + 1)
                largest(b % 2)

            def weights2(b):
                step(V.reciprocal(SM[:, b % 2, :], SM[:, b % 2, :]))
                ch(V.tensor_tensor(SM[:, b % 2, 1:2], SM[:, b % 2, 1:2], nlam, ALU.mult))
                step(V.tensor_scalar(LG[:, b % 2, 0, :], LG[:, b % 2, 0, :], SM[:, b % 2, 0:1], None, ALU.mult))
                V.scalar_tensor_tensor(LG[:, b % 2, 0, :], LG[:, b % 2, 1, :], SM[:, b % 2, 1:2], LG[:, b % 2, 0, :], ALU.mult, ALU.add)\
                    .then_inc(sem("weights_ready"), 1)

            def result2(b):
                V.tensor_copy(OD[:, b // 2, (b % 2) * P:(b % 2 + 1) * P], bank[b % 2][:, 0:P]).then_inc(sem("o_taken"), 1)

            attend(16, 8, 1, scores2, weights2, result2)
            dve.wait_ge(sem("rooted"), 5)
            ch(V.tensor_scalar(OD[:, :, :], OD[:, :, :], subln, 1.0 - LAM0, ALU.mult, ALU.mult))
            step(V.reciprocal(RD[:, :, :], RD[:, :, :]))
            V.tensor_tensor(OD[:, :, :], OD[:, :, :], RD[:, :, :], ALU.mult).then_inc(sem("o_normed"), 1)
            take_gemm(dve, "ao", add_to_x)
            norm(4, lambda ct: col("ffn0", ct))

            def gated(j, i):
                if j % 2 == 1:
                    for m in range(2):
                        f = j - 1 + m + 4 * i
                        dve.wait_ge(acc_ready, phases["f13"]["t0"] + 2 * j + m + 1 + 8 * i)
                        dve.wait_ge(sem("silu_taken"), j + m + 4 * i)
                        V.tensor_tensor(FAF[:, bass.ds(f * T, T)], FAF[:, bass.ds(f * T, T)], bank[2 + m][:, 0:T], ALU.mult)\
                            .then_inc(sem("gate_taken"), 1)
                    for m in range(2):
                        f = j - 1 + m + 4 * i
                        dve.wait_ge(sem("gate_taken"), j + m + 4 * i)
                        V.tensor_copy(fa_hi_r[:, bass.ds(f, 1), :].rearrange("p k t -> p (k t)"), FAF[:, bass.ds(f * T, T)])\
                            .then_inc(sem("x_split"), 1)
                        dve.wait_ge(sem("x_split"), 2 * (j - 1 + m) + 3 + 8 * i)
                        V.tensor_tensor(fa_lo_r[:, bass.ds(f, 1), :].rearrange("p k t -> p (k t)"), FAF[:, bass.ds(f * T, T)],
                                        fa_hi_r.bitcast(F32)[:, bass.ds(f, 1), :].rearrange("p k t -> p (k t)"), ALU.subtract)\
                            .then_inc(sem("x_split"), 1)

            dve.wait_ge(sem("h_ready"), 5)
            V.tensor_copy(h_r[:, 0], hT[:, :, :]).then_inc(sem("x_split"), 1)
            dve.wait_ge(sem("x_split"), 1)
            V.tensor_tensor(h_r[:, 1], hT[:, :, :], h_r[:, 0].bitcast(F32), ALU.subtract).then_inc(sem("x_split"), 1)

            def split_ffn(j, i):
                w = wait_chunk(dve, "f13", j, i)
                V.tensor_copy(ffn_hi(j), w).then_inc(sem("hi_ready"), 1)
                dve.wait_ge(sem("hi_ready"), 4 * i + (j + 1))
                V.tensor_tensor(view(phases["f13"], j, ring_r), w, ffn_hi(j).bitcast(F32), ALU.subtract).then_inc(sem("lo_ready"), 1)

            def ffn(j, i):
                if j + 2 < 6:
                    split_ffn(j + 2, i)
                gated(j, i)

            split_ffn(0, 0)
            split_ffn(1, 0)
            each_chunk(dve, "f13", ffn)
            dve.wait_ge(sem("gate_taken"), FT)

            def split_f2(j):
                w = wait_chunk(dve, "f2", j, 0)
                V.tensor_copy(f2_hi(j), w).then_inc(sem("hi_ready"), 1)
                dve.wait_ge(sem("hi_ready"), FT + j + 1)
                V.tensor_tensor(view(phases["f2"], j, ring_r), w, f2_hi(j).bitcast(F32), ALU.subtract).then_inc(sem("lo_ready"), 1)

            split_f2(0)
            split_f2(1)
            for q in range(KT):
                if q + 2 < KT:
                    split_f2(q + 2)
                dve.wait_ge(acc_ready, phases["f2"]["t0"] + q + 1)
                V.tensor_tensor(xT[:, q, :], bank[q % 4][:, 0:T], xT[:, q, :], ALU.add).then_inc(acc_taken["dve"], 1)

            def ple(i, nrm):
                norm(nrm, lambda ct: col(f"ple{i}", ct))
                take_gemm(dve, f"pp{i}", lambda q, lin, b: V.tensor_tensor(PG[:, q, :], PG[:, q, :], b, ALU.mult))
                dve.wait_ge(*took(f"pp{i}", 8))
                V.tensor_tensor(xT[:, :, :], xT[:, :, :], PG[:, :, :], ALU.add).then_inc(sem("embedded"), 1)

            ple(0, 5)
            dve.wait_ge(sem("embedded"), 1)
            norm(6, lambda ct: col("mix1", ct))
            dve.wait_ge(sem("mean_summed"), 3)
            mean = bank[4][:, 0:T].unsqueeze(1).to_broadcast([P, KT, T])
            V.scalar_tensor_tensor(CVV[:, :, :], mean, -1.0 / D, CVV[:, :, :], ALU.mult, ALU.add).then_inc(sem("centred"), 1)
            dve.wait_ge(sem("rooted"), 6)
            step(V.reciprocal(nr[:, :], nr[:, :]))
            for ct in range(KT):
                ch(V.scalar_tensor_tensor(CVV[:, ct, :], CVV[:, ct, :], col("cln_g", ct), nr[:, :], ALU.mult, ALU.mult))
            ch.settle()
            for ct in range(KT):
                ins = V.tensor_scalar(CVV[:, ct, :], CVV[:, ct, :], col("cln_b", ct), None, ALU.add)
                if ct < KT - 1:
                    ch(ins)
            ins.then_inc(sem("cln_done"), 1)
            dve.wait_ge(sem("bs_loaded"), 16)
            for b in range(4):
                dve.wait_ge(sem("spatial_ready"), b + 1)
                v = bank[b][:, :].rearrange("p (g u t) -> p g u t", g=2, u=TT)
                bs = BSB[:, 2 * b:2 * b + 2, :].unsqueeze(2).to_broadcast([P, 2, TT, P])
                sp_ = VTS[:, b // 2, 512 * (b % 2):512 * (b % 2) + 512].rearrange("p (g u t) -> p g u t", g=2, u=TT)
                u = CU[:, 2 * b:2 * b + 2, :].rearrange("p g (u t) -> p g u t", u=TT)
                if b == 0:
                    dve.wait_ge(sem("spatial_ready"), 4)
                step(V.tensor_tensor(sp_, v, bs, ALU.add))
                V.tensor_tensor(u, u, sp_, ALU.mult).then_inc(sem("spatial_taken"), 1)
            take_gemm(dve, "cout", add_to_x)
            norm(7, lambda ct: col("ffn1", ct))
            dve.wait_ge(sem("router_ready"), 1)
            step(V.tensor_copy(RL[:, :, :], bank[5][:, 0:TT * NE].rearrange("p (u e) -> p u e", u=TT)))
            dve.wait_ge(sem("moe_const"), 1)
            big = [R64[:, m, :, :].rearrange("p u (e f) -> p u e f", e=NE) for m in range(2)]
            own = RL[:, :, :].unsqueeze(3).to_broadcast([P, TT, NE, NE])
            other = RL[:, :, :].unsqueeze(2).to_broadcast([P, TT, NE, NE])
            ch(V.tensor_tensor(big[0], other, own, ALU.is_gt))
            step(V.tensor_tensor(big[1], other, own, ALU.is_equal))
            step(V.tensor_tensor(big[1], big[1], LOWE[:, :, :].unsqueeze(1).to_broadcast([P, TT, NE, NE]), ALU.mult))
            step(V.tensor_tensor(big[0], big[0], big[1], ALU.add))
            ch(V.tensor_reduce(SEL[:, :, :], big[0], AX_X, ALU.add))
            step(V.tensor_reduce(NEG[:, 0:TT], RL[:, :, :], AX_X, ALU.max))
            ch(V.tensor_scalar(SEL[:, :, :], SEL[:, :, :], 1.5, None, ALU.is_lt))
            V.tensor_tensor(GATE[:, :, :], RL[:, :, :], NEG[:, 0:TT].unsqueeze(2).to_broadcast([P, TT, NE]), ALU.subtract)\
                .then_inc(sem("gates_centred"), 1)
            dve.wait_ge(sem("gate_exps"), 1)
            ch.settle()
            step(V.tensor_tensor(GATE[:, :, :], GATE[:, :, :], SEL[:, :, :], ALU.mult))
            step(V.tensor_reduce(NEG[:, 0:TT], GATE[:, :, :], AX_X, ALU.add))
            step(V.reciprocal(NEG[:, 0:TT], NEG[:, 0:TT]))
            V.tensor_tensor(GATE[:, :, :], GATE[:, :, :], NEG[:, 0:TT].unsqueeze(2).to_broadcast([P, TT, NE]), ALU.mult)\
                .then_inc(sem("sel_ready"), 1)
            dve.wait_ge(sem("sel_ready"), 1)
            dve.wait_ge(sem("rank_ready"), 1)
            ch(V.tensor_copy(RANK[:, :, :], bank[6][:, 0:TT * NE].rearrange("p (u e) -> p u e", u=TT)))
            V.tensor_copy(CNT[:, 0, :], bank[6][:, 2 * NE:3 * NE]).then_inc(sem("rank_taken"), 1)
            dve.wait_ge(sem("rank_taken"), 1)
            step(V.tensor_scalar(CNT[:, 1, :], CNT[:, 0, :], float(SLOTS), None, ALU.is_gt))
            ch(V.tensor_reduce(OVER[:, 0:1], CNT[:, 1, :], AX_X, ALU.add))
            step(V.tensor_tensor(big[0][:, 0], LOWE[:, :, :], CNT[:, 1, :].unsqueeze(1).to_broadcast([P, NE, NE]), ALU.mult))
            step(V.tensor_reduce(CNT[:, 2, :], big[0][:, 0], AX_X, ALU.add))
            ch(V.tensor_tensor(CNT[:, 3, :], CNT[:, 1, :], ECOL, ALU.mult))
            for r in range(ROUNDS):
                ch.settle()
                step(V.scalar_tensor_tensor(CNT[:, 0, :], CNT[:, 2, :], float(r), CNT[:, 3, :], ALU.is_equal, ALU.mult))
                ch(V.tensor_reduce(OVER[:, r + 1:r + 2], CNT[:, 0, :], AX_X, ALU.add))
            ch.settle()
            V.tensor_copy(OVERI[0:1, :], OVER[0:1, :]).then_inc(sem("over_ready"), 1)

            def split_chunk(j, e):
                if not is_split(j):
                    return
                """The expert's chunk j in parts; the low one in its slot of the ring."""
                w = wait_chunk(dve, "moe", j, e).rearrange("p k n -> p (k n)")
                hi = HIS[j % RING][:, 0:w.shape[1]]
                V.tensor_copy(hi, w).then_inc(sem("hi_ready"), 1)
                dve.wait_ge(sem("hi_ready"), SPLITS * e + (FT + KT + split_no(j)))
                V.tensor_tensor(view(phases["moe"], j, ring_r).rearrange("p k n -> p (k n)"), w, hi.bitcast(F32), ALU.subtract).then_inc(sem("lo_ready"), 1)

            def gate(i, p, acc, acc0):
                dve.wait_ge(acc, acc0 + (2 * p + 2))
                dve.wait_ge(sem("moe_silu"), (UPS // 2) * i + (p + 1))
                aa = AA[:, WC * p:WC * p + WC]
                V.tensor_tensor(aa, aa, bank[2 + p % 2][:, 0:WC], ALU.mult).then_inc(sem("moe_gated"), 1)

            AHEAD = 2

            def select(i, e, which):
                for tt in range(TT):
                    V.tensor_scalar(PSEL[:, tt, :], IOTA[:, which, :], RANK[:, tt, bass.ds(e, 1)], SEL[:, tt, bass.ds(e, 1)],
                                    ALU.is_equal, ALU.mult).then_inc(sem("psel_ready"), 1)
                for tt in range(TT):
                    dve.wait_ge(sem("psel_ready"), 4 * i + (tt + 1))
                    V.tensor_scalar(GSEL[:, tt, :], PSEL[:, tt, :], GATE[:, tt, bass.ds(e, 1)], None, ALU.mult)\
                        .then_inc(sem("psel_ready"), 1)

            def expert(i, e, acc, acc0, parts, following):
                if parts:
                    dve.wait_ge(sem("hg_taken"), 2 * i + 2)
                    V.tensor_copy(HG_HI[:, :, :], HG[:, :, :]).then_inc(sem("x_split"), 1)
                    dve.wait_ge(sem("x_split"), 2 * i + (2 * FT + 3))
                    V.tensor_tensor(HG_LO[:, :, :], HG[:, :, :], HG_HI.bitcast(F32)[:, :, :], ALU.subtract).then_inc(sem("x_split"), 1)
                    for j in range(AHEAD, UPS):
                        split_chunk(j, e)
                        if j % 2 == 1 and j >= 3:
                            gate(i, (j - 3) // 2, acc, acc0)
                    split_chunk(UPS, e)
                    gate(i, UPS // 2 - 1, acc, acc0)
                    for g in range(5):
                        fs = tiles_split(g)
                        f = slice(fs[0], fs[-1] + 1)
                        dve.wait_ge(sem("at_taken"), 6 * i + (g + 1))
                        V.tensor_copy(AT_HI[:, f, :], AT[:, f, :])\
                            .then_inc(sem("at_split"), 1)
                        dve.wait_ge(sem("at_split"), 10 * i + (2 * g + 1))
                        V.tensor_tensor(AT_LO[:, f, :], AT[:, f, :], AT_HI.bitcast(F32)[:, f, :], ALU.subtract).then_inc(sem("at_split"), 1)
                        if g in (1, 2):
                            split_chunk(UPS + g, e)
                    for j in range(UPS + 3, UPS + DOWNS):
                        split_chunk(j, e)
                    if following:
                        select(i + 1, e + 1, 0)
                        for j in range(AHEAD):
                            split_chunk(j, e + 1)
                else:
                    for p in range(UPS // 2):
                        gate(i, p, acc, acc0)
                for g in range(4):
                    dve.wait_ge(sem("scat_ready"), 4 * i + (g + 1))
                    x = xT[:, 2 * g:2 * g + 2, :]
                    V.tensor_tensor(x, bank[2 + g][:, :].rearrange("p (k t) -> p k t", k=2), x, ALU.add).then_inc(sem("scat_taken"), 1)
                dve.wait_ge(sem("scat_taken"), 4 * i + 4)
                V.memset(NEG[:, 0:1], 0.0)

            select(0, 0, 0)
            for j in range(AHEAD):
                split_chunk(j, 0)
            t0, per = phases["moe"]["t0"], UPS + DOWNS
            with dve.Fori(0, NE - 1) as e:
                expert(e, e, acc_ready, per * e + t0, True, True)
            expert(NE - 1, NE - 1, acc_ready, per * (NE - 1) + t0, True, False)

            def over(r):
                e = dve.value_load(OVERI[0:1, bass.ds(r + 1, 1)], min_val=0, max_val=NE - 1)
                select(r + NE, e, 1)
                expert(r + NE, e, sem("over_acc"), per * r, False, False)

            dve.wait_ge(sem("over_ready"), 1)
            with dve.Fori(0, ROUNDS) as r:
                over_round(dve, r, lambda: over(r))
            V.memset(NEG[:, 1:2], 0.0).then_inc(sem("moe_done"), 1)
            dve.wait_ge(sem("moe_done"), 1)
            ple(1, 8)
            dve.wait_ge(sem("embedded"), 2)
            norm(9, lambda ct: col("fnorm", ct), dst=hT)

        def dve_angles(dve, V, ch, step):
            dve.wait_ge(sem("late_loaded"), 32)
            ch(V.tensor_copy(ANG3[:, 0, :], POSB.bitcast(I32)))
            step(V.tensor_copy(ANG3[:, 1, :], POSB2.bitcast(I32)))
            for k in range(3):
                ch(V.tensor_scalar(ANG[:, k, :], ANG3[:, k // 2, :], invf[:, k:k + 1], None, ALU.mult))
            ch.settle()
            step(V.tensor_scalar(ANG2[:, :, :], ANG[:, :, :], 1.0 / (2 * np.pi), MAGIC, ALU.mult, ALU.add))
            step(V.tensor_scalar(ANG2[:, :, :], ANG2[:, :, :], MAGIC, None, ALU.subtract))
            for c in TWO_PI:
                step(V.scalar_tensor_tensor(ANG[:, :, :], ANG2[:, :, :], -c, ANG[:, :, :], ALU.mult, ALU.add))
            step(V.tensor_scalar(ANG[:, :, :], ANG[:, :, :], PI, -PI, ALU.min, ALU.max))
            step(V.tensor_scalar(ANG3[:, :, :], ANG[:, :, :], PI / 2, -2 * PI, ALU.is_gt, ALU.mult))
            step(V.scalar_tensor_tensor(ANG2[:, :, :], ANG[:, :, :], PI / 2, ANG3[:, :, :], ALU.add, ALU.add))
            V.tensor_scalar(ANG2[:, :, :], ANG2[:, :, :], PI, -PI, ALU.min, ALU.max).then_inc(sem("angles_ready"), 1)

        def view(ph, j, ring=ring):
            k, n = ph["shape"](j) if "shape" in ph else (ph["k"], ph["ncol"])
            return ring[:, ph["at"][j] % RING, 0:k * n].rearrange("p (k n) -> p k n", k=k)

        loaded = [sem(f"weights_loaded_{s}") for s in range(RING)]
        used = {"pe": sem("acc_ready"), "dve": sem("ada_used")}
        acc_ready = used["pe"]

        def each_chunk(eng, name, body, first=0):
            ph = phases[name]
            g = ph["group"]
            if ph["loop"]:
                for j in range(g * first):
                    body(j, 0)
                with eng.Fori(first, ph["n"] // g) as i:
                    for j in range(g):
                        body(j, i)
                for j in range(ph["n"] - ph["n"] % g, ph["n"]):
                    body(j, 0)
            else:
                for j in range(ph["n"]):
                    body(j, 0)

        def wait_chunk(eng, name, j, i):
            ph = phases[name]
            c = ph["at"][j]
            eng.wait_ge(loaded[c % RING], 16 * (c // RING + 1) + (16 * (ph["group"] // RING) * i if ph["loop"] else 0))
            return view(ph, j)

        acc_taken = {"act": sem("acc_taken_act"), "dve": sem("acc_taken_dve")}

        def took(name, n):
            ph = phases[name]
            return acc_taken[ph["taker"]], ph["taken0"] + n

        def pe_gemm(name, rhs, after, special=(), between=None):
            ph = phases[name]
            n = ph["tiles"]
            for s, v in after:
                nc.tensor.wait_ge(s, v)
            per = ph["group"] * ph["tiles"]

            def body(j, i):
                w = wait_chunk(nc.tensor, name, j, i)
                for m in range(n):
                    q = j * ph["tiles"] + m
                    if q == 0 and ph["loop"]:
                        nc.tensor.wait_ge(took(name, 0)[0], took(name, 0)[1] + per * i)
                    elif q >= 4:
                        nc.tensor.wait_ge(took(name, 0)[0], took(name, q - 3)[1] + per * i)
                    if q in special:
                        special[q](bank[q % 4], w).then_inc(acc_ready, 1)
                        continue
                    width = min(P, ph["ncol"] - m * P)
                    for k in range(ph["k"]):
                        mm = nc.tensor.matmul(bank[q % 4][0:width, 0:T], w[:, k, m * P:m * P + width], rhs(k),
                                              start=(k == 0), stop=(k == ph["k"] - 1))
                    mm.then_inc(acc_ready, 1)
                if between is not None:
                    between(j)

            each_chunk(nc.tensor, name, body)

        def take_gemm(eng, name, op):
            ph = phases[name]
            n = ph["tiles"]
            per = ph["group"] * ph["tiles"]

            def body(j, i):
                for m in range(n):
                    q = j * ph["tiles"] + m
                    lin = per * i
                    eng.wait_ge(acc_ready, ph["t0"] + q + 1 + lin)
                    op(q, lin, bank[q % 4][:, 0:T]).then_inc(acc_taken[ph["taker"]], 1)

            each_chunk(eng, name, body)

        def pe_sum(dst, src, after, done):
            for s, v in after:
                nc.tensor.wait_ge(s, v)
            for k in range(KT):
                mm = nc.tensor.matmul(dst, ones[:, :], src[:, k, :], start=(k == 0), stop=(k == KT - 1))
            mm.then_inc(done, 1)

        def pe_head_sum(dst, src, after, done):
            for s, v in after:
                nc.tensor.wait_ge(s, v)
            for k in range(KT):
                mm = nc.tensor.matmul(dst, hs(k), src[:, k, :], start=(k == 0), stop=(k == KT - 1))
            mm.then_inc(done, 1)

        def pe_head_spread(src, after, done):
            for s, v in after:
                nc.tensor.wait_ge(s, v)
            for k in range(KT):
                mm = nc.tensor.matmul(bank[4 + k // 2][:, (k % 2) * T:(k % 2 + 1) * T], he(k), src,
                                      start=True, stop=True)
            mm.then_inc(done, 1)

        def spread(k2):
            return bank[4 + k2][:, :].rearrange("p (k t) -> p k t", k=2)

        block = ctx.enter_context(nc.Block())
        NPAR = 20

        @block.sync
        def _(sp):
            sp.wait_ge(sem("params_loaded"), 16 * NPAR)

            def fetch(ph, j):
                c = ph["at"][j]
                if c >= RING:
                    reader, v = chunks[c - RING]
                    sp.wait_ge(used[reader], v)
                sp.dma_start(view(ph, j), ph["src"](j, 0)).then_inc(loaded[c % RING], 16)

            for name, ph in phases.items():
                g, n = ph["group"], ph["n"]
                if name == "zA":
                    for other, j in merged:
                        fetch(phases[other], j)
                elif name != "ada1":
                    for j in range(n if not ph["loop"] else g):
                        fetch(ph, j)
                if ph["loop"]:
                    with sp.Fori(0, n // g - 1) as i:
                        for j in range(g, 2 * g):
                            c = ph["at"][j]
                            sp.wait_ge(used["pe"], chunks[c - RING][1] + ph["tiles"] * g * i)
                            sp.dma_start(view(ph, j - g), ph["src"](j - g, i + 1)).then_inc(loaded[c % RING], 16)
                    for j in range(n - n % g, n):
                        fetch(ph, j)
            finish_sync(sp)

        @block.gpsimd
        def _(pool):
            ch = Chain(pool, sem("pool_step"))

            def step(ins):
                ch(ins)
                ch.settle()

            q = sem("pool_params_loaded")
            pool.dma_start(CROW[0:124, 0, :], a["conv_w"][0, 0:31, 0, :].rearrange("j (c p) -> (j c) p", p=P)[0:124, :]).then_inc(q, 16)
            pool.dma_start(CROW[0:124, 1, :], a["conv_w"][0, 0:31, 0, :].rearrange("j (c p) -> (j c) p", p=P)[124:248, :]).then_inc(q, 16)
            pool.dma_start(WU[0:64, :], a["rwkv_w_up"][0]).then_inc(q, 16)
            pool.dma_start(WU[64:128, :], a["rwkv_a_up"][0]).then_inc(q, 16)
            step(pool.memset(ident[:, :], 0.0))
            pool.affine_select(out=ident[:, :], in_=ident[:, :], compare_op=ALU.not_equal, fill=1.0, base=0,
                               pattern=[[-1, P]], channel_multiplier=1).then_inc(sem("ident_ready"), 1)
            pool.wait_ge(sem("ident_ready"), 1)
            step(pool.memset(ones[:, :], 1.0))
            for m in (swap_a, swap_i, swap_d, hsel, bmask):
                step(pool.memset(m[:, :] if m is not bmask else m[:, :, :], 0.0))
            step(pool.memset(hsel[0:64, 14:15], 1.0))
            step(pool.memset(hsel[64:128, 15:16], 1.0))
            for b in range(NC4):
                step(pool.memset(bmask[C * b:C * b + C, :, C * b:C * b + C], 1.0))
            step(pool.affine_select(out=bmask[:, 0, :], in_=bmask[:, 0, :], compare_op=ALU.is_gt, fill=0.0, base=0,
                                  pattern=[[1, P]], channel_multiplier=-1))
            step(pool.affine_select(out=bmask[:, 1, :], in_=bmask[:, 1, :], compare_op=ALU.is_ge, fill=0.0, base=0,
                                  pattern=[[1, P]], channel_multiplier=-1))
            step(pool.memset(segm[:, :], 1.0))
            step(pool.memset(segm[:, 0:T:C], 0.0))
            for m, half, blk in ((swap_a, 64, 128), (swap_i, 32, 64), (swap_d, 8, 64)):
                for h, base in ((0, -half), (1, 0)):
                    v = m[:, :].rearrange("p (b x) -> p b x", x=blk)[:, :, h * half:(h + 1) * half]
                    step(pool.affine_select(out=v, in_=v, compare_op=ALU.not_equal, fill=1.0, base=base,
                                          pattern=[[-blk, P // blk], [-1, half]], channel_multiplier=1))
            step(pool.memset(hspread[:, :, :], 1.0))
            step(pool.affine_select(out=hspread[:, :, :], in_=hspread[:, :, :], compare_op=ALU.is_ge, fill=0.0, base=0,
                                  pattern=[[P, KT], [1, P]], channel_multiplier=-64))
            step(pool.affine_select(out=hspread[:, :, :], in_=hspread[:, :, :], compare_op=ALU.is_ge, fill=0.0, base=63,
                                  pattern=[[-P, KT], [-1, P]], channel_multiplier=64))
            pool.memset(UP[:, :, 0:30], 0.0).then_inc(sem("const_ready"), 1)
            pool.wait_ge(sem("lt_ready"), 8)
            for n in range(NC4):
                pool.dma_start(ltd[n], LTC[C * n:C * n + C, :, :]).then_inc(sem("lt_stored"), 16)
            pool.wait_ge(sem("lt_stored"), 16 * NC4)
            for n in range(NC4):
                pool.dma_start(LTP[C * n:C * n + C, :, :], ltd[n].rearrange("s q t -> q s t")).then_inc(sem("lt_pairs"), 16)
            pool.wait_ge(sem("inverse_ready"), 1)
            pool.dma_start(ttd, TTP[:, :, :].rearrange("p a b -> p (a b)")).then_inc(sem("tt_stored"), 16)
            pool.wait_ge(sem("tt_stored"), 16)
            for tt in range(TT):
                if tt == 0:
                    pool.wait_ge(sem("tbd_cleared"), 1)
                else:
                    pool.wait_ge(sem("u_ready"), 4)
                for n in range(NC4):
                    src = ttd.rearrange("(n u q) (c t) -> n u c q t", n=NC4, u=TT, c=C)[n, tt]
                    pool.dma_start(TBD[C * n:C * n + C, :, C * n:C * n + C], src).then_inc(sem("tbd_ready"), 16)
            more_pool(pool, ch)


        def chunk_ends(tt):
            return pend[:, :, NC4 * tt:NC4 * tt + NC4]

        @block.tensor
        def _(pe):
            mm = nc.tensor.matmul

            pe.wait_ge(sem("ident_ready"), 1)
            pe.wait_ge(sem("x_loaded"), 16)
            for ct in range(KT):
                for tt in range(TT):
                    ins = nc.tensor.transpose(bank[ct][:, tt * P:(tt + 1) * P], XTOK[:, tt, ct * P:(ct + 1) * P], ident[:, :])
                ins.then_inc(sem("x_turned"), 1)
            pe.wait_ge(sem("params_loaded"), 16 * NPAR)
            pe.wait_ge(sem("pool_params_loaded"), 64)
            pe.wait_ge(sem("x_taken"), 1)
            nc.tensor.transpose(bank[0][:, 0:P], PROW[:, 0, :], ident[:, :])
            nc.tensor.transpose(bank[0][:, P:2 * P], PROW[:, 1, :], ident[:, :])
            nc.tensor.transpose(bank[0][:, 256:380], CROW[0:124, 0, :], ident[0:124, 0:124])
            nc.tensor.transpose(bank[0][:, 380:504], CROW[0:124, 1, :], ident[0:124, 0:124]).then_inc(sem("params_turned"), 1)
            pe.wait_ge(sem("const_ready"), 1)

            def ada(layer, lo=0, hi=6):
                ph = phases[f"ada{layer}"]
                for m in range(lo, hi):
                    pe.wait_ge(sem("ada_used"), ph["t0"] + m + 1)
                    for j in range(4):
                        ins = mm(bank[5][:, 4 * m + j:4 * m + j + 1], ADA[:, m % 2, j * P:(j + 1) * P], ones[:, 0:1],
                                 start=True, stop=True)
                    ins.then_inc(sem("ada_summed"), 1)

            def norm(i, after):
                pe_sum(bank[4][:, 0:T], NSQ[i], [(sem("norm_squares"), 2 * (i + 1))] + after, sem("norm_summed"))

            norm(0, [])
            ada(0)
            pe_gemm("zA", lambda k: hT[:, k, :], [(sem("h_ready"), 1), (sem("params_taken"), 2)],
                    between=lambda j: ada(1, (0, 1, 3, 5)[j], (1, 3, 5, 6)[j]))
            pe_gemm("zB", lambda k: hT[:, k, :], [took("zA", 16)])
            pe_gemm("zL", lambda k: hT[:, k, :], [took("zB", 32)])
            for part, (lo, done) in enumerate(((0, "wup_ready"), (64, "aup_ready"))):
                pe.wait_ge(sem("lora_ready"), 1)
                for ct in range(KT):
                    if part == 1 and ct % 2 == 0:
                        pe.wait_ge(sem("wup_taken"), ct + 2)
                    ins = mm(bank[4 + ct // 2][:, (ct % 2) * T:(ct % 2 + 1) * T], WU[lo:lo + 64, ct * P:(ct + 1) * P],
                             LO[lo:lo + 64, 0:T], start=True, stop=True)
                    if ct % 2 == 1:
                        ins.then_inc(sem(done), 1)
            pe_gemm("zG", lambda k: hT[:, k, :], [took("zL", 1)])
            pe_sum(bank[4][:, 0:T], YY, [(taps, 248), (sem("aup_taken"), 8)], sem("mean_summed"))
            pe_sum(bank[5][:, 0:T], VAL, [(sem("squares_ready"), 1)], sem("var_summed"))
            pe_head_sum(bank[6][0:16, 0:T], VAL, [(sem("squares_ready"), 2)], sem("key_sum"))
            pe_head_spread(nr[0:16, :], [(sem("key_norm"), 1)], sem("key_spread"))
            pe_head_sum(bank[0][0:16, 0:T], X1, [(sem("rk_ready"), 1), took("zG", 8)], sem("bonus_sum"))

            pe.wait_ge(sem("rwkv_ready"), 1)
            for g in range(8):
                tt = g // 4
                if g >= 4:
                    pe.wait_ge(sem("lt_ready"), g - 3)
                else:
                    pe.wait_ge(sem("key_applied"), 4)
                for j in range(4):
                    h = 8 * (g % 4 // 2) + 2 * j + g % 2
                    r = slice(64 * (h % 2), 64 * (h % 2) + 64)
                    t = slice(tt * P, tt * P + P)
                    ins = mm(bank[4 + g % 4][:, j * P:(j + 1) * P], X4[r, h // 2, t], AR[r, h // 2, 0, t], start=True, stop=True)
                ins.then_inc(sem("lt_banks"), 1)

            for tt in range(TT):
                t = slice(tt * P, tt * P + P)
                for m, (src, _) in enumerate(TOKS):
                    for half in range(2):
                        b = (2 * m + half) % 4
                        n = 8 * tt + 2 * m + half
                        if n >= 4:
                            pe.wait_ge(sem("toks_taken"), n - 3)
                        else:
                            pe.wait_ge(sem("bonus_taken"), 1)
                        if tt == 1 and m == 0 and half == 0:
                            pe.wait_ge(sem("y_ready"), 2)
                        for j in range(4):
                            ins = nc.tensor.transpose(bank[b][:, j * P:(j + 1) * P], src(4 * half + j, t), ident[:, :])
                        ins.then_inc(sem("toks_ready"), 1)
                for g in range(8):
                    n = 8 * tt + g
                    if n >= 4:
                        pe.wait_ge(sem("kar_taken"), n - 3)
                    else:
                        pe.wait_ge(sem("lt_ready"), 8)
                    if tt == 1 and g == 0:
                        pe.wait_ge(sem("state_ready"), NC4 + 1)
                        pe.wait_ge(sem("ycarry_taken"), 4)
                    for j in range(2):
                        h = 4 * (g // 2) + 2 * j + g % 2
                        r = slice(64 * (h % 2), 64 * (h % 2) + 64)
                        ins = mm(bank[4 + g % 4][:, j * 256:(j + 1) * 256].rearrange("p (a t) -> p a t", a=2),
                                 KK[r, h // 2, t], AR[r, h // 2, :, t], start=True, stop=True)
                    ins.then_inc(sem("kar_ready"), 1)
                pe.wait_ge(sem("toks_taken"), 8 * tt + 8)
                for g in range(4):
                    for j in range(4):
                        h = 8 * (g // 2) + 2 * j + g % 2
                        r = slice(64 * (h % 2), 64 * (h % 2) + 64)
                        ins = mm(bank[g][:, j * P:(j + 1) * P], X4[r, h // 2, t], AR[r, h // 2, 1, t], start=True, stop=True)
                    ins.then_inc(sem("br_ready"), 1)
                for g in range(4):
                    pe.wait_ge(sem("kar_taken"), 8 * tt + 8)
                    for j in range(4):
                        h = 4 * g + j
                        ins = mm(bank[4 + g][:, j * P:(j + 1) * P], A2T[:, h, :], VTOK[:, (h // 2) * P:(h // 2 + 1) * P],
                                 start=True, stop=True)
                    ins.then_inc(sem("w_ready"), 1)
                pe.wait_ge(sem("tbd_ready"), 64 * (tt + 1))
                pe.wait_ge(sem("br_taken"), 4 * (tt + 1))
                for g in range(2):
                    for j in range(8):
                        h = 8 * g + j
                        ins = mm(bank[g][64 * (h % 2):64 * (h % 2) + 64, (j // 2) * P:(j // 2 + 1) * P],
                                 ATOK[:, h * HD:(h + 1) * HD], TBD[:, h, :], start=True, stop=True)
                    ins.then_inc(sem("apt_ready"), 1)
                for g in range(4):
                    if g == 0:
                        pe.wait_ge(sem("w_taken"), 8 * (tt + 1))
                    for j in range(4):
                        h = 4 * g + j
                        ins = mm(bank[2 + g][:, j * P:(j + 1) * P], TBD[:, h, :], WW[:, (h // 2) * P:(h // 2 + 1) * P],
                                 start=True, stop=True)
                    ins.then_inc(sem("u_ready"), 1)
                for n in range(NC4):
                    i = NC4 * tt + n
                    rows = slice(C * n, C * n + C)
                    tc = slice(tt * P + C * n, tt * P + C * n + C)
                    if n == 0:
                        pe.wait_ge(sem("apt_taken"), 2 * (tt + 1))
                        pe.wait_ge(sem("u_taken"), 8 * (tt + 1))
                    pe.wait_ge(sem("state_ready"), i + 1)
                    for h in range(NH):
                        r = slice(64 * (h % 2), 64 * (h % 2) + 64)
                        ins = mm(bank[4 + h % 2][rows, (h // 2) * HD:(h // 2 + 1) * HD],
                                 APT[r, h // 2, rows], SS[r, h // 2, :], start=True, stop=True)
                    ins.then_inc(sem("as_ready"), 1)
                    for h in range(NH):
                        r = slice(64 * (h % 2), 64 * (h % 2) + 64)
                        mm(bank[7][r, (h // 2) * HD:(h // 2 + 1) * HD], KTOK[rows, h * HD:(h + 1) * HD],
                           VTOK[rows, h * HD:(h + 1) * HD], start=(h < 2), stop=False, skip_group_check=True)
                    if i >= 1:
                        pe.wait_ge(sem("ycarry_taken"), i)
                    for h in range(NH):
                        r = slice(64 * (h % 2), 64 * (h % 2) + 64)
                        ins = mm(bank[6][r, (h // 2) * C:(h // 2 + 1) * C], SS[r, h // 2, :], AR[r, h // 2, 1, tc],
                                 start=True, stop=True)
                    ins.then_inc(sem("ycarry_ready"), 1)
                    pe.wait_ge(sem("sa_ready"), 2 * i + 2)
                    for h in range(NH):
                        r = slice(64 * (h % 2), 64 * (h % 2) + 64)
                        ins = mm(bank[7][r, (h // 2) * HD:(h // 2 + 1) * HD], BTOK[rows, h * HD:(h + 1) * HD],
                                 UU[rows, h * HD:(h + 1) * HD], start=False, stop=True, skip_group_check=True)
                    ins.then_inc(sem("update_ready"), 1)
                for g in range(2):
                    for j in range(8):
                        h = 8 * g + j
                        o = bank[g][64 * (h % 2):64 * (h % 2) + 64, (j // 2) * P:(j // 2 + 1) * P]
                        mm(o, UU[:, h * HD:(h + 1) * HD], A3T[:, h, :], start=True, stop=False)
                        ins = mm(o, VTOK[:, h * HD:(h + 1) * HD], A4T[:, h, :], start=False, stop=True)
                    ins.then_inc(sem("yin_ready"), 1)

            pe_head_sum(bank[4][0:16, 0:T], YT, [(sem("y_ready"), 4)], sem("mean_summed"))
            pe_head_spread(nr[0:16, :], [(sem("gn_mean_ready"), 1)], sem("gn_mean_spread"))
            pe_head_sum(bank[0][0:16, 0:T], X1, [(sem("squares_ready"), 3)], sem("var_summed"))
            pe_head_spread(nr[0:16, :], [(sem("gn_rstd"), 1), (sem("centred"), 5)], sem("gn_rstd_spread"))
            pe_head_spread(stb[:, :], [(sem("gn_scaled"), 4)], sem("bonus_spread"))
            pe_gemm("eo", lambda k: YY[:, k, :] if k < 8 else YT[:, k - 8, :], [(sem("yb_ready"), 1)])
            pe_rest(pe)

        @block.scalar
        def _(act):
            ch = Chain(act, sem("act_step"))
            A = nc.scalar.activation
            q = sem("params_loaded")
            sent = [0]

            def par(dst, src):
                act.dma_start(dst, src).then_inc(q, 16)
                sent[0] += 1

            def rows(name, src):
                v = VEC[name]
                n = 1
                for s in src.shape:
                    n *= s
                n //= P
                flat = src
                if len(src.shape) == 2:
                    flat = src.rearrange("a b -> (a b)")
                elif len(src.shape) == 3:
                    flat = src.rearrange("a b c -> (a b c)")
                par(PROW[v % P:v % P + n, v // P, :], flat.rearrange("(r p) -> r p", p=P))

            rows("c", a["c"])
            rows("norm_g0", a["norm_g"])
            rows("final_g", a["final_g"])
            rows("ab00", a["ada_b"])
            rows("cv0", a["conv_vec"])
            rows("mu_r", a["rwkv_mu_rkv"])
            rows("w0", a["rwkv_vec"])
            rows("r_k", a["rwkv_r_k"])
            rows("mix0", a["ln_mix_2"])
            rows("ffn0", a["ln_ffn_2"])
            rows("ple0", a["ln_ple_2"])
            rows("fnorm", a["final_norm_2"])
            rows("cln_g", a["c_ln_g_2"])
            rows("cln_b", a["c_ln_b_2"])
            par(acw[:, :, :], a["a_conv_w_2"][0].rearrange("(c p) j -> p c j", p=P))
            par(mulora, a["rwkv_mu_lora"][0].rearrange("a b -> (a b)").unsqueeze(1))
            par(subln, a["a_subln_2"][0].unsqueeze(1))
            par(invf, a["inv_freq"])
            par(POSI[:, 0:1], a["positions"][0, 0:P].unsqueeze(1))
            par(POSI[:, 1:2], a["positions"][0, P:T].unsqueeze(1))
            assert sent[0] == NPAR, sent
            act.dma_start(XTOK[:, :, :], a["x"][0].rearrange("(u p) n -> p u n", p=P)).then_inc(sem("x_loaded"), 16)

            for ct in range(4, 8):
                act.wait_ge(sem("x_turned"), ct + 1)
                A(xT[:, ct, :], bank[ct][:, 0:T], ACT.Copy).then_inc(sem("x_taken_act"), 1)
            act.wait_ge(sem("params_turned"), 1)
            A(pc[:, :], bank[0][:, 0:256], ACT.Copy).then_inc(sem("params_taken"), 1)
            A(cw[:, 0:248], bank[0][:, 256:504], ACT.Copy).then_inc(sem("params_taken"), 1)
            act.wait_ge(sem("params_taken"), 2)
            A(cond[:, :], cols8("c"), ACT.Silu).then_inc(sem("cond_ready"), 1)

            def norm(i, after):
                for s, v in after:
                    act.wait_ge(s, v)
                for half in range(2):
                    k = slice(4 * half, 4 * half + 4)
                    A(NSQ[i][:, k, :], xT[:, k, :], ACT.Square).then_inc(sem("norm_squares"), 1)
                act.wait_ge(sem("norm_summed"), i + 1)
                A(nr[:, :], bank[4][:, 0:T], ACT.Sqrt, bias=1e-6, scale=1.0 / D).then_inc(sem("norm_rooted"), 1)

            norm(0, [(sem("x_taken"), 4), (sem("x_taken_act"), 4)])

            def take_a(q, lin, b):
                return A(UP[:, q, 30:30 + T], b, ACT.Copy) if q < 8 else A(GLU[:, q - 8, :], b, ACT.Sigmoid)

            take_gemm(act, "zA", take_a)
            take_gemm(act, "zB", lambda q, lin, b: A(ZE[:, bass.ds(q * T + lin * T, T)], b, ACT.Copy))
            take_gemm(act, "zL", lambda q, lin, b: A(LO[:, 0:T], b, ACT.Copy))
            act.wait_ge(sem("lora_lerped"), 1)
            A(LO[0:64, 0:T], LO[0:64, 0:T], ACT.Tanh).then_inc(sem("lora_ready"), 1)
            for ct in range(KT):
                act.wait_ge(sem("wup_ready"), ct // 2 + 1)
                A(X1[:, ct, :], bank[4 + ct // 2][:, (ct % 2) * T:(ct % 2 + 1) * T], ACT.Sigmoid,
                  bias=col("w0", ct)).then_inc(sem("wup_taken"), 1)
            for ct in range(KT):
                act.wait_ge(sem("aup_ready"), ct // 2 + 1)
                A(X2[:, ct, :], bank[4 + ct // 2][:, (ct % 2) * T:(ct % 2 + 1) * T], ACT.Sigmoid,
                  bias=col("a0", ct)).then_inc(sem("aup_taken"), 1)
            take_gemm(act, "zG", lambda q, lin, b: A(BG[:, q, :], b, ACT.Silu))
            act.wait_ge(sem("centred"), 1)
            A(VAL[:, :, :], YY[:, :, :], ACT.Square).then_inc(sem("squares_ready"), 1)
            A(AG[:, :, :], AG[:, :, :], ACT.Silu).then_inc(sem("agate_ready"), 1)
            act.wait_ge(sem("var_summed"), 1)
            A(nr[:, :], bank[5][:, 0:T], ACT.Sqrt, bias=1e-5, scale=1.0 / D).then_inc(sem("rooted"), 1)
            act.wait_ge(sem("conv_scaled"), 1)
            for ct in range(KT):
                ins = A(YY[:, ct, :], YY[:, ct, :], ACT.Silu, bias=col("cv2", ct), scale=col("cv1", ct))
            ins.then_inc(sem("conv_silu"), 1)
            act.wait_ge(sem("keys_scaled"), 1)
            A(VAL[:, :, :], X4[:, :, :], ACT.Square).then_inc(sem("squares_ready"), 1)
            act.wait_ge(sem("key_sum"), 1)
            A(nr[0:16, :], bank[6][0:16, 0:T], ACT.Sqrt).then_inc(sem("rooted"), 1)
            act.wait_ge(sem("decay_sums"), 1)
            A(AR[:, :, 1, :], X3[:, :, :], ACT.Exp, scale=-DECAY).then_inc(sem("decays"), 1)
            act.wait_ge(sem("decay_before"), 1)
            A(AR[:, :, 0, :], X1[:, :, :], ACT.Exp, scale=-DECAY).then_inc(sem("decays"), 1)
            A(X3[:, :, :], X3[:, :, :], ACT.Exp, scale=DECAY).then_inc(sem("decays"), 1)
            act.wait_ge(sem("bonus_sum"), 1)
            A(stb[:, :], bank[0][0:16, 0:T], ACT.Copy).then_inc(sem("bonus_taken"), 1)

            for tt in range(TT):
                for m, (_, dst) in enumerate(TOKS):
                    for half in range(2):
                        n = 8 * tt + 2 * m + half
                        act.wait_ge(sem("toks_ready"), n + 1)
                        if tt == 1 and m == 0 and half == 0:
                            act.wait_ge(sem("yin_ready"), 2)
                        A(dst[:, 512 * half:512 * half + 512], bank[(2 * m + half) % 4][:, :], ACT.Copy)\
                            .then_inc(sem("toks_taken"), 1)
                for g in range(4):
                    act.wait_ge(sem("w_ready"), 4 * tt + g + 1)
                    for h in range(2):
                        src = bank[4 + g][:, :].rearrange("p (c h v) -> p c h v", c=2, h=2)[:, :, h, h * HD:(h + 1) * HD]
                        dst = WW[:, 256 * g:256 * g + 256].rearrange("p (c h v) -> p c h v", c=2, h=2)[:, :, h, :]
                        A(dst, src, ACT.Copy).then_inc(sem("w_taken"), 1)
                for g in range(2):
                    act.wait_ge(sem("apt_ready"), 2 * tt + g + 1)
                    A(APT[:, 4 * g:4 * g + 4, :], bank[g][:, :].rearrange("p (c t) -> p c t", c=4), ACT.Copy)\
                        .then_inc(sem("apt_taken"), 1)
                for n in range(NC4):
                    i = NC4 * tt + n
                    act.wait_ge(sem("ycarry_ready"), i + 1)
                    A(YT[:, :, tt * P + C * n:tt * P + C * n + C], bank[6][:, 0:T].rearrange("p (c t) -> p c t", c=KT), ACT.Copy)\
                        .then_inc(sem("ycarry_taken"), 1)

            act.wait_ge(sem("mean_summed"), 2)
            A(nr[0:16, :], bank[4][0:16, 0:T], ACT.Copy, scale=1.0 / HD).then_inc(sem("gn_mean_ready"), 1)
            act.wait_ge(sem("centred"), 5)
            A(X1[:, :, :], YT[:, :, :], ACT.Square).then_inc(sem("squares_ready"), 1)
            act.wait_ge(sem("var_summed"), 2)
            A(nr[0:16, :], bank[0][0:16, 0:T], ACT.Sqrt, bias=64e-5, scale=1.0 / HD).then_inc(sem("rooted"), 1)
            act_rest(act, ch, A, norm)

        @block.vector
        def _(dve):
            V = nc.vector
            ch = Chain(dve, sem("dve_step"))

            def step(ins):
                ch(ins)
                ch.settle()

            for ct in range(4):
                dve.wait_ge(sem("x_turned"), ct + 1)
                V.tensor_copy(xT[:, ct, :], bank[ct][:, 0:T]).then_inc(sem("x_taken"), 1)
            dve.wait_ge(sem("x_taken_act"), 4)

            def ada(layer):
                ph = phases[f"ada{layer}"]
                for m in range(6):
                    w = wait_chunk(dve, f"ada{layer}", m, 0)
                    if 6 * layer + m >= 2:
                        dve.wait_ge(sem("ada_summed"), 6 * layer + m - 1)
                    acc = ADA[:, m % 2, :]
                    step(V.tensor_scalar(acc, w[:, 0, :], cond[:, 0:1], None, ALU.mult))
                    for k in range(1, KT):
                        ins = V.scalar_tensor_tensor(acc, w[:, k, :], cond[:, k:k + 1], acc, ALU.mult, ALU.add)
                        if k < KT - 1:
                            step(ins)
                    ins.then_inc(sem("ada_used"), 1)
                dve.wait_ge(sem("ada_summed"), 6 * (layer + 1))
                b = VEC[f"ab{layer}0"]
                step(V.tensor_tensor(mod[:, layer, :], bank[5][:, 0:24], pc[:, b:b + 24], ALU.add))
                step(V.tensor_scalar(gs[:, 8 * layer:8 * layer + 8], mod[:, layer, 8:16], 1.0, None, ALU.add))
                V.tensor_tensor(gs[:, 8 * layer:8 * layer + 8], gs[:, 8 * layer:8 * layer + 8],
                                cols8(f"norm_g{layer}"), ALU.mult).then_inc(sem("mod_ready"), 1)
                dve.wait_ge(sem("mod_ready"), layer + 1)

            def norm(i, gain, shift=None, dst=None):
                dst = hT if dst is None else dst
                dve.wait_ge(sem("norm_rooted"), i + 1)
                step(V.reciprocal(nr[:, :], nr[:, :]))
                for ct in range(KT):
                    ins = V.scalar_tensor_tensor(dst[:, ct, :], xT[:, ct, :], gain(ct), nr[:, :], ALU.mult, ALU.mult)
                    if shift is not None or ct < KT - 1:
                        ch(ins)
                if shift is not None:
                    ch.settle()
                    for ct in range(KT):
                        ins = V.tensor_scalar(dst[:, ct, :], dst[:, ct, :], shift(ct), None, ALU.add)
                        if ct < KT - 1:
                            ch(ins)
                ins.then_inc(sem("h_ready"), 1)

            dve.wait_ge(sem("cond_ready"), 1)
            ada(0)
            norm(0, lambda ct: gs[:, ct:ct + 1], lambda ct: mod[:, 0, ct:ct + 1])

            ada(1)
            dve.wait_ge(*took("zA", 16))
            dve.wait_ge(sem("const_ready"), 1)
            step(V.tensor_tensor(UP[:, :, 30:30 + T], UP[:, :, 30:30 + T], GLU[:, :, :], ALU.mult))
            for ct in range(KT):
                V.tensor_scalar(YY[:, ct, :], UP[:, ct, 0:T], cw[:, ct:ct + 1], col("cv0", ct), ALU.mult, ALU.add)\
                    .then_inc(taps, 1)
            with dve.Fori(1, 31) as j:
                for ct in range(KT):
                    dve.wait_ge(taps, 8 * j - 8 + ct + 1)
                    V.scalar_tensor_tensor(YY[:, ct, :], UP[:, ct, bass.ds(j, T)], cw[:, bass.ds(8 * j + ct, 1)],
                                           YY[:, ct, :], ALU.mult, ALU.add).then_inc(taps, 1)
            dve.wait_ge(taps, 248)

            def lerp(z, d, mu, done):
                ch(V.tensor_tensor(d[:, :, 1:T], z[:, :, 0:T - 1], z[:, :, 1:T], ALU.subtract))
                step(V.tensor_scalar(d[:, :, 0:1], z[:, :, 0:1], -1.0, None, ALU.mult))
                for ct in range(z.shape[1]):
                    ins = V.scalar_tensor_tensor(z[:, ct, :], d[:, ct, :], mu(ct), z[:, ct, :], ALU.mult, ALU.add)
                    if ct < z.shape[1] - 1:
                        ch(ins)
                ins.then_inc(done, 1)

            dve.wait_ge(*took("zL", 1))
            lo = LO[:, :].rearrange("p (a t) -> p a t", a=2)
            lerp(lo[:, 0:1, :], lo[:, 1:2, :], lambda ct: mulora, sem("lora_lerped"))
            dve.wait_ge(*took("zB", 32))
            for n, (z, name) in enumerate(((KK, "mu_k"), (RR, "mu_r"), (VV, "mu_v"))):
                lerp(z, VAL, lambda ct, name=name: col(name, ct), sem("rkv_lerped"))
                dve.wait_ge(sem("rkv_lerped"), n + 1)
            dve.wait_ge(sem("mean_summed"), 1)
            mean = bank[4][:, 0:T].unsqueeze(1).to_broadcast([P, KT, T])
            V.scalar_tensor_tensor(YY[:, :, :], mean, -1.0 / D, YY[:, :, :], ALU.mult, ALU.add).then_inc(sem("centred"), 1)
            for ct in range(KT):
                ins = V.tensor_scalar(X4[:, ct, :], KK[:, ct, :], col("k_k", ct), None, ALU.mult)
                if ct < KT - 1:
                    ch(ins)
            ins.then_inc(sem("keys_scaled"), 1)
            dve.wait_ge(sem("keys_scaled"), 1)
            dve.wait_ge(sem("rooted"), 1)
            step(V.reciprocal(nr[:, :], nr[:, :]))
            nrb = nr[:, :].unsqueeze(1).to_broadcast([P, KT, T])
            V.tensor_tensor(YY[:, :, :], YY[:, :, :], nrb, ALU.mult).then_inc(sem("conv_scaled"), 1)
            dve.wait_ge(sem("wup_taken"), 8)
            for ct in range(KT):
                ins = V.tensor_tensor_scan(X3[:, ct, :], segm[:, :], X1[:, ct, :], 0.0, ALU.mult, ALU.add)
                if ct < KT - 1:
                    ch(ins)
            ins.then_inc(sem("decay_sums"), 1)
            dve.wait_ge(sem("decay_sums"), 1)
            V.tensor_tensor(X1[:, :, :], X3[:, :, :], X1[:, :, :], ALU.subtract).then_inc(sem("decay_before"), 1)
            dve.wait_ge(sem("rooted"), 2)
            step(V.tensor_scalar(nr[0:16, :], nr[0:16, :], 1e-12, None, ALU.max))
            V.reciprocal(nr[0:16, :], nr[0:16, :]).then_inc(sem("key_norm"), 1)
            dve.wait_ge(sem("conv_silu"), 1)
            dve.wait_ge(sem("agate_ready"), 1)
            V.tensor_tensor(YY[:, :, :], YY[:, :, :], AG[:, :, :], ALU.mult).then_inc(sem("conv_normed"), 1)
            dve.wait_ge(sem("key_spread"), 1)
            for g in range(4):
                V.tensor_tensor(X4[:, 2 * g:2 * g + 2, :], X4[:, 2 * g:2 * g + 2, :], spread(g), ALU.mult)\
                    .then_inc(sem("key_applied"), 1)
            dve.wait_ge(sem("key_applied"), 4)
            dve.wait_ge(sem("aup_taken"), 8)
            dve.wait_ge(sem("decays"), 3)
            step(V.scalar_tensor_tensor(AR[:, :, 0, :], X4[:, :, :], -1.0, AR[:, :, 0, :], ALU.mult, ALU.mult))
            step(V.tensor_tensor(X4[:, :, :], X4[:, :, :], X2[:, :, :], ALU.mult))
            step(V.tensor_tensor(X4[:, :, :], X4[:, :, :], X3[:, :, :], ALU.mult))
            for ct in range(KT):
                ch(V.tensor_scalar(X2[:, ct, :], X2[:, ct, :], col("k_a", ct), col("k_a", ct), ALU.mult, ALU.subtract))
            ch.settle()
            step(V.scalar_tensor_tensor(KK[:, :, :], X2[:, :, :], 1.0, KK[:, :, :], ALU.add, ALU.mult))
            step(V.tensor_tensor(X1[:, :, :], RR[:, :, :], KK[:, :, :], ALU.mult))
            for ct in range(KT):
                ins = V.tensor_scalar(X1[:, ct, :], X1[:, ct, :], col("r_k", ct), None, ALU.mult)
                if ct < KT - 1:
                    ch(ins)
            ins.then_inc(sem("rk_ready"), 1)
            step(V.tensor_copy(pend[:, :, :], AR[:, :, 1, C - 1:T:C]))
            ch(V.tensor_tensor(AR[:, :, 1, :], AR[:, :, 1, :], RR[:, :, :], ALU.mult))
            ch(V.memset(SS[:, :, :], 0.0))
            ch(V.memset(TTP[:, :, :], 0.0))
            ch.settle()
            V.tensor_tensor(KK[:, :, :], KK[:, :, :], X3[:, :, :], ALU.mult).then_inc(sem("rwkv_ready"), 1)
            V.memset(TTP[:, :, :].rearrange("p a b -> p (a b)")[:, 0:C * C:C + 1], 1.0).then_inc(sem("state_ready"), 1)

            dve.wait_ge(sem("bonus_sum"), 1)
            for g in range(8):
                dve.wait_ge(sem("lt_banks"), g + 1)
                b = bank[4 + g % 4][:, :].rearrange("p (q t) -> p q t", q=4)
                for n in range(NC4):
                    r = slice(C * n, C * n + C)
                    m = bmask[r, 0, r].unsqueeze(1).to_broadcast([C, 4, C])
                    q = 16 * (g // 4) + 8 * (g % 4 // 2) + g % 2
                    ins = V.tensor_tensor(LTC[r, q:q + 7:2, :], b[r, :, r], m, ALU.mult)
                ins.then_inc(sem("lt_ready"), 1)
            dve.wait_ge(sem("lt_pairs"), 16 * NC4)
            dve.wait_ge(sem("state_ready"), 1)
            for t in range(1, C):
                prod = TMP[:, 0:t * t].rearrange("p (c s) -> p c s", c=t)
                l = LTP[:, 0:t, t].unsqueeze(1).to_broadcast([P, t, t])
                step(V.tensor_tensor(prod, TTP[:, 0:t, 0:t], l, ALU.mult))
                ins = V.tensor_reduce(TTP[:, 0:t, t:t + 1], prod, AX_X, ALU.add)
                if t < C - 1:
                    step(ins)
            ins.then_inc(sem("inverse_ready"), 1)
            dve.wait_ge(sem("inverse_ready"), 1)
            V.memset(TBD[:, :, :], 0.0).then_inc(sem("tbd_cleared"), 1)

            m0 = bmask[:, 0, :].unsqueeze(1)
            m1 = bmask[:, 1, :].unsqueeze(1)
            for tt in range(TT):
                for g in range(8):
                    dve.wait_ge(sem("kar_ready"), 8 * tt + g + 1)
                    if tt == 1 and g == 0:
                        dve.wait_ge(sem("yin_ready"), 2)
                    b = bank[4 + g % 4][:, :].rearrange("p (h a t) -> p h a t", h=2, a=2)
                    q = slice(4 * (g // 2) + g % 2, 4 * (g // 2) + g % 2 + 3, 2)
                    ch(V.tensor_tensor(A2T[:, q, :], b[:, :, 0, :], m0.to_broadcast([P, 2, P]), ALU.mult))
                    V.tensor_tensor(A4T[:, q, :], b[:, :, 1, :], m1.to_broadcast([P, 2, P]), ALU.mult)\
                        .then_inc(sem("kar_taken"), 1)
                for g in range(4):
                    dve.wait_ge(sem("br_ready"), 4 * tt + g + 1)
                    b = bank[g][:, :].rearrange("p (h t) -> p h t", h=4)
                    q = slice(8 * (g // 2) + g % 2, 8 * (g // 2) + g % 2 + 7, 2)
                    V.tensor_tensor(A3T[:, q, :], b, m1.to_broadcast([P, 4, P]), ALU.mult)\
                        .then_inc(sem("br_taken"), 1)
                for g in range(4):
                    dve.wait_ge(sem("u_ready"), 4 * tt + g + 1)
                    for h in range(2):
                        src = bank[2 + g][:, :].rearrange("p (c h v) -> p c h v", c=2, h=2)[:, :, h, h * HD:(h + 1) * HD]
                        dst = UU[:, 256 * g:256 * g + 256].rearrange("p (c h v) -> p c h v", c=2, h=2)[:, :, h, :]
                        V.tensor_copy(dst, src).then_inc(sem("u_taken"), 1)
                dve.wait_ge(sem("u_taken"), 8 * (tt + 1))
                for n in range(NC4):
                    i = NC4 * tt + n
                    rows = slice(C * n, C * n + C)
                    dve.wait_ge(sem("as_ready"), i + 1)
                    for half in range(2):
                        u = UU[rows, :].rearrange("p (c h v) -> p c h v", c=KT, h=2)[:, :, half, :]
                        V.tensor_tensor(u, bank[4 + half][rows, :].rearrange("p (c v) -> p c v", c=KT), u, ALU.add).then_inc(sem("sa_ready"), 1)
                    dve.wait_ge(sem("update_ready"), i + 1)
                    step(V.tensor_tensor(SS[:, :, :], bank[7][:, :].rearrange("p (c v) -> p c v", c=KT), SS[:, :, :], ALU.add))
                    pe_ = pend[:, :, i:i + 1].to_broadcast([P, KT, HD])
                    V.tensor_tensor(SS[:, :, :], SS[:, :, :], pe_, ALU.mult).then_inc(sem("state_ready"), 1)
                    dve.wait_ge(sem("state_ready"), i + 2)
                dve.wait_ge(sem("ycarry_taken"), 4 * (tt + 1))
                for g in range(2):
                    dve.wait_ge(sem("yin_ready"), 2 * tt + g + 1)
                    o = YT[:, 4 * g:4 * g + 4, tt * P:(tt + 1) * P]
                    V.tensor_tensor(o, bank[g][:, :].rearrange("p (c t) -> p c t", c=4), o, ALU.add).then_inc(sem("y_ready"), 1)

            dve.wait_ge(sem("y_ready"), 4)
            dve.wait_ge(sem("gn_mean_spread"), 1)
            for g in range(4):
                o = YT[:, 2 * g:2 * g + 2, :]
                V.scalar_tensor_tensor(o, spread(g), -1.0, o, ALU.mult, ALU.add).then_inc(sem("centred"), 1)
            dve.wait_ge(sem("rooted"), 3)
            V.reciprocal(nr[0:16, :], nr[0:16, :]).then_inc(sem("gn_rstd"), 1)
            dve.wait_ge(sem("gn_rstd_spread"), 1)
            for g in range(4):
                o = YT[:, 2 * g:2 * g + 2, :]
                V.tensor_tensor(o, o, spread(g), ALU.mult).then_inc(sem("gn_scaled"), 1)
            dve.wait_ge(sem("gn_scaled"), 4)
            for ct in range(KT):
                ch(V.tensor_scalar(YT[:, ct, :], YT[:, ct, :], col("lnx_w", ct), col("lnx_b", ct), ALU.mult, ALU.add))
            dve.wait_ge(sem("bonus_spread"), 1)
            for g in range(4):
                ch(V.tensor_tensor(X2[:, 2 * g:2 * g + 2, :], VV[:, 2 * g:2 * g + 2, :], spread(g), ALU.mult))
            ch.settle()
            step(V.tensor_tensor(YT[:, :, :], YT[:, :, :], X2[:, :, :], ALU.add))
            V.tensor_tensor(YT[:, :, :], YT[:, :, :], BG[:, :, :], ALU.mult).then_inc(sem("yb_ready"), 1)
            dve_angles(dve, V, ch, step)
            take_gemm(dve, "eo", lambda q, lin, b: V.scalar_tensor_tensor(
                xT[:, q, :], b, mod[:, 0, 16 + q:17 + q], xT[:, q, :], ALU.mult, ALU.add))
            dve_rest(dve, V, ch, step, norm)


def kernel(**inputs):
    import numpy as _np
    import concourse.bacc as _bacc
    from concourse import mybir as _mybir
    from concourse.bass_utils import run_bass_kernel_spmd as _run

    nc = _bacc.Bacc("TRN2", target_bir_lowering=False, num_devices=1)
    arrays, args = {}, {}
    for name, value in inputs.items():
        v = _np.ascontiguousarray(value)
        arrays[f"in_{name}_dram"] = v
        args[name] = nc.dram_tensor(f"in_{name}_dram", v.shape, _mybir.dt.from_np(v.dtype), kind="ExternalInput").ap()
    inv = _np.zeros((128, 6), _np.float32)
    p = _np.arange(128)
    inv[:, 0] = (10000.0 ** (-(2 * (p % 64)) / 128)).astype(_np.float32)
    inv[:, 1] = (10000.0 ** (-(2 * (p % 32)) / 64)).astype(_np.float32)
    inv[:, 2] = _np.where(p % 64 < 16, 500000.0 ** (-(2 * (p % 8)) / 16), 0).astype(_np.float32)
    inv[:, 3] = _np.where(p < 64, -1, 1)
    inv[:, 4] = _np.where(p % 64 < 32, -1, 1)
    inv[:, 5] = _np.where(p % 64 < 8, -1, 1)
    arrays["inv_freq_dram"] = inv
    args["inv_freq"] = nc.dram_tensor("inv_freq_dram", inv.shape, _mybir.dt.float32, kind="ExternalInput").ap()
    out = nc.dram_tensor("out_dram", (1, 256, 1024), _mybir.dt.float32, kind="ExternalOutput").ap()
    build(nc, args, out)
    r = _run(nc, [arrays], core_ids=[0])
    return r.results[0]["out_dram"]
```
